# Optimizing a Trainium2 kernel written in Bass

```python
import jax, jax.numpy as jnp
from jax import lax
import numpy as np
import math

D_MODEL = 1024
BATCH = 1
SEQ = 256
DEPTH = 1

GRID_W = 64
CTX_LEN = 256
HEAD_DIM = 64
ATTN_HEADS = 8
ATTN_KV_HEADS = 2
GQA_GROUP = ATTN_HEADS // ATTN_KV_HEADS
RET_HEADS = 8
ATTN_WIDTH = ATTN_HEADS * HEAD_DIM
KV_WIDTH = ATTN_KV_HEADS * HEAD_DIM
RET_WIDTH = RET_HEADS * HEAD_DIM
MIX_WIDTH = ATTN_WIDTH + RET_WIDTH
IN_PROJ_WIDTH = ATTN_WIDTH + 2 * KV_WIDTH + 4 * RET_WIDTH
SPLITS = (ATTN_WIDTH, ATTN_WIDTH + KV_WIDTH, ATTN_WIDTH + 2 * KV_WIDTH,
          ATTN_WIDTH + 2 * KV_WIDTH + RET_WIDTH, ATTN_WIDTH + 2 * KV_WIDTH + 2 * RET_WIDTH,
          ATTN_WIDTH + 2 * KV_WIDTH + 3 * RET_WIDTH)
FFN_HIDDEN = -(-8 * D_MODEL // (3 * 256)) * 256
N_MOD = 6
QBLOCK = 128
RET_CHUNK = 128
ROPE_BASE = 10000.0
ATTN_SCALE = HEAD_DIM ** -0.5
EPS = 1e-6


def rms_norm(x, g):
    xf = x.astype(jnp.float32)
    y = xf * lax.rsqrt(jnp.mean(xf * xf, axis=-1, keepdims=True) + EPS)
    return (y * g.astype(jnp.float32)).astype(x.dtype)

def head_group_norm(o):
    mu = jnp.mean(o, axis=-1, keepdims=True)
    var = jnp.mean(jnp.square(o - mu), axis=-1, keepdims=True)
    return (o - mu) * lax.rsqrt(var + EPS)

def modulate(h, shift, scale):
    return h * (1 + scale) + shift

def axial_rope(rows):
    row = jnp.broadcast_to(jnp.arange(rows)[:, None], (rows, GRID_W)).reshape(-1).astype(jnp.float32)
    col = jnp.broadcast_to(jnp.arange(GRID_W)[None, :], (rows, GRID_W)).reshape(-1).astype(jnp.float32)
    n_freq = HEAD_DIM // 4
    inv = ROPE_BASE ** (-jnp.arange(n_freq, dtype=jnp.float32) / n_freq)
    ang = jnp.concatenate([row[:, None] * inv, col[:, None] * inv], axis=-1)
    return jnp.cos(ang), jnp.sin(ang)

def apply_rope(x, cos, sin):
    half = HEAD_DIM // 2
    x1, x2 = x[..., :half], x[..., half:]
    c, s = cos[None, :, None, :], sin[None, :, None, :]
    return jnp.concatenate([x1 * c - x2 * s, x1 * s + x2 * c], axis=-1).astype(x.dtype)

def project(h, w_in, q_norm_g, k_norm_g):
    B, N, _ = h.shape
    qa, ka, va, qr, kr, vr, gr = jnp.split(h @ w_in, SPLITS, axis=-1)
    heads = lambda a: a.reshape(B, N, -1, HEAD_DIM)
    qa = rms_norm(heads(qa), q_norm_g)
    ka = rms_norm(heads(ka), k_norm_g)
    return qa, ka, heads(va), heads(qr), heads(kr) * ATTN_SCALE, heads(vr), gr

def gqa_block(q, k, v):
    B, Q = q.shape[:2]
    qg = q.reshape(B, Q, ATTN_KV_HEADS, GQA_GROUP, HEAD_DIM)
    s = jnp.einsum('bqkgd,btkd->bkgqt', qg, k, preferred_element_type=jnp.float32) * ATTN_SCALE
    p = jax.nn.softmax(s, axis=-1).astype(v.dtype)
    o = jnp.einsum('bkgqt,btkd->bqkgd', p, v)
    return o.reshape(B, Q, ATTN_WIDTH)

def latent_attention(q, k_lat, v_lat, k_ctx, v_ctx):
    B, N = q.shape[:2]
    k_all = jnp.concatenate([k_ctx, k_lat], axis=1)
    v_all = jnp.concatenate([v_ctx, v_lat], axis=1)
    qb = q.reshape(B, N // QBLOCK, QBLOCK, ATTN_HEADS, HEAD_DIM).swapaxes(0, 1)
    o = lax.map(lambda qi: gqa_block(qi, k_all, v_all), qb)
    return o.swapaxes(0, 1).reshape(B, N, ATTN_WIDTH)

def retention_chunkwise(q, k, v, log_gamma, state0):
    B, N, H, d = q.shape
    C = RET_CHUNK
    nc = N // C
    lg = log_gamma.astype(jnp.float32)
    chunks = lambda a: a.astype(jnp.float32).reshape(B, nc, C, H, d).transpose(1, 0, 3, 2, 4)
    pos = jnp.arange(C, dtype=jnp.float32)
    diff = pos[:, None] - pos[None, :]
    decay_mat = jnp.where(diff >= 0, jnp.exp(lg[:, None, None] * jnp.maximum(diff, 0.0)), 0.0)
    q_decay = jnp.exp(lg[:, None] * (pos + 1.0))[..., None]
    k_decay = jnp.exp(lg[:, None] * (C - 1.0 - pos))[..., None]
    chunk_decay = jnp.exp(lg * C)[:, None, None]

    def step(state, qkv):
        qc, kc, vc = qkv
        inner = jnp.einsum('bhid,bhjd->bhij', qc, kc) * decay_mat
        o = jnp.einsum('bhij,bhjd->bhid', inner, vc) + jnp.einsum('bhid,bhde->bhie', qc, state) * q_decay
        state = state * chunk_decay + jnp.einsum('bhjd,bhje->bhde', kc * k_decay, vc)
        return state, o

    state, o = lax.scan(step, state0.astype(jnp.float32), (chunks(q), chunks(k), chunks(v)))
    return o.transpose(1, 0, 3, 2, 4).reshape(B, N, H, d), state

def bidir_retention(q, k, v, lg_f, lg_b, state_f, state_b):
    o_f, s_f = retention_chunkwise(q, k, v, lg_f, state_f)
    o_b, s_b = retention_chunkwise(q[:, ::-1], k[:, ::-1], v[:, ::-1], lg_b, state_b)
    return o_f + o_b[:, ::-1], s_f, s_b

def merge_heads(att, ret, g_r, w_out):
    B, N = att.shape[:2]
    ret = head_group_norm(ret).reshape(B, N, RET_WIDTH).astype(g_r.dtype) * jax.nn.silu(g_r)
    return jnp.concatenate([att, ret], axis=-1) @ w_out

def swiglu(h, w_ffn_in, w_ffn_out):
    a, b = jnp.split(h @ w_ffn_in, 2, axis=-1)
    return (jax.nn.silu(a) * b) @ w_ffn_out

def first_inputs(seed: int = 0) -> dict:
    key = jax.random.key(seed)
    ks = jax.random.split(key, 18)
    D = D_MODEL
    nrm = lambda k, shape: jax.random.normal(k, shape, jnp.float32)
    w = lambda k, shape, fan_in, g=1.0: nrm(k, shape) * (g * fan_in ** -0.5)
    gain = lambda k, shape: 1.0 + 0.05 * nrm(k, shape)
    gammas = 1.0 - 2.0 ** (-5.0 - jnp.arange(RET_HEADS, dtype=jnp.float32))
    base = jnp.log(-jnp.log(gammas))
    return {
        'x': nrm(ks[0], (BATCH, SEQ, D)),
        'c': nrm(ks[1], (BATCH, D)),
        'ctx': nrm(ks[2], (BATCH, CTX_LEN, D)),
        'c_ctx': nrm(ks[3], (D,)),
        'w_mod': w(ks[4], (DEPTH, D, N_MOD * D), D, 0.5),
        'b_mod': 0.02 * nrm(ks[5], (DEPTH, N_MOD * D)),
        'g_pre_mix': gain(ks[6], (DEPTH, D)),
        'g_post_mix': gain(ks[7], (DEPTH, D)),
        'g_pre_ffn': gain(ks[8], (DEPTH, D)),
        'g_post_ffn': gain(ks[9], (DEPTH, D)),
        'w_in': w(ks[10], (DEPTH, D, IN_PROJ_WIDTH), D),
        'q_norm_g': gain(ks[11], (DEPTH, HEAD_DIM)),
        'k_norm_g': gain(ks[12], (DEPTH, HEAD_DIM)),
        'ret_decay_fwd': base + 0.1 * nrm(ks[13], (DEPTH, RET_HEADS)),
        'ret_decay_bwd': base + 0.1 * nrm(ks[14], (DEPTH, RET_HEADS)),
        'w_out': w(ks[15], (DEPTH, MIX_WIDTH, D), MIX_WIDTH),
        'w_ffn_in': w(ks[16], (DEPTH, D, 2 * FFN_HIDDEN), D),
        'w_ffn_out': w(ks[17], (DEPTH, FFN_HIDDEN, D), FFN_HIDDEN),
    }

def first_block(x, c, ctx, c_ctx, w_mod, b_mod, g_pre_mix, g_post_mix, g_pre_ffn, g_post_ffn,
              w_in, q_norm_g, k_norm_g, ret_decay_fwd, ret_decay_bwd, w_out, w_ffn_in, w_ffn_out):
    B, n_lat, _ = x.shape
    rows = n_lat // GRID_W
    cos, sin = axial_rope(rows)
    for layer in range(DEPTH):
        mod_x = (jax.nn.silu(c) @ w_mod[layer] + b_mod[layer])[:, None, :]
        mod_c = jax.nn.silu(c_ctx) @ w_mod[layer] + b_mod[layer]
        sh_m, sc_m, gt_m, sh_f, sc_f, gt_f = jnp.split(mod_x, N_MOD, axis=-1)
        csh_m, csc_m, cgt_m, csh_f, csc_f, cgt_f = jnp.split(mod_c, N_MOD, axis=-1)
        lg_f = -jnp.exp(ret_decay_fwd[layer].astype(jnp.float32))
        lg_b = -jnp.exp(ret_decay_bwd[layer].astype(jnp.float32))

        hx = modulate(rms_norm(x, g_pre_mix[layer]), sh_m, sc_m)
        hc = modulate(rms_norm(ctx, g_pre_mix[layer]), csh_m, csc_m)
        qa_x, ka_x, va_x, qr_x, kr_x, vr_x, gr_x = project(hx, w_in[layer], q_norm_g[layer], k_norm_g[layer])
        qa_c, ka_c, va_c, qr_c, kr_c, vr_c, gr_c = project(hc, w_in[layer], q_norm_g[layer], k_norm_g[layer])

        zero_state = jnp.zeros((B, RET_HEADS, HEAD_DIM, HEAD_DIM), jnp.float32)
        ret_c, st_f, st_b = bidir_retention(qr_c, kr_c, vr_c, lg_f, lg_b, zero_state, zero_state)

        att_x = latent_attention(apply_rope(qa_x, cos, sin), apply_rope(ka_x, cos, sin), va_x, ka_c, va_c)
        ret_x, _, _ = bidir_retention(apply_rope(qr_x, cos, sin), apply_rope(kr_x, cos, sin), vr_x,
                                      lg_f, lg_b, st_f, st_b)
        mix_x = merge_heads(att_x, ret_x, gr_x, w_out[layer])
        x_new = x + gt_m * rms_norm(mix_x, g_post_mix[layer])
        hf = modulate(rms_norm(x_new, g_pre_ffn[layer]), sh_f, sc_f)
        x_new = x_new + gt_f * rms_norm(swiglu(hf, w_ffn_in[layer], w_ffn_out[layer]), g_post_ffn[layer])

        if layer < DEPTH - 1:
            att_c = gqa_block(qa_c, ka_c, va_c)
            mix_c = merge_heads(att_c, ret_c, gr_c, w_out[layer])
            ctx = ctx + cgt_m * rms_norm(mix_c, g_post_mix[layer])
            hfc = modulate(rms_norm(ctx, g_pre_ffn[layer]), csh_f, csc_f)
            ctx = ctx + cgt_f * rms_norm(swiglu(hfc, w_ffn_in[layer], w_ffn_out[layer]), g_post_ffn[layer])
        x = x_new
    return x


D_MIX = D_MODEL
HGRN_W = D_MIX // 2
CONV_W = D_MIX - HGRN_W
HGRN_HEADS = 4
HGRN_DV = HGRN_W // HGRN_HEADS
HGRN_DK = 128
HGRN_F = HGRN_HEADS * HGRN_DK
CONV_GROUPS = 8
CONV_K = 3
CHUNK = 64
MEM_LEN = 256
MEM_HEADS = 4
MEM_HD = D_MODEL // MEM_HEADS
D_FF = int(math.ceil(8 * D_MODEL / 3 / 256) * 256)
IN_COLS = 3 * HGRN_F // HGRN_F * 0 + HGRN_F + HGRN_F + HGRN_W + HGRN_W + 3 * CONV_W


def rms_norm_2(x, g):
    xf = x.astype(jnp.float32)
    y = xf * lax.rsqrt(jnp.mean(xf * xf, axis=-1, keepdims=True) + EPS)
    return (y * g.astype(jnp.float32)).astype(x.dtype)

def swiglu_2(h, w_gate, w_up, w_down):
    return (jax.nn.silu(h @ w_gate) * (h @ w_up)) @ w_down

def hgrn2_chunkwise(q, k, v, logf):
    b_, s_, h_, dk = q.shape
    dv = v.shape[-1]
    n = s_ // CHUNK

    def to_chunks(t):
        return t.astype(jnp.float32).reshape(b_, n, CHUNK, h_, t.shape[-1]).transpose(1, 0, 3, 2, 4)

    qc, kc, vc, lc = to_chunks(q), to_chunks(k), to_chunks(v), to_chunks(logf)
    bc = jnp.cumsum(lc, axis=-2)
    causal = jnp.tril(jnp.ones((CHUNK, CHUNK), dtype=bool))[None, None, :, :, None]

    def step(state, inp):
        qi, ki, vi, bi = inp
        diff = bi[:, :, :, None, :] - bi[:, :, None, :, :]
        decay = jnp.exp(jnp.where(causal, diff, -jnp.inf))
        scores = jnp.einsum('bhtk,bhsk,bhtsk->bhts', qi, ki, decay)
        o = jnp.einsum('bhts,bhsv->bhtv', scores, vi) + \
            jnp.einsum('bhtk,bhkv->bhtv', qi * jnp.exp(bi), state)
        b_last = bi[:, :, -1:, :]
        new_state = jnp.exp(b_last[:, :, 0, :])[..., None] * state + \
            jnp.einsum('bhsk,bhsv->bhkv', ki * jnp.exp(b_last - bi), vi)
        return new_state, o

    s0 = jnp.zeros((b_, h_, dk, dv), jnp.float32)
    _, o = lax.scan(step, s0, (qc, kc, vc, bc))
    return o.transpose(1, 0, 3, 2, 4).reshape(b_, s_, h_, dv)

def causal_depthwise_conv(u, w):
    s_ = u.shape[1]
    up = jnp.pad(u, ((0, 0), (CONV_K - 1, 0), (0, 0)))
    return sum(w[:, j] * up[:, j:j + s_, :] for j in range(CONV_K))

def second_inputs(seed: int = 0) -> dict:
    key = jax.random.key(seed)
    ks = jax.random.split(key, 24)
    L = DEPTH

    def w(k, shape, fan_in):
        return jax.random.normal(k, shape, jnp.float32) * fan_in ** -0.5

    def gain(k, shape):
        return 1.0 + 0.02 * jax.random.normal(k, shape, jnp.float32)

    return {
        "x": jax.random.normal(ks[0], (BATCH, SEQ, D_MODEL), jnp.float32),
        "mem": jax.random.normal(ks[1], (BATCH, MEM_LEN, D_MODEL), jnp.float32),
        "ffn1_norm": gain(ks[2], (L, D_MODEL)),
        "ffn1_gate": w(ks[3], (L, D_MODEL, D_FF), D_MODEL),
        "ffn1_up": w(ks[4], (L, D_MODEL, D_FF), D_MODEL),
        "ffn1_down": w(ks[5], (L, D_FF, D_MODEL), D_FF),
        "mix_norm": gain(ks[6], (L, D_MODEL)),
        "w_in": w(ks[7], (L, D_MODEL, IN_COLS), D_MODEL),
        "lb_param": 0.1 * jax.random.normal(ks[8], (L + 1, HGRN_F), jnp.float32),
        "hgrn_out_norm": gain(ks[9], (L, HGRN_W)),
        "conv_w": w(ks[10], (L, CONV_W, CONV_K), CONV_K),
        "w_out": w(ks[11], (L, D_MIX, D_MODEL), D_MIX),
        "xattn_norm": gain(ks[12], (L, D_MODEL)),
        "mem_norm": gain(ks[13], (L, D_MODEL)),
        "w_q_mem": w(ks[14], (L, D_MODEL, D_MODEL), D_MODEL),
        "w_kv_mem": w(ks[15], (L, D_MODEL, 2 * D_MODEL), D_MODEL),
        "w_o_mem": w(ks[16], (L, D_MODEL, D_MODEL), D_MODEL),
        "ffn2_norm": gain(ks[17], (L, D_MODEL)),
        "ffn2_gate": w(ks[18], (L, D_MODEL, D_FF), D_MODEL),
        "ffn2_up": w(ks[19], (L, D_MODEL, D_FF), D_MODEL),
        "ffn2_down": w(ks[20], (L, D_FF, D_MODEL), D_FF),
        "final_norm": gain(ks[21], (D_MODEL,)),
    }

def second_block(x, mem, ffn1_norm, ffn1_gate, ffn1_up, ffn1_down, mix_norm, w_in,
              lb_param, hgrn_out_norm, conv_w, w_out, xattn_norm, mem_norm,
              w_q_mem, w_kv_mem, w_o_mem, ffn2_norm, ffn2_gate, ffn2_up,
              ffn2_down, final_norm):
    b_, s_, _ = x.shape
    lb_all = jnp.cumsum(jax.nn.softmax(lb_param.astype(jnp.float32), axis=0), axis=0)

    for l in range(DEPTH):
        x = x + 0.5 * swiglu_2(rms_norm_2(x, ffn1_norm[l]), ffn1_gate[l], ffn1_up[l], ffn1_down[l])

        h = rms_norm_2(x, mix_norm[l])
        z = h @ w_in[l]
        o1 = HGRN_F; o2 = o1 + HGRN_F; o3 = o2 + HGRN_W; o4 = o3 + HGRN_W
        o5 = o4 + CONV_W; o6 = o5 + CONV_W
        zq, zf, zi, zg = z[..., :o1], z[..., o1:o2], z[..., o2:o3], z[..., o3:o4]
        zb, zc, zu = z[..., o4:o5], z[..., o5:o6], z[..., o6:]

        lb = lb_all[l]
        f = lb + (1.0 - lb) * jax.nn.sigmoid(zf.astype(jnp.float32))
        logf = jnp.log(f)
        kk = 1.0 - f
        q = jax.nn.silu(zq.astype(jnp.float32)) * HGRN_DK ** -0.5
        shp_k = (b_, s_, HGRN_HEADS, HGRN_DK)
        o_h = hgrn2_chunkwise(q.reshape(shp_k), kk.reshape(shp_k),
                              zi.reshape(b_, s_, HGRN_HEADS, HGRN_DV), logf.reshape(shp_k))
        g_h = hgrn_out_norm[l].astype(jnp.float32).reshape(HGRN_HEADS, HGRN_DV)
        o_h = o_h * lax.rsqrt(jnp.mean(o_h * o_h, axis=-1, keepdims=True) + EPS) * g_h
        y_hgrn = (o_h.reshape(b_, s_, HGRN_W) * jax.nn.silu(zg.astype(jnp.float32))).astype(x.dtype)

        y_conv = zb * causal_depthwise_conv(zc * zu, conv_w[l])

        x = x + jnp.concatenate([y_hgrn, y_conv.astype(x.dtype)], axis=-1) @ w_out[l]

        hq = rms_norm_2(x, xattn_norm[l])
        mn = rms_norm_2(mem, mem_norm[l])
        qm = (hq @ w_q_mem[l]).reshape(b_, s_, MEM_HEADS, MEM_HD)
        kv = mn @ w_kv_mem[l]
        km = kv[..., :D_MODEL].reshape(b_, MEM_LEN, MEM_HEADS, MEM_HD)
        vm = kv[..., D_MODEL:].reshape(b_, MEM_LEN, MEM_HEADS, MEM_HD)
        sc = jnp.einsum('bshd,bmhd->bhsm', qm.astype(jnp.float32), km.astype(jnp.float32)) * MEM_HD ** -0.5
        p = jax.nn.softmax(sc, axis=-1)
        att = jnp.einsum('bhsm,bmhd->bshd', p, vm.astype(jnp.float32)).astype(x.dtype)
        x = x + att.reshape(b_, s_, D_MODEL) @ w_o_mem[l]

        x = x + 0.5 * swiglu_2(rms_norm_2(x, ffn2_norm[l]), ffn2_gate[l], ffn2_up[l], ffn2_down[l])

    return rms_norm_2(x, final_norm)


def setup_inputs(seed=0):
    out = dict(first_inputs(seed))
    for name, value in second_inputs(seed + 1).items():
        if name != "x":
            out[name + "_2"] = value
    return out


def reference(
    x, c, ctx, c_ctx, w_mod, b_mod, g_pre_mix, g_post_mix, g_pre_ffn, g_post_ffn, w_in,
    q_norm_g, k_norm_g, ret_decay_fwd, ret_decay_bwd, w_out, w_ffn_in, w_ffn_out, mem_2,
    ffn1_norm_2, ffn1_gate_2, ffn1_up_2, ffn1_down_2, mix_norm_2, w_in_2, lb_param_2,
    hgrn_out_norm_2, conv_w_2, w_out_2, xattn_norm_2, mem_norm_2, w_q_mem_2, w_kv_mem_2,
    w_o_mem_2, ffn2_norm_2, ffn2_gate_2, ffn2_up_2, ffn2_down_2, final_norm_2,
):
    x = first_block(
        x, c, ctx, c_ctx, w_mod, b_mod, g_pre_mix, g_post_mix, g_pre_ffn, g_post_ffn, w_in,
        q_norm_g, k_norm_g, ret_decay_fwd, ret_decay_bwd, w_out, w_ffn_in, w_ffn_out,
    )
    return second_block(
        x, mem_2, ffn1_norm_2, ffn1_gate_2, ffn1_up_2, ffn1_down_2, mix_norm_2, w_in_2,
        lb_param_2, hgrn_out_norm_2, conv_w_2, w_out_2, xattn_norm_2, mem_norm_2, w_q_mem_2,
        w_kv_mem_2, w_o_mem_2, ffn2_norm_2, ffn2_gate_2, ffn2_up_2, ffn2_down_2, final_norm_2,
    )


_drawn_inputs = setup_inputs


def setup_inputs(seed=0):
    import zlib

    import numpy as np

    out = dict(_drawn_inputs(seed))
    spreads = {}
    factors = {'g_post_mix': 2.733,
     'g_post_ffn': 2.841,
     'q_norm_g': 8.0,
     'k_norm_g': 8.0,
     'ffn1_norm_2': 5.902,
     'mix_norm_2': 2.919,
     'lb_param_2': 8.0,
     'hgrn_out_norm_2': 8.0,
     'xattn_norm_2': 8.0,
     'mem_norm_2': 8.0,
     'ffn2_norm_2': 24.046,
     'final_norm_2': 8.085}
    for name, (base, spread) in spreads.items():
        noise = np.random.default_rng([zlib.crc32(name.encode()), seed]).standard_normal(out[name].shape)
        drawn = base * np.exp(spread * noise) if base else spread * noise
        out[name] = __import__('jax').numpy.asarray(drawn.astype(out[name].dtype))
    for name, factor in factors.items():
        out[name] = (out[name] * factor).astype(out[name].dtype)
    return out
```

```python
from contextlib import ExitStack

import numpy as np

import concourse.bass as bass
from concourse import mybir

F32 = mybir.dt.float32
F32R = mybir.dt.float32r
I32 = mybir.dt.int32
ALU = mybir.AluOpType
ACT = mybir.ActivationFunctionType
AX = mybir.AxisListType

P = 128
T = 256
TB = T // P
D = 1024
KC = D // P
HD = 64
HEADS = 8
KV_HEADS = 2
GROUP = HEADS // KV_HEADS
PAIRS = HEADS // 2
FFN = 2816
UP = FFN // 256
HG_HEADS = 4
MEM_HEADS = 4
MEM_HD = D // MEM_HEADS
EPS = 1e-6
UNIT = 2048
RING = 3
LEVELS = 7

W_KV = 0
W_IN = W_KV + 8
W_OUT = W_IN + 11
W_UP = [W_OUT + 4, 0, 0]
W_DN = [W_UP[0] + 2 * UP, 0, 0]
W_UP[1] = W_DN[0] + UP
W_DN[1] = W_UP[1] + 2 * UP
W_IN2 = W_DN[1] + UP
W_OUT2 = W_IN2 + 14
W_Q = W_OUT2 + 4
W_O = W_Q + 4
W_UP[2] = W_O + 4
W_DN[2] = W_UP[2] + 2 * UP
N_W = W_DN[2] + UP
N_MOD = 24
MOD_A = 8

STREAM = [("w", v) for v in range(W_KV, W_IN)] + [("mod", m) for m in range(MOD_A)]
IN_MODS = [1, 1, 2, 2, 2, 2, 2, 1, 1, 1, 1]
_m = MOD_A
for _j in range(11):
    STREAM.append(("w", W_IN + _j))
    for _ in range(IN_MODS[_j]):
        STREAM.append(("mod", _m))
        _m += 1
STREAM += [("w", v) for v in range(W_OUT, N_W)]
HEAD_UNITS = W_OUT + N_MOD
RAW_AT = {unit: u for u, unit in enumerate(STREAM)}

COLS = {}
_at = 0
for _name, _n in [("g_pre_mix", 8), ("g_post_mix", 8), ("g_pre_ffn", 8), ("g_post_ffn", 8), ("b_mod", 48),
                  ("ffn1_norm", 8), ("mix_norm", 8), ("xattn_norm", 8), ("mem_norm", 8), ("ffn2_norm", 8),
                  ("conv_w", 12), ("cond", 16), ("decay_rows", 16), ("decay_pairs", 8), ("qk_gain", 128)]:
    COLS[_name] = (_at, _at + _n)
    _at += _n
N_COLS = _at

CONST1 = {}
_at = 0
for _name, _n in [("fwd_dist", 384), ("bwd_dist", 384), ("from_start", T), ("to_end", T), ("ctx_dist", 4),
                  ("rope_cos", TB * HD), ("rope_sin", TB * HD)]:
    CONST1[_name] = (_at, _at + _n)
    _at += _n
N_CONST1 = _at


def shape_constants():
    i = np.arange(P, dtype=np.float32)
    ident = np.eye(P, dtype=np.float32)
    fixed = np.concatenate([ident, np.ones((P, P), np.float32)], axis=1)

    diff = i[None, :] - i[:, None]
    zero = np.zeros((P, P), np.float32)
    fwd = np.concatenate([zero, np.maximum(diff, 0), P + diff], axis=1)
    bwd = np.concatenate([P - diff, np.maximum(-diff, 0), zero], axis=1)
    t = np.arange(T, dtype=np.float32)
    rows = lambda a: np.broadcast_to(a, (P, a.shape[-1]))
    ctx_dist = np.stack([T - 1 - i, T - 1 - (i + P), i, i + P], axis=1)
    inv = (10000.0 ** (-np.arange(HD // 4, dtype=np.float32) / (HD // 4))).astype(np.float32)
    row, col = np.floor(t / 64), t % 64
    ang = np.concatenate([row[:, None] * inv, col[:, None] * inv], axis=1).astype(np.float32)
    cos, sin = np.cos(ang), np.sin(ang)
    tiles = lambda a: a.reshape(TB, P, HD).transpose(1, 0, 2).reshape(P, TB * HD)
    first = np.concatenate([fwd, bwd, rows(t + 1), rows(T - t), ctx_dist,
                            tiles(np.concatenate([cos, cos], 1)), tiles(np.concatenate([-sin, sin], 1))], axis=1)

    sums, masks = [], [ident]
    src, dst = np.arange(P)[:, None], np.arange(P)[None, :]
    for level in range(LEVELS):
        h = 1 << level
        seg_s, seg_t = src // (2 * h), dst // (2 * h)
        late_s, late_t = (src // h) % 2 == 1, (dst // h) % 2 == 1
        same = seg_s == seg_t
        sums.append(same & ((late_t & late_s & (src <= dst)) | (~late_t & ~late_s & (src > dst))))
        masks.append(same & ~late_s & late_t)
    sums += [src > dst, src <= dst]
    second = np.concatenate([m.astype(np.float32) for m in sums + masks], axis=1)
    return [np.ascontiguousarray(a, dtype=np.float32) for a in (fixed, first, second)]


class BankPlan:

    def __init__(self):
        self.fills = [0] * 8
        self.signals = [0] * 8
        self.of = {}

    def streamed(self, name, bank):
        self.of[name] = (bank, self.fills[bank], None)
        self.fills[bank] += 1

    def signalled(self, name, bank):
        self.of[name] = (bank, self.fills[bank], self.signals[bank])
        self.fills[bank] += 1
        self.signals[bank] += 1


def plan_banks():
    plan = BankPlan()

    def transposes(stage, n):
        for q in range(n):
            plan.signalled((stage, q), 5 + q % 2)

    def ffn(f):
        for c in range(UP):
            for tb in range(TB):
                plan.streamed(("up", f, c, tb), (c % 3) * 2 + tb)
        for c in range(UP):
            plan.signalled(("gateT", f, c), 6)
        for tb in range(TB):
            for half in range(2):
                plan.streamed(("down", f, tb, half), tb * 2 + half)

    transposes("memT", 4)
    for c in range(4):
        for tb in range(TB):
            plan.streamed(("kv", c, tb), (c % 2) * 2 + tb)
    plan.streamed("mod_a", 7)
    transposes("keyT", 4)
    transposes("xT", 4)
    transposes("ctxT", 4)
    for part, banks in [("kr", [0, 1, 2, 3]), ("vr", [4, 5, 6, 0]), ("kava", [1, 2, 3, 4]),
                        ("qa", [5, 6]), ("qr", [0, 1]), ("gr", [2, 3])]:
        for tile, bank in enumerate(banks):
            plan.streamed((part, tile), bank)
    plan.streamed("mod_b", 7)
    transposes("gain_row", 4)
    plan.signalled("states", 7)
    transposes("krT", 2)
    transposes("kaT", 1)
    transposes("qaT", 2)
    transposes("qrT", 2)
    for s in range(2 * HEADS):
        plan.signalled(("scores", s), s % 2)
        if s % 2 == 0:
            plan.signalled(("ret_scores", s // 2), 3)
        plan.signalled(("probsT", s), 2)
    plan.streamed(("att", 0), 4)
    plan.streamed(("att", 1), 5)
    plan.streamed(("ret", 0), 6)
    plan.streamed(("ret", 1), 7)
    transposes("mixT", 4)
    for c in range(2):
        for tb in range(TB):
            plan.streamed(("mix_out", tb, c), tb * 2 + c)
    transposes("ffn0T", 4)
    ffn(0)
    transposes("ffn1T", 4)
    ffn(1)
    transposes("mix2T", 4)
    for part, banks in [("zf", [0, 1]), ("zq", [2, 3]), ("zi", [0, 1]), ("zc", [2, 3]), ("zu", [0, 1]),
                        ("zb", [2, 3]), ("zg", [0, 1])]:
        for tb, bank in enumerate(banks):
            plan.streamed((part, tb), bank)
    transposes("hqT", 2)
    transposes("hkT", 2)
    for blk in range(TB):
        plan.signalled(("diag", blk), 5 + blk)
    for level in range(LEVELS):
        for blk in range(TB):
            plan.signalled(("decay", level, blk), [4, 7][blk])
            plan.signalled(("pairs", level, blk), 5 + blk)
    for blk in range(TB):
        plan.signalled(("decay", LEVELS, blk), [4, 7][blk])
    plan.signalled("cross", 5)
    plan.signalled("uT0", 6)
    plan.signalled("uT1", 5)
    plan.signalled("bT0", 6)
    plan.signalled("bT1", 5)
    for blk in range(TB):
        plan.signalled(("hgrn", blk), [4, 7][blk])
    plan.signalled(("mix2oT", 0), 6)
    plan.signalled(("mix2oT", 1), 5)
    for c in range(2):
        for tb in range(TB):
            plan.streamed(("mix2_out", tb, c), tb * 2 + c)
    transposes("xattT", 4)
    for c in range(2):
        for tb in range(TB):
            plan.streamed(("mq", tb, c), tb * 2 + c)
    transposes("mqT", 4)
    for h in range(MEM_HEADS):
        for tb in range(TB):
            plan.signalled(("mscores", h, tb), [4, 7][tb])
        plan.signalled(("mprobsT", h), 5 + h % 2)
    for half in range(2):
        for tb in range(TB):
            plan.streamed(("matt", half, tb), tb * 2 + half)
    transposes("mattT", 4)
    for c in range(2):
        for tb in range(TB):
            plan.streamed(("mem_out", tb, c), tb * 2 + c)
    transposes("ffn2T", 4)
    ffn(2)
    return plan


def two_blocks_kernel(nc, io):
    plan = plan_banks()
    sems = ExitStack()
    stack = ExitStack()
    named = {}

    def sem(name):
        if name not in named:
            named[name] = sems.enter_context(nc.semaphore(name))
        return named[name]

    with sems, stack:
        def sb(name, shape, dt=F32):
            return stack.enter_context(nc.sbuf_tensor(name, shape, dt))

        raw = sb("raw", [P, RING, UNIT])
        w_hi = sb("w_hi", [P, RING, UNIT], F32R)
        w_lo = sb("w_lo", [P, RING, UNIT], F32R)
        x = sb("x_res", [P, TB, D])
        hT_hi = sb("hT_hi", [P, KC, T], F32R)
        hT_lo = sb("hT_lo", [P, KC, T], F32R)
        xn = sb("xn", [P, TB, D])
        rows = sb("rows", [P, TB, D])
        memKT = sb("memKT", [P, KC, T])
        memV = sb("memV", [P, TB, D])
        fixed = sb("fixed", [P, 2 * P])
        cols = sb("cols", [P, N_COLS])
        eps = sb("eps", [P, 1])
        ssq = sb("ssq", [P, 2])
        rms = sb("rms", [P, 2])
        rstd = sb("rstd", [P, 2])
        silu_c = sb("silu_c", [P, KC, 2])
        mod = sb("mod", [P, 48, 2])
        a_mix = sb("a_mix", [P, KC, 2])
        a_ffn = sb("a_ffn", [P, KC])
        gain_col = sb("gain_col", [P, 2, KC])
        shifted_T = sb("shifted_T", [P, 2, 2 * T])
        ident = fixed[:, 0:P]
        ones = fixed[:, P:2 * P]

        def col(name, a=0, b=None):
            lo, hi = COLS[name]
            return cols[:, lo + a:(lo + b if b is not None else hi)]

        ARENA = 18440
        spot = ExitStack()
        hcT_hi = spot.enter_context(nc.sbuf_tensor("hcT_hi", [P, KC, T], F32R))
        hcT_lo = spot.enter_context(nc.sbuf_tensor("hcT_lo", [P, KC, T], F32R))
        spot.close()
        gT_hi = spot.enter_context(nc.sbuf_tensor("gT_hi", [P, 2 * UP, T], F32R))
        gT_lo = spot.enter_context(nc.sbuf_tensor("gT_lo", [P, 2 * UP, T], F32R))
        spot.close()
        logf_hi = spot.enter_context(nc.sbuf_tensor("logf_hi", [P, TB, 512], F32R))
        logf_lo = spot.enter_context(nc.sbuf_tensor("logf_lo", [P, TB, 512], F32R))
        sums_r = spot.enter_context(nc.sbuf_tensor("sums_r", [P, LEVELS + 2, P], F32R))
        spot.close()
        arena = sb("arena", [P, ARENA])

        def carve(start, *shape):
            n = int(np.prod(shape))
            assert start + n <= ARENA, (start, n)
            v = arena[:, start:start + n]
            if len(shape) == 2:
                return v.rearrange("p (a b) -> p a b", b=shape[1])
            if len(shape) == 3:
                return v.rearrange("p (a b c) -> p a b c", b=shape[1], c=shape[2])
            return v

        at = 4096
        qaT, kaT = carve(0, PAIRS, T), carve(1024, 4 * P)
        qrT, krT = carve(1536, PAIRS, T), carve(2560, PAIRS, T)
        const1 = carve(at, N_CONST1); at += N_CONST1
        vr = carve(at, 4, 512); ctx_in = carve(at, TB, D); at += 2048
        kava = carve(at, 4, 256); at += 1024
        staged = carve(at, 4, 512); mem_in = carve(at, TB, D)
        decay_arg, decay_mat = carve(at, 384), carve(at + 384, 384)
        q_dec = carve(at + 768, 2, T); q_decayed = carve(at + 1280, 2, T); at += 2048
        krn = carve(at, TB, 512); y_mix = carve(at, TB, D); at += 1024
        qrn = carve(at, TB, 512); at += 1024
        qan = carve(at, TB, 512); at += 1024
        k_fb = carve(at, 2, TB, 512); mem_k = carve(at, TB, D)
        ret_p, probs = carve(at, 2, 2 * T), carve(at + 1024, 2, 512); at += 2048
        rope_a, rope_b = carve(at, 512), carve(at + 512, 512); probsT = carve(at, 2, 4 * P); at += 1024
        silu_gr = carve(at, TB, 512); tables = carve(at, 4, TB * HD); at += 1024
        ka_all = carve(at, 4, P); at += 512
        state = shifted_T[:, 0, :].rearrange("p (a b c) -> p a b c", a=2, b=PAIRS)
        ctx_decay = sb("ctx_decay", [P, 4, HEADS])
        lg_rows = sb("lg_rows", [P, 16])
        lg_pairs = sb("lg_pairs", [P, 8])
        head_ss = sb("head_ss", [P, 16])
        head_rms = sb("head_rms", [P, 16])
        head_rstd = sb("head_rstd", [P, 16])
        row_max = sb("row_max", [P, 16])
        row_sum = sb("row_sum", [P, 16])
        row_inv = sb("row_inv", [P, 16])

        def c1(name, a=0, b=None):
            lo, hi = CONST1[name]
            return const1[:, lo + a:(lo + b if b is not None else hi)]

        gate = carve(2 * 2 * UP * T, 3, TB, 256)
        y_ffn = carve(2 * 2 * UP * T + 3 * TB * 256, TB, D)

        at = 2048 + (LEVELS + 2) * P
        const2 = carve(at, (2 * LEVELS + 3) * P); at += (2 * LEVELS + 3) * P
        fgate = carve(at, TB, 512); at += 1024
        hk = carve(at, TB, 512); uT = carve(at, 4 * (T + 2)); at += 1032
        hq = carve(at, TB, 512); conv = carve(at, 4, T); at += 1024
        hv = carve(at, TB, 512); at += 1024
        zc_sb = carve(at, TB, 512); at += 1024
        zb_sb = carve(at, TB, 512); at += 1024
        silu_zg = carve(at, TB, 512); at += 1024
        hkT, hqT = carve(at, 8 * P), carve(at + 1024, 8 * P); at += 2048
        scT = carve(at, 8 * P); at += 1024
        crossT = carve(at, 4 * P); at += 512
        head_row = rows[:, 1, 0:512]
        lb_p = carve(at, 2, 512); lb = carve(at + 1024, 512); one_lb = carve(at + 1536, 512); at += 2048
        hgrn_sq = lb_p[:, 0, :]
        level_mask = const2[:, (LEVELS + 2) * P:].rearrange("p (l t) -> p l t", t=P)
        qk_dec = [xn[:, b, :] for b in range(2)]

        mq = carve(0, TB, D)
        mqT = carve(2048, KC, T)
        mprobs = carve(4096, 2, T)
        mprobsT = carve(4608, 2, 4 * P)

        bank = [stack.enter_context(nc.psum_tensor(f"bank{b}", [P, 512], F32)) for b in range(8)]
        bank_full = [sem(f"bank{b}_full") for b in range(8)]
        bank_read = [sem(f"bank{b}_read") for b in range(8)]
        raw_ready = [sem(f"raw_ready{s}") for s in range(RING)]
        mod_used = sem("mod_used")
        hi_ready = sem("hi_ready")
        split_ready = sem("split_ready")
        split_used = sem("split_used")

        def free(eng, name):
            b, k, _ = plan.of[name]
            if k:
                eng.wait_ge(bank_read[b], k)
            return bank[b]

        def filled(eng, name):
            b, _, s = plan.of[name]
            eng.wait_ge(bank_full[b], s + 1)
            return bank[b]

        def read_out(eng, name):
            b, k, _ = plan.of[name]
            eng.wait_ge(bank_read[b], k + 1)

        def bank_of(name):
            return bank[plan.of[name][0]]

        def full_sem(name):
            return bank_full[plan.of[name][0]]

        def read_sem(name):
            return bank_read[plan.of[name][0]]

        def heads_bc(ap, n, d):
            return ap.unsqueeze(2).to_broadcast([P, n, d])

        def over_heads(ap, n, d):
            return ap.unsqueeze(1).to_broadcast([P, n, d])

        def x_ready(n):
            return lambda eng: eng.wait_ge(sem("x_ready"), n)

        def x_added(name):
            return lambda eng: [read_out(eng, (*name, tb, c)) for tb in range(TB) for c in range(2)]

        shift_buf = lambda k: shifted_T[:, k % 2, :].rearrange("p (a t) -> p a t", t=T)

        block = stack.enter_context(nc.Block())

        @block.sync
        def _(sp):
            small = [(mem_in, io["mem"], "mem_loaded"), (cols[:], io["cols"], "cols_loaded"),
                     (fixed[:], io["fixed"], "fixed_loaded")]
            for dst, src, name in small:
                sp.dma_start(dst, src).then_inc(sem(name), 16)
            for u in range(HEAD_UNITS):
                if u >= RING:
                    kind, n = STREAM[u - RING]
                    sp.wait_ge(split_ready if kind == "w" else mod_used, n + 1)
                sp.dma_start(raw[:, u % RING, :], io["weights"][u]).then_inc(raw_ready[u % RING], 16)
                if u == 1:
                    for dst, src, name in [(x[:], io["x"], "x_loaded"), (ctx_in, io["ctx"], "ctx_loaded"),
                                           (const1, io["const1"], "const1_loaded")]:
                        sp.dma_start(dst, src).then_inc(sem(name), 16)
            first = len(STREAM) - HEAD_UNITS
            for u in range(HEAD_UNITS, HEAD_UNITS + RING):
                kind, n = STREAM[u - RING]
                sp.wait_ge(split_ready if kind == "w" else mod_used, n + 1)
                sp.dma_start(raw[:, u % RING, :], io["weights"][u]).then_inc(raw_ready[u % RING], 16)
            assert first % RING == 0
            with sp.Fori(0, first // RING - 1) as i:
                for j in range(RING):
                    u0 = HEAD_UNITS + RING + j
                    sp.wait_ge(split_ready, i * RING + (W_OUT + j + 1))
                    sp.dma_start(raw[:, u0 % RING, :], io["weights"][bass.ds(i * RING + u0, 1)].rearrange("a p n -> (a p) n"))\
                        .then_inc(raw_ready[u0 % RING], 16)
            for tb in range(TB):
                sp.wait_ge(sem("out_ready"), tb + 1)
                sp.dma_start(io["out"][tb], xn[:, tb, :]).then_inc(sem("stored"), 16)
            sp.wait_ge(sem("stored"), 16 * TB)

        @block.gpsimd
        def _(pool):
            def low_part(v_slot, u_slot, count):
                pool.wait_ge(hi_ready, count)
                pool.tensor_tensor(w_lo[:, v_slot, :], raw[:, u_slot, :], w_hi[:, v_slot, :].bitcast(F32),
                                   ALU.subtract).then_inc(split_ready, 1)

            for v in range(W_OUT):
                low_part(v % RING, RAW_AT[("w", v)] % RING, v + 1)
            with pool.Fori(0, (N_W - W_OUT) // RING) as i:
                for j in range(RING):
                    v0 = W_OUT + j
                    low_part(v0 % RING, RAW_AT[("w", v0)] % RING, i * RING + (v0 + 1))

        @block.scalar
        def _(act):
            chained = [0]

            def chain(ins):
                chained[0] += 1
                ins.then_inc(sem("act_chain"), 1)
                act.wait_ge(sem("act_chain"), chained[0])

            def high_part(v_slot, u_slot, loads, used, waits=True):
                act.wait_ge(raw_ready[u_slot], loads)
                if waits:
                    act.wait_ge(split_used, used)
                act.activation(w_hi[:, v_slot, :], raw[:, u_slot, :], ACT.Copy).then_inc(hi_ready, 1)

            split = [0]

            def split_to(n):
                while split[0] < min(n, N_W):
                    v = split[0]
                    u = RAW_AT[("w", v)]
                    high_part(v % RING, u % RING, 16 * (u // RING + 1), v - RING + 1, v >= RING)
                    split[0] += 1

            def split_behind(p):
                passed = RAW_AT[("w", p + 1)]
                reach = lambda v: all(STREAM[u][0] == "w" or u < passed for u in range(RAW_AT[("w", v)] - RING + 1))
                n = p + 1
                while n < p + 1 + RING and reach(n):
                    n += 1
                split_to(n)

            def used(v):
                act.wait_ge(split_used, v + 1)

            norms = [0]

            def norm_stats(src, ready):
                ready(act)
                n = norms[0]
                norms[0] += 1
                if n:
                    act.wait_ge(sem("norm_rstd"), n)
                act.activation(xn_junk[0], src[:, 0, :], ACT.Square, accum_out=ssq[:, 0:1]).then_inc(sem("norm_ss_a"), 1)
                act.wait_ge(sem("norm_ss_a"), n + 1)
                act.wait_ge(sem("norm_ss_v"), n + 1)
                act.activation(rms[:, :], ssq[:, :], ACT.Sqrt, scale=1.0 / D, bias=eps[:, 0:1]).then_inc(sem("norm_rms"), 1)
                act.wait_ge(sem("norm_rstd"), n + 1)

            xn_junk = [rows[:, 0, :]]

            def norm_scale(src, dst):
                act.activation(dst[:, 0, :], src[:, 0, :], ACT.Copy, scale=rstd[:, 0:1]).then_inc(sem("xn_a"), 1)

            def split_T(stage, gain=None, shifted=False, hi=hT_hi, n=4):
                for q in range(n):
                    if shifted:
                        act.wait_ge(sem("full_T"), shifts[0] + 1)
                        act.activation(hi[:, 2 * q:2 * q + 2, :], shift_buf(shifts[0]), ACT.Copy).then_inc(sem("T_hi"), 1)
                        shifts[0] += 1
                        continue
                    b = filled(act, (stage, q))
                    if gain is None:
                        act.activation(hi[:, 2 * q:2 * q + 2, :].rearrange("p a t -> p (a t)"), b[:, :], ACT.Copy)\
                            .then_inc(sem("T_hi"), 1)
                    else:
                        act.activation(hi[:, 2 * q, :], b[:, 0:T], ACT.Copy, scale=gain[:, 2 * q:2 * q + 1])
                        act.activation(hi[:, 2 * q + 1, :], b[:, T:2 * T], ACT.Copy, scale=gain[:, 2 * q + 1:2 * q + 2])\
                            .then_inc(sem("T_hi"), 1)

            shifts = [0]

            def copy_out(name, dst, func=ACT.Copy, n=512):
                act.activation(dst, bank_of(name)[:, 0:n], func).then_inc(read_sem(name), 1)

            act.wait_ge(sem("eps_set"), 1)
            act.wait_ge(sem("cols_loaded"), 16)
            norm_stats(mem_in, lambda e: e.wait_ge(sem("mem_loaded"), 16))
            norm_scale(mem_in, xn)
            split_to(1)
            split_T("memT", col("mem_norm"))
            split_to(3)
            act.activation(silu_c[:].rearrange("p k c -> p (k c)"), col("cond"), ACT.Silu).then_inc(sem("silu_c"), 1)
            act.activation(lg_rows[:, :], col("decay_rows"), ACT.Exp).then_inc(sem("lg_exp"), 1)
            act.activation(lg_pairs[:, :], col("decay_pairs"), ACT.Exp).then_inc(sem("lg_exp"), 1)
            for c in range(4):
                for half in range(2):
                    split_behind(W_KV + 2 * c + half)
                used(W_KV + 2 * c + 1)
                for tb in range(TB):
                    dst = (mem_k if c < 2 else memV)[:, tb, (c % 2) * 512:(c % 2 + 1) * 512]
                    copy_out(("kv", c, tb), dst)
                if c == 0:
                    norm_stats(x, lambda e: e.wait_ge(sem("x_loaded"), 16))
                    filled(act, ("memT", 3))
                    norm_scale(x, xn)
                if c == 1:
                    norm_stats(ctx_in, lambda e: e.wait_ge(sem("ctx_loaded"), 16))
                    norm_scale(ctx_in, rows)
                if c == 2:
                    act.wait_ge(sem("lg_neg"), 2)
                    act.wait_ge(sem("const1_loaded"), 16)
                    for fb in range(2):
                        for jb in range(TB):
                            a = act.activation(ctx_decay[:, 2 * fb + jb, :], lg_rows[:, 8 * fb:8 * fb + 8], ACT.Exp,
                                               scale=c1("ctx_dist", 2 * fb + jb, 2 * fb + jb + 1))
                            a.then_inc(sem("ctx_decay"), 1)
            for q in range(4):
                b = filled(act, ("keyT", q))
                act.activation(memKT[:, 2 * q:2 * q + 2, :].rearrange("p a t -> p (a t)"), b[:, :], ACT.Copy)\
                    .then_inc(read_sem(("keyT", q)), 1)
            split_T("xT", shifted=True)
            split_T("ctxT", shifted=True, hi=hcT_hi)

            for part, v, n in [("kr", 0, 2), ("vr", 2, 2), ("kava", 4, 1), ("qa", 5, 2), ("qr", 7, 2), ("gr", 9, 2)]:
                split_behind(W_IN + v + n - 1)
                used(W_IN + v + n - 1)
                if part == "kr":
                    for tile in range(4):
                        copy_out((part, tile), staged[:, tile, :])
                elif part == "vr":
                    for tile in range(4):
                        copy_out((part, tile), vr[:, tile, :])
                elif part == "kava":
                    for tile in range(4):
                        copy_out((part, tile), kava[:, tile, :], n=256)
                    act.wait_ge(sem("ka_ss"), 1)
                    act.activation(head_rms[:, 0:8], head_ss[:, 0:8], ACT.Sqrt, scale=1.0 / HD, bias=eps[:, 0:1])\
                        .then_inc(sem("ka_rms"), 1)
                elif part == "qa":
                    act.wait_ge(sem("kr_done"), 1)
                    for tb in range(TB):
                        copy_out((part, tb), staged[:, tb, :])
                    act.wait_ge(sem("qa_ss"), 1)
                    act.activation(head_rms[:, :], head_ss[:, :], ACT.Sqrt, scale=1.0 / HD, bias=eps[:, 0:1])\
                        .then_inc(sem("qa_rms"), 1)
                elif part == "qr":
                    for tb in range(TB):
                        copy_out((part, tb), staged[:, 2 + tb, :])
                else:
                    act.wait_ge(sem("rope_done"), 6)
                    for tb in range(TB):
                        copy_out((part, tb), silu_gr[:, tb, :], ACT.Silu)
            for q in range(4):
                b = filled(act, ("gain_row", q))
                act.activation(rows[:, q // 2, (q % 2) * 512:(q % 2 + 1) * 512], b[:, :], ACT.Copy)\
                    .then_inc(read_sem(("gain_row", q)), 1)
            for name, dst in [("krT", krT), ("kaT", None), ("qaT", qaT), ("qrT", qrT)]:
                for q in range(1 if dst is None else 2):
                    b = filled(act, (name, q))
                    d = kaT if dst is None else dst[:, 2 * q:2 * q + 2, :].rearrange("p a t -> p (a t)")
                    act.activation(d, b[:, :], ACT.Copy).then_inc(read_sem((name, q)), 1)

            def attention_probs(s):
                act.wait_ge(sem("neg_max"), s + 1)
                if s >= 2:
                    filled(act, ("probsT", s - 2))
                act.activation(probs[:, s % 2, :], bank_of(("scores", s))[:, :], ACT.Exp, scale=HD ** -0.5,
                               bias=row_max[:, s:s + 1], accum_out=row_sum[:, s:s + 1]).then_inc(read_sem(("scores", s)), 1)

            for s in range(2 * HEADS):
                r = s // 2
                if s % 2 == 0:
                    act.wait_ge(sem("decay_arg"), r + 1)
                    if r:
                        read_out(act, ("ret_scores", r - 1))
                    act.activation(decay_mat, decay_arg, ACT.Exp).then_inc(sem("decay_mat"), 1)
                    if r % 2 == 0:
                        if r:
                            act.wait_ge(sem("q_decayed"), r)
                        act.activation(q_dec[:, 0, :], c1("from_start"), ACT.Exp, scale=lg_pairs[:, r // 2:r // 2 + 1])
                        act.activation(q_dec[:, 1, :], c1("to_end"), ACT.Exp, scale=lg_pairs[:, 4 + r // 2:5 + r // 2])\
                            .then_inc(sem("q_dec"), 1)
                attention_probs(s)
                b = filled(act, ("probsT", s))
                if s >= 2:
                    act.wait_ge(sem("att_step"), s - 1)
                act.activation(probsT[:, s % 2, :], b[:, :], ACT.Copy).then_inc(read_sem(("probsT", s)), 1)
            for tb in range(TB):
                act.wait_ge(sem("ret_centred"), tb + 1)
                act.activation(probs[:, tb, :], xn[:, tb, 512:1024], ACT.Square).then_inc(sem("ret_sq"), 1)
            act.wait_ge(sem("ret_var"), 1)
            act.activation(head_rms[:, :], head_ss[:, :], ACT.Sqrt, scale=1.0 / HD, bias=eps[:, 0:1])\
                .then_inc(sem("ret_rms"), 1)
            split_T("mixT")

            def post_norm(y, name, last):
                used(last)
                for c in range(2):
                    copy_out((*name, 0, c), y[:, 0, c * 512:(c + 1) * 512])
                read_out(act, (*name, 0, 0))
                read_out(act, (*name, 0, 1))
                norm_stats(y, lambda e: None)

            xn_junk[0] = xn[:, 0, :]
            split_to(W_OUT + 4)
            post_norm(y_mix, ("mix_out",), W_OUT + 3)
            split_to(W_OUT + 4 + RING)

            def ffn(f):
                up, dn = W_UP[f], W_DN[f]

                def silu_gate(c, before, i=None):
                    act.wait_ge(split_used, before)
                    for tb in range(TB):
                        act.activation(gate[:, c % 3, tb, :], bank[(c % 3) * 2 + tb][:, 0:256], ACT.Silu)\
                            .then_inc(sem("gate_silu"), 1)

                g0 = plan.of[("gateT", f, 0)][2]

                def gate_hi(c, full, at):
                    act.wait_ge(bank_full[6], full)
                    act.activation(gT_hi[:, at, :] if isinstance(at, slice) else gT_hi[:, bass.ds(at, 2), :],
                                   bank[6][:, :].rearrange("p (a t) -> p a t", t=T), ACT.Copy).then_inc(sem("gateT_hi"), 1)

                split_to(up + RING)
                for c in range(2):
                    split_to(up + 2 * c + 5)
                    silu_gate(c, up + 2 * c + 2)
                    if c:
                        gate_hi(0, g0 + 1, slice(0, 2))
                v0 = split[0]
                u0 = RAW_AT[("w", v0)]
                assert v0 == up + 7
                with act.Fori(0, 3) as i:
                    for j in range(3):
                        for e in range(2):
                            k = 2 * j + e
                            high_part((v0 + k) % RING, (u0 + k) % RING, i * 32 + 16 * ((u0 + k) // RING + 1),
                                      i * 6 + (v0 + k - RING + 1))
                        c = 2 + j
                        silu_gate(c, i * 6 + (up + 2 * c + 2))
                        gate_hi(c - 1, i * 3 + (g0 + c), i * 6 + 2 * (c - 1))
                split[0] += 18
                split_to(dn + 1 + RING)
                gate_hi(UP - 1, g0 + UP, slice(2 * UP - 2, 2 * UP))
                split_to(dn + UP)

            def pre_norm(stage, ready, gain=None, shifted=False):
                norm_stats(x, ready)
                norm_scale(x, xn)
                split_T(stage, gain, shifted)

            pre_norm("ffn0T", x_ready(1), shifted=True)
            ffn(0)
            post_norm(y_ffn, ("down", 0), W_DN[0] + UP - 1)
            split_to(W_UP[1] + RING)
            pre_norm("ffn1T", x_ready(2), col("ffn1_norm"))
            act.dma_start(rows[:, 0, :], io["final_norm"].to_broadcast([P, D])).then_inc(sem("final_loaded"), 16)
            ffn(1)
            used(W_DN[1] + UP - 1)
            for dst, src, name in [(const2, io["const2"], "const2_loaded"),
                                   (lb_p.rearrange("p a n -> p (a n)"), io["lb_param"].to_broadcast([P, D]), "lb_loaded"),
                                   (head_row, io["hgrn_out_norm"].to_broadcast([P, 512]), "head_row_loaded")]:
                act.dma_start(dst, src).then_inc(sem(name), 16)
            pre_norm("mix2T", x_added(("down", 1)), col("mix_norm"))
            split_to(W_IN2 + RING)

            act.wait_ge(sem("const2_loaded"), 16)
            act.activation(sums_r[:].rearrange("p l t -> p (l t)"), const2[:, 0:(LEVELS + 2) * P], ACT.Copy)\
                .then_inc(sem("sums_ready"), 1)
            act.wait_ge(sem("lb_diff"), 1)
            act.activation(lb_p[:].rearrange("p a n -> p (a n)"), lb_p[:].rearrange("p a n -> p (a n)"), ACT.Exp)\
                .then_inc(sem("lb_exp"), 1)

            def streamed_out(k, part, dst, func=ACT.Copy):
                split_to(W_IN2 + 2 * k + 2 + RING)
                used(W_IN2 + 2 * k + 1)
                for tb in range(TB):
                    copy_out((part, tb), dst[:, tb, :], func)

            def level_decays(level):
                for blk in range(TB):
                    b = filled(act, ("decay", level, blk))
                    if blk == 0 and level >= 2:
                        filled(act, ("pairs", level - 2, 1))
                    act.activation(qk_dec[level % 2][:, blk * 512:(blk + 1) * 512], b[:, :], ACT.Exp)\
                        .then_inc(read_sem(("decay", level, blk)), 1)

            streamed_out(0, "zf", fgate, ACT.Sigmoid)
            act.wait_ge(sem("fgate"), 1)
            streamed_out(1, "zq", hq, ACT.Silu)
            act.activation(fgate[:].rearrange("p a n -> p (a n)"), fgate[:].rearrange("p a n -> p (a n)"), ACT.Ln)\
                .then_inc(sem("logf"), 1)
            act.wait_ge(sem("logf"), 1)
            act.activation(logf_hi[:].rearrange("p a n -> p (a n)"), fgate[:].rearrange("p a n -> p (a n)"), ACT.Copy)\
                .then_inc(sem("logf_hi"), 1)
            streamed_out(2, "zi", hv)
            for q in range(2):
                b = filled(act, ("hqT", q))
                act.activation(hqT[:, q * 512:(q + 1) * 512], b[:, :], ACT.Copy, scale=P ** -0.5)\
                    .then_inc(read_sem(("hqT", q)), 1)
            for q in range(2):
                b = filled(act, ("hkT", q))
                act.activation(hkT[:, q * 512:(q + 1) * 512], b[:, :], ACT.Copy).then_inc(read_sem(("hkT", q)), 1)
            for step in range(8):
                split_to(W_IN2 + 6 + step + RING)
                level_decays(step)
                if step == 1:
                    streamed_out(3, "zc", zc_sb)
                if step == 3:
                    split_to(W_IN2 + 10 + RING)
                if step == 5:
                    streamed_out(5, "zb", zb_sb)
            streamed_out(6, "zg", silu_zg, ACT.Silu)
            for j in range(2):
                b = filled(act, f"uT{j}")
                act.activation(uT.rearrange("p (c t) -> p c t", t=T + 2)[:, 2 * j:2 * j + 2, 2:T + 2],
                               b[:, :].rearrange("p (c t) -> p c t", t=T), ACT.Copy).then_inc(read_sem(f"uT{j}"), 1)
            for j in range(2):
                read_out(act, f"bT{j}")
                act.activation(hT_hi[:, 4 + 2 * j:6 + 2 * j, :], conv[:, 2 * j:2 * j + 2, :], ACT.Copy)\
                    .then_inc(sem("conv_hi"), 1)
            for blk in range(TB):
                b = filled(act, ("hgrn", blk))
                if blk:
                    act.wait_ge(sem("hgrn_ss"), blk)
                act.activation(hgrn_sq, b[:, :], ACT.Square).then_inc(sem("hgrn_sq"), 1)
            act.wait_ge(sem("hgrn_ss"), TB)
            act.activation(head_rms[:, 0:8], head_ss[:, 0:8], ACT.Sqrt, scale=1.0 / P, bias=eps[:, 0:1])\
                .then_inc(sem("hgrn_rms"), 1)
            split_T("mix2oT", n=2)
            split_to(W_OUT2 + 4 + RING)
            pre_norm("xattT", x_added(("mix2_out",)), col("xattn_norm"))

            split_to(W_Q + 4)
            used(W_Q + 3)
            for c in range(2):
                for tb in range(TB):
                    copy_out(("mq", tb, c), mq[:, tb, c * 512:(c + 1) * 512])
            for q in range(4):
                b = filled(act, ("mqT", q))
                act.activation(mqT[:, 2 * q:2 * q + 2, :].rearrange("p a t -> p (a t)"), b[:, :], ACT.Copy)\
                    .then_inc(read_sem(("mqT", q)), 1)
            split_to(W_O + RING)
            for h in range(MEM_HEADS):
                for tb in range(TB):
                    s = TB * h + tb
                    act.wait_ge(sem("neg_max"), 16 + s + 1)
                    if h:
                        filled(act, ("mprobsT", h - 1))
                    act.activation(mprobs[:, tb, :], bank_of(("mscores", h, tb))[:, 0:T], ACT.Exp, scale=MEM_HD ** -0.5,
                                   bias=row_max[:, s:s + 1], accum_out=row_sum[:, s:s + 1])\
                        .then_inc(read_sem(("mscores", h, tb)), 1)
                b = filled(act, ("mprobsT", h))
                if h >= 2:
                    act.wait_ge(sem("matt_step"), h - 1)
                act.activation(mprobsT[:, h % 2, :], b[:, :], ACT.Copy).then_inc(read_sem(("mprobsT", h)), 1)
            split_T("mattT")
            split_to(W_O + 4 + RING)
            pre_norm("ffn2T", x_added(("mem_out",)), col("ffn2_norm"))
            ffn(2)
            norm_stats(x, x_added(("down", 2)))

        @block.vector
        def _(dve):
            chained = [0]

            def chain(ins):
                chained[0] += 1
                ins.then_inc(sem("dve_chain"), 1)
                dve.wait_ge(sem("dve_chain"), chained[0])

            norms = [0]
            junk = [rows[:, 1, :]]

            def norm_stats(src, ready):
                ready(dve)
                n = norms[0]
                norms[0] += 1
                dve.tensor_tensor_reduce(out=junk[0], in0=src[:, 1, :], in1=src[:, 1, :], scale=1.0, scalar=0.0,
                                         op0=ALU.mult, op1=ALU.add, accum_out=ssq[:, 1:2]).then_inc(sem("norm_ss_v"), 1)
                dve.wait_ge(sem("norm_rms"), n + 1)
                dve.reciprocal(rstd[:, :], rms[:, :]).then_inc(sem("norm_rstd"), 1)
                dve.wait_ge(sem("norm_rstd"), n + 1)

            def norm_scale(src, dst):
                dve.tensor_scalar(dst[:, 1, :], src[:, 1, :], rstd[:, 1:2], None, ALU.mult).then_inc(sem("xn_v"), 1)

            hi_seen = [0]
            shifts = [0]

            def split_T(stage, gain=None, shift=None, hi=hT_hi, lo=hT_lo, n=4):
                for q in range(n):
                    name = (stage, q)
                    if shift is not None:
                        a, s = shift
                        b = filled(dve, name)
                        buf = shift_buf(shifts[0])
                        for e in range(2):
                            k = 2 * q + e
                            ins = dve.tensor_scalar(buf[:, e, :], b[:, e * T:(e + 1) * T], a[:, k:k + 1], s[:, k:k + 1],
                                                    ALU.mult, ALU.add)
                        ins.then_inc(sem("full_T"), 1)
                        shifts[0] += 1
                        hi_seen[0] += 1
                        dve.wait_ge(sem("T_hi"), hi_seen[0])
                        dve.tensor_tensor(lo[:, 2 * q:2 * q + 2, :], buf, hi[:, 2 * q:2 * q + 2, :].bitcast(F32), ALU.subtract)\
                            .then_inc(read_sem(name), 1)
                        continue
                    hi_seen[0] += 1
                    dve.wait_ge(sem("T_hi"), hi_seen[0])
                    b = bank_of(name)
                    if gain is None:
                        dve.tensor_tensor(lo[:, 2 * q:2 * q + 2, :], b[:, :].rearrange("p (a t) -> p a t", t=T),
                                          hi[:, 2 * q:2 * q + 2, :].bitcast(F32), ALU.subtract).then_inc(read_sem(name), 1)
                    else:
                        for e in range(2):
                            k = 2 * q + e
                            ins = dve.scalar_tensor_tensor(out=lo[:, k, :], in0=b[:, e * T:(e + 1) * T],
                                                           scalar=gain[:, k:k + 1], in1=hi[:, k, :].bitcast(F32),
                                                           op0=ALU.mult, op1=ALU.subtract)
                        ins.then_inc(read_sem(name), 1)

            ropes = [0]

            def rope(src, cos, sin, dst, n):
                v = src.rearrange("p (h d) -> p h d", d=HD)
                a = rope_a[:, 0:n * HD].rearrange("p (h d) -> p h d", d=HD)
                b = rope_b[:, 0:n * HD].rearrange("p (h d) -> p h d", d=HD)
                dve.tensor_tensor(a, v, over_heads(cos, n, HD), ALU.mult)
                dve.tensor_tensor(b[:, :, 0:HD // 2], v[:, :, HD // 2:HD], over_heads(sin[:, 0:HD // 2], n, HD // 2), ALU.mult)
                chain(dve.tensor_tensor(b[:, :, HD // 2:HD], v[:, :, 0:HD // 2], over_heads(sin[:, HD // 2:HD], n, HD // 2),
                                        ALU.mult))
                if len(dst.shape) == 4:
                    a = a.rearrange("p (k j) d -> p k j d", k=KV_HEADS)
                    b = b.rearrange("p (k j) d -> p k j d", k=KV_HEADS)
                dve.tensor_tensor(dst, a, b, ALU.add).then_inc(sem("rope_done"), 1)
                ropes[0] += 1
                dve.wait_ge(sem("rope_done"), ropes[0])

            heads = lambda ap: ap.rearrange("p (h d) -> p h d", d=HD)

            dve.memset(eps[:, :], EPS).then_inc(sem("eps_set"), 1)
            dve.wait_ge(sem("fixed_loaded"), 16)
            norm_stats(mem_in, lambda e: e.wait_ge(sem("mem_loaded"), 16))
            norm_scale(mem_in, xn)
            dve.wait_ge(sem("cols_loaded"), 16)
            split_T("memT", col("mem_norm"))
            dve.wait_ge(sem("lg_exp"), 2)
            dve.tensor_scalar(lg_rows[:, :], lg_rows[:, :], -1.0, None, ALU.mult).then_inc(sem("lg_neg"), 1)
            dve.tensor_scalar(lg_pairs[:, :], lg_pairs[:, :], -1.0, None, ALU.mult).then_inc(sem("lg_neg"), 1)
            norm_stats(x, lambda e: e.wait_ge(sem("x_loaded"), 16))
            filled(dve, ("memT", 3))
            norm_scale(x, xn)
            norm_stats(ctx_in, lambda e: e.wait_ge(sem("ctx_loaded"), 16))
            norm_scale(ctx_in, rows)
            dve.wait_ge(sem("const1_loaded"), 16)
            half = HD // 2
            for n, base in ((0, 0), (1, HD)):
                g = col("qk_gain", base, base + HD)
                cs, sn = (tables[:, 2 * n + e, :].rearrange("p (b d) -> p b d", d=HD) for e in range(2))
                cos_t = c1("rope_cos").rearrange("p (b d) -> p b d", d=HD)
                sin_t = c1("rope_sin").rearrange("p (b d) -> p b d", d=HD)
                dve.tensor_tensor(cs, cos_t, over_heads(g, TB, HD), ALU.mult)
                dve.tensor_tensor(sn[:, :, 0:half], sin_t[:, :, 0:half], over_heads(g[:, half:HD], TB, half), ALU.mult)
                chain(dve.tensor_tensor(sn[:, :, half:HD], sin_t[:, :, half:HD], over_heads(g[:, 0:half], TB, half), ALU.mult))
            dve.wait_ge(sem("ctx_decay"), 4)
            chain(dve.tensor_scalar(ctx_decay[:], ctx_decay[:], HD ** -0.5, None, ALU.mult))

            dve.wait_ge(mod_used, MOD_A)
            b = bank_of("mod_a")
            chain(dve.tensor_tensor(mod[:, 0:16, :], b[:, 0:32].rearrange("p (j c) -> p j c", c=2),
                                    heads_bc(col("b_mod", 0, 16), 16, 2), ALU.add))
            chain(dve.tensor_scalar(a_mix[:], mod[:, 8:16, :], 1.0, None, ALU.add))
            dve.tensor_tensor(a_mix[:], a_mix[:], heads_bc(col("g_pre_mix"), 8, 2), ALU.mult).then_inc(read_sem("mod_a"), 1)
            read_out(dve, "mod_a")
            split_T("xT", shift=(a_mix[:, :, 0], mod[:, 0:8, 0]))
            split_T("ctxT", shift=(a_mix[:, :, 1], mod[:, 0:8, 1]), hi=hcT_hi, lo=hcT_lo)

            read_out(dve, ("kr", 1))
            for tb in range(TB):
                rope(staged[:, tb, :], c1("rope_cos", tb * HD, (tb + 1) * HD), c1("rope_sin", tb * HD, (tb + 1) * HD),
                     heads(krn[:, tb, :]), HEADS)
            read_out(dve, ("kr", 3))
            for fb in range(2):
                for jb in range(TB):
                    ins = dve.tensor_tensor(heads(k_fb[:, fb, jb, :]), heads(staged[:, 2 + jb, :]),
                                            heads_bc(ctx_decay[:, 2 * fb + jb, :], HEADS, HD), ALU.mult)
            ins.then_inc(sem("kr_done"), 1)
            read_out(dve, ("kava", 3))
            sq = rope_a.rearrange("p (a b) -> p a b", b=P)
            chain(dve.tensor_tensor(sq, kava[:, :, 0:P], kava[:, :, 0:P], ALU.mult))
            dve.reduce_sum(head_ss[:, 0:8], rope_a.rearrange("p (h d) -> p h d", d=HD), AX.X).then_inc(sem("ka_ss"), 1)
            dve.wait_ge(sem("ka_rms"), 1)
            chain(dve.reciprocal(head_rstd[:, 0:8], head_rms[:, 0:8]))
            for tile in range(4):
                ins = dve.tensor_tensor(heads(kava[:, tile, 0:P]), heads(kava[:, tile, 0:P]),
                                        heads_bc(head_rstd[:, 2 * tile:2 * tile + 2], 2, HD), ALU.mult)
            chain(ins)
            for tile in range(2):
                dve.tensor_tensor(heads(ka_all[:, tile, :]), heads(kava[:, 2 + tile, 0:P]),
                                  over_heads(col("qk_gain", HD, 2 * HD), KV_HEADS, HD), ALU.mult)
                rope(kava[:, tile, 0:P], tables[:, 2, tile * HD:(tile + 1) * HD], tables[:, 3, tile * HD:(tile + 1) * HD],
                     heads(ka_all[:, 2 + tile, :]), KV_HEADS)
            read_out(dve, ("qa", 1))
            for tb in range(TB):
                chain(dve.tensor_tensor(rope_a, staged[:, tb, :], staged[:, tb, :], ALU.mult))
                ins = dve.reduce_sum(head_ss[:, tb * 8:tb * 8 + 8], heads(rope_a), AX.X)
                if tb == 0:
                    chain(ins)
            ins.then_inc(sem("qa_ss"), 1)
            dve.wait_ge(sem("qa_rms"), 1)
            chain(dve.reciprocal(head_rstd[:, :], head_rms[:, :]))
            for tb in range(TB):
                ins = dve.tensor_tensor(heads(staged[:, tb, :]), heads(staged[:, tb, :]),
                                        heads_bc(head_rstd[:, tb * 8:tb * 8 + 8], HEADS, HD), ALU.mult)
            chain(ins)
            for tb in range(TB):
                rope(staged[:, tb, :], tables[:, 0, tb * HD:(tb + 1) * HD], tables[:, 1, tb * HD:(tb + 1) * HD],
                     qan[:, tb, :].rearrange("p (j k d) -> p k j d", k=KV_HEADS, d=HD), HEADS)
            read_out(dve, ("qr", 1))
            for tb in range(TB):
                rope(staged[:, 2 + tb, :], c1("rope_cos", tb * HD, (tb + 1) * HD), c1("rope_sin", tb * HD, (tb + 1) * HD),
                     heads(qrn[:, tb, :]), HEADS)

            dve.wait_ge(mod_used, N_MOD)
            b = bank_of("mod_b")
            chain(dve.tensor_tensor(mod[:, 16:48, :], b[:, 0:64].rearrange("p (j c) -> p j c", c=2),
                                    heads_bc(col("b_mod", 16, 48), 32, 2), ALU.add))
            dve.tensor_tensor(gain_col[:, 0, :], mod[:, 16:24, 0], col("g_post_mix"), ALU.mult)
            dve.tensor_tensor(gain_col[:, 1, :], mod[:, 40:48, 0], col("g_post_ffn"), ALU.mult)
            chain(dve.tensor_scalar(a_ffn[:, :], mod[:, 32:40, 0], 1.0, None, ALU.add))
            dve.tensor_tensor(a_ffn[:, :], a_ffn[:, :], col("g_pre_ffn"), ALU.mult).then_inc(read_sem("mod_b"), 1)
            read_out(dve, "mod_b")
            for g in range(2):
                dve.tensor_tensor(xn[:, g, :].rearrange("p (k t) -> p k t", t=P), over_heads(ident, KC, P),
                                  heads_bc(gain_col[:, g, :], KC, P), ALU.mult).then_inc(sem("gain_diag"), 1)

            b = filled(dve, "states")
            dve.tensor_copy(shifted_T[:, 0, :], b[:, :]).then_inc(read_sem("states"), 1)

            def decay_of(r):
                if r:
                    dve.wait_ge(sem("decay_mat"), r)
                chain(dve.tensor_scalar(decay_arg, c1("fwd_dist"), lg_rows[:, r:r + 1], None, ALU.mult))
                dve.scalar_tensor_tensor(out=decay_arg, in0=c1("bwd_dist"), scalar=lg_rows[:, 8 + r:9 + r], in1=decay_arg,
                                         op0=ALU.mult, op1=ALU.add).then_inc(sem("decay_arg"), 1)

            def negative_max(s, name, n, scale):
                b = filled(dve, name)
                chain(dve.reduce_max(row_max[:, s:s + 1], b[:, 0:n], AX.X))
                dve.tensor_scalar(row_max[:, s:s + 1], row_max[:, s:s + 1], -scale, None, ALU.mult).then_inc(sem("neg_max"), 1)

            decay_of(0)
            for s in range(2 * HEADS):
                r = s // 2
                negative_max(s, ("scores", s), 512, HD ** -0.5)
                if s % 2 == 0:
                    dve.wait_ge(sem("decay_mat"), r + 1)
                    chain(dve.tensor_tensor(decay_mat[:, P:2 * P], decay_mat[:, P:2 * P], ident, ALU.add))
                    b = filled(dve, ("ret_scores", r))
                    if r >= 2:
                        dve.wait_ge(sem("ret_step"), r - 1)
                    for jb in range(TB):
                        ins = dve.scalar_tensor_tensor(out=ret_p[:, r % 2, jb * T:(jb + 1) * T], in0=b[:, jb * T:(jb + 1) * T],
                                                       scalar=HD ** -0.5, in1=decay_mat[:, (1 - jb) * P:(3 - jb) * P],
                                                       op0=ALU.mult, op1=ALU.mult)
                    ins.then_inc(read_sem(("ret_scores", r)), 1)
                    if r % 2 == 0:
                        dve.wait_ge(sem("q_dec"), r // 2 + 1)
                        read_out(dve, ("qrT", 1))
                        if r:
                            dve.wait_ge(sem("ret_step"), r)
                        for fb in range(2):
                            dve.tensor_tensor(q_decayed[:, fb, :], qrT[:, r // 2, :], q_dec[:, fb, :], ALU.mult)\
                                .then_inc(sem("q_decayed"), 1)
                    if r < HEADS - 1:
                        decay_of(r + 1)
            read_out(dve, ("scores", 15))
            read_out(dve, ("scores", 14))
            chain(dve.reciprocal(row_inv[:, :], row_sum[:, :]))
            inv = row_inv[:, :].rearrange("p (h b) -> p h b", b=TB)
            dve.wait_ge(sem("att_step"), 2 * HEADS)
            for tb in range(TB):
                b = bank_of(("att", tb))
                dve.tensor_tensor(heads(xn[:, tb, 0:512]), heads(b[:, :]), heads_bc(inv[:, :, tb], HEADS, HD), ALU.mult)\
                    .then_inc(read_sem(("att", tb)), 1)
            dve.wait_ge(sem("ret_step"), HEADS)
            for tb in range(TB):
                b = bank_of(("ret", tb))
                chain(dve.reduce_sum(row_max[:, tb * 8:tb * 8 + 8], heads(b[:, :]), AX.X))
                chain(dve.tensor_scalar(row_max[:, tb * 8:tb * 8 + 8], row_max[:, tb * 8:tb * 8 + 8], -1.0 / HD, None, ALU.mult))
                ins = dve.tensor_tensor(heads(xn[:, tb, 512:1024]), heads(b[:, :]),
                                        heads_bc(row_max[:, tb * 8:tb * 8 + 8], HEADS, HD), ALU.add)
                ins.then_inc(sem("ret_centred"), 1)
            for tb in range(TB):
                dve.wait_ge(sem("ret_sq"), tb + 1)
                ins = dve.reduce_sum(head_ss[:, tb * 8:tb * 8 + 8], heads(probs[:, tb, :]), AX.X)
            ins.then_inc(sem("ret_var"), 1)
            dve.wait_ge(sem("ret_rms"), 1)
            chain(dve.reciprocal(head_rstd[:, :], head_rms[:, :]))
            for tb in range(TB):
                v = xn[:, tb, 512:1024]
                chain(dve.tensor_tensor(heads(v), heads(v), heads_bc(head_rstd[:, tb * 8:tb * 8 + 8], HEADS, HD), ALU.mult))
                dve.tensor_tensor(v, v, silu_gr[:, tb, :], ALU.mult).then_inc(read_sem(("ret", tb)), 1)
            split_T("mixT")

            def post_norm(y, name, last, g):
                dve.wait_ge(split_used, last + 1)
                for c in range(2):
                    dve.tensor_copy(y[:, 1, c * 512:(c + 1) * 512], bank_of((*name, 1, c))[:, :])\
                        .then_inc(read_sem((*name, 1, c)), 1)
                read_out(dve, (*name, 1, 0))
                read_out(dve, (*name, 1, 1))
                norm_stats(y, lambda e: None)
                for tb in range(TB):
                    ins = dve.scalar_tensor_tensor(out=y[:, tb, :], in0=y[:, tb, :], scalar=rstd[:, tb:tb + 1],
                                                   in1=rows[:, g, :], op0=ALU.mult, op1=ALU.mult)
                chain(ins)
                for tb in range(TB):
                    ins = dve.tensor_tensor(x[:, tb, :], x[:, tb, :], y[:, tb, :], ALU.add)
                ins.then_inc(sem("x_ready"), 1)

            junk[0] = xn[:, 1, :]

            def pre_norm(stage, ready, gain=None, shift=None):
                norm_stats(x, ready)
                norm_scale(x, xn)
                split_T(stage, gain, shift)

            def add_to_x(name, last, scale=None):
                dve.wait_ge(split_used, last + 1)
                for c in range(2):
                    for tb in range(TB):
                        key = (*name, tb, c)
                        xs = x[:, tb, c * 512:(c + 1) * 512]
                        dve.scalar_tensor_tensor(out=xs, in0=bank_of(key)[:, :], scalar=1.0 if scale is None else scale,
                                                 in1=xs, op0=ALU.mult, op1=ALU.add).then_inc(read_sem(key), 1)

            def ffn(f):
                silu0 = 2 * UP * f

                def gated(c, silus):
                    for tb in range(TB):
                        dve.wait_ge(sem("gate_silu"), silus + tb + 1)
                        b = (c % 3) * 2 + tb
                        dve.tensor_tensor(gate[:, c % 3, tb, :], gate[:, c % 3, tb, :], bank[b][:, 256:512], ALU.mult)\
                            .then_inc(bank_read[b], 1)

                def gate_lo(his, at):
                    dve.wait_ge(sem("gateT_hi"), his)
                    s = at if isinstance(at, slice) else bass.ds(at, 2)
                    dve.tensor_tensor(gT_lo[:, s, :], bank[6][:, :].rearrange("p (a t) -> p a t", t=T),
                                      gT_hi[:, s, :].bitcast(F32), ALU.subtract).then_inc(bank_read[6], 1)

                gated(0, silu0)
                gated(1, silu0 + 2)
                gate_lo(UP * f + 1, slice(0, 2))
                with dve.Fori(0, 3) as i:
                    for j in range(3):
                        c = 2 + j
                        gated(c, i * 6 + (silu0 + 2 * c))
                        gate_lo(i * 3 + (UP * f + c), i * 6 + 2 * (c - 1))
                gate_lo(UP * (f + 1), slice(2 * UP - 2, 2 * UP))

            post_norm(y_mix, ("mix_out",), W_OUT + 3, 0)
            pre_norm("ffn0T", x_ready(1), shift=(a_ffn, mod[:, 24:32, 0]))
            ffn(0)
            post_norm(y_ffn, ("down", 0), W_DN[0] + UP - 1, 1)
            pre_norm("ffn1T", x_ready(2), col("ffn1_norm"))
            ffn(1)
            add_to_x(("down", 1), W_DN[1] + UP - 1, 0.5)
            pre_norm("mix2T", x_added(("down", 1)), col("mix_norm"))

            dve.wait_ge(sem("lb_loaded"), 16)
            chain(dve.tensor_tensor(lb, lb_p[:, 0, :], lb_p[:, 1, :], ALU.max))
            dve.tensor_tensor(lb_p[:], lb_p[:], over_heads(lb, 2, 512), ALU.subtract).then_inc(sem("lb_diff"), 1)
            dve.wait_ge(sem("lb_exp"), 1)
            chain(dve.tensor_tensor(lb, lb_p[:, 0, :], lb_p[:, 1, :], ALU.add))
            chain(dve.reciprocal(lb, lb))
            chain(dve.tensor_tensor(lb, lb, lb_p[:, 0, :], ALU.mult))
            chain(dve.tensor_scalar(one_lb, lb, -1.0, 1.0, ALU.mult, ALU.add))
            chain(dve.memset(scT, 0.0))
            read_out(dve, ("zf", 1))
            chain(dve.tensor_tensor(fgate[:], fgate[:], over_heads(one_lb, TB, 512), ALU.mult))
            chain(dve.tensor_tensor(fgate[:], fgate[:], over_heads(lb, TB, 512), ALU.add))
            dve.tensor_scalar(hk[:], fgate[:], -1.0, 1.0, ALU.mult, ALU.add).then_inc(sem("fgate"), 1)
            dve.wait_ge(sem("logf_hi"), 1)
            dve.tensor_tensor(logf_lo[:], fgate[:], logf_hi[:].bitcast(F32), ALU.subtract).then_inc(sem("logf_lo"), 1)

            mask = lambda n: over_heads(level_mask[:, n, :], 4, P).bitcast(I32)
            sc = lambda blk: scT[:, blk * 512:(blk + 1) * 512].rearrange("p (h t) -> p h t", t=P)

            def keep_pairs(level, name):
                for blk in range(TB):
                    b = filled(dve, (*name, blk))
                    dve.copy_predicated(sc(blk), mask(level + 1), b[:, :].rearrange("p (h t) -> p h t", t=P))\
                        .then_inc(read_sem((*name, blk)), 1)

            def decayed(level):
                buf = qk_dec[level % 2]
                for late, other in ((1, hqT), (0, hkT)):
                    h = 1 << level
                    v = buf.rearrange("p (n two h) -> p n two h", two=2, h=h)[:, :, late, :] if level < LEVELS else \
                        buf[:, late * 512:late * 512 + 512]
                    o = other.rearrange("p (n two h) -> p n two h", two=2, h=h)[:, :, late, :] if level < LEVELS else \
                        other[:, late * 512:late * 512 + 512]
                    ins = dve.tensor_tensor(v, v, o, ALU.mult)
                ins.then_inc(sem("level_decayed"), 1)

            dve.wait_ge(sem("const2_loaded"), 16)
            read_out(dve, ("hkT", 0))
            read_out(dve, ("hkT", 1))
            keep_pairs(-1, ("diag",))
            for level in range(LEVELS + 1):
                read_out(dve, ("decay", level, 0))
                read_out(dve, ("decay", level, 1))
                decayed(level)
                if level:
                    keep_pairs(level - 1, ("pairs", level - 1))
                if level == 4:
                    dve.wait_ge(split_used, W_IN2 + 10)
                    read_out(dve, ("zc", 1))
                    for tb in range(TB):
                        dve.tensor_tensor(zc_sb[:, tb, :], zc_sb[:, tb, :], bank_of(("zu", tb))[:, :], ALU.mult)\
                            .then_inc(read_sem(("zu", tb)), 1)
            b = filled(dve, "cross")
            dve.tensor_copy(crossT, b[:, :]).then_inc(read_sem("cross"), 1)
            u3 = uT.rearrange("p (c t) -> p c t", t=T + 2)
            dve.memset(u3[:, :, 0:2], 0.0).then_inc(sem("u_pad"), 1)
            read_out(dve, "uT0")
            read_out(dve, "uT1")
            dve.wait_ge(sem("u_pad"), 1)
            taps = lambda c, j: col("conv_w", 3 * c + j, 3 * c + j + 1)
            for c in range(4):
                ins = dve.tensor_scalar(conv[:, c, :], u3[:, c, 2:T + 2], taps(c, 2), None, ALU.mult)
            chain(ins)
            for j in (1, 0):
                for c in range(4):
                    ins = dve.scalar_tensor_tensor(out=conv[:, c, :], in0=u3[:, c, j:T + j], scalar=taps(c, j),
                                                   in1=conv[:, c, :], op0=ALU.mult, op1=ALU.add)
                chain(ins)
            for j in range(2):
                b = filled(dve, f"bT{j}")
                dve.tensor_tensor(conv[:, 2 * j:2 * j + 2, :], conv[:, 2 * j:2 * j + 2, :],
                                  b[:, :].rearrange("p (c t) -> p c t", t=T), ALU.mult).then_inc(read_sem(f"bT{j}"), 1)
            for j in range(2):
                dve.wait_ge(sem("conv_hi"), j + 1)
                dve.tensor_tensor(hT_lo[:, 4 + 2 * j:6 + 2 * j, :], conv[:, 2 * j:2 * j + 2, :],
                                  hT_hi[:, 4 + 2 * j:6 + 2 * j, :].bitcast(F32), ALU.subtract).then_inc(sem("conv_lo"), 1)
            read_out(dve, ("zg", 1))
            dve.wait_ge(sem("head_row_loaded"), 16)
            chain(dve.tensor_tensor(silu_zg[:], silu_zg[:], over_heads(head_row, TB, 512), ALU.mult))
            for blk in range(TB):
                dve.wait_ge(sem("hgrn_sq"), blk + 1)
                dve.reduce_sum(head_ss[:, 4 * blk:4 * blk + 4], hgrn_sq.rearrange("p (h d) -> p h d", d=P), AX.X)\
                    .then_inc(sem("hgrn_ss"), 1)
            dve.wait_ge(sem("hgrn_rms"), 1)
            chain(dve.reciprocal(head_rstd[:, 0:8], head_rms[:, 0:8]))
            for blk in range(TB):
                b = bank_of(("hgrn", blk))
                v = xn[:, blk, 0:512]
                dve.tensor_tensor(v.rearrange("p (h d) -> p h d", d=P), b[:, :].rearrange("p (h d) -> p h d", d=P),
                                  heads_bc(head_rstd[:, 4 * blk:4 * blk + 4], 4, P), ALU.mult)\
                    .then_inc(read_sem(("hgrn", blk)), 1)
                read_out(dve, ("hgrn", blk))
                dve.tensor_tensor(v, v, silu_zg[:, blk, :], ALU.mult).then_inc(sem("hgrn_out"), 1)
            split_T("mix2oT", n=2)
            add_to_x(("mix2_out",), W_OUT2 + 3)
            pre_norm("xattT", x_added(("mix2_out",)), col("xattn_norm"))

            for h in range(MEM_HEADS):
                for tb in range(TB):
                    negative_max(TB * h + tb, ("mscores", h, tb), T, MEM_HD ** -0.5)
            for tb in range(TB):
                read_out(dve, ("mscores", MEM_HEADS - 1, tb))
            chain(dve.reciprocal(row_inv[:, 0:8], row_sum[:, 0:8]))
            inv = row_inv[:, 0:8].rearrange("p (h b) -> p h b", b=TB)
            for h2 in range(2):
                dve.wait_ge(sem("matt_step"), 2 * h2 + 2)
                for tb in range(TB):
                    b = bank_of(("matt", h2, tb))
                    dve.tensor_tensor(xn[:, tb, h2 * 512:(h2 + 1) * 512].rearrange("p (h d) -> p h d", d=MEM_HD),
                                      b[:, :].rearrange("p (h d) -> p h d", d=MEM_HD),
                                      heads_bc(inv[:, 2 * h2:2 * h2 + 2, tb], 2, MEM_HD), ALU.mult)\
                        .then_inc(read_sem(("matt", h2, tb)), 1)
            split_T("mattT")
            add_to_x(("mem_out",), W_O + 3)
            pre_norm("ffn2T", x_added(("mem_out",)), col("ffn2_norm"))
            ffn(2)
            add_to_x(("down", 2), W_DN[2] + UP - 1, 0.5)

            norm_stats(x, x_added(("down", 2)))
            dve.wait_ge(sem("final_loaded"), 16)
            for tb in range(TB):
                dve.scalar_tensor_tensor(out=xn[:, tb, :], in0=x[:, tb, :], scalar=rstd[:, tb:tb + 1], in1=rows[:, 0, :],
                                         op0=ALU.mult, op1=ALU.mult).then_inc(sem("out_ready"), 1)

        @block.tensor
        def _(pe):
            def three(out, hi, lo, rhi, rlo, start, stop):
                pe.matmul(out, hi, rhi, start=start, stop=False)
                pe.matmul(out, hi, rlo, start=False, stop=False)
                return pe.matmul(out, lo, rhi, start=False, stop=stop)

            def unit(v, ready, tiles, ks, n, first, last, slot=None):
                pe.wait_ge(split_ready, ready)
                s = v % RING
                for hi, lo, tb, out in tiles:
                    for e, k in enumerate(ks):
                        t = slice(tb * P, (tb + 1) * P)
                        w = slice(e * n, (e + 1) * n)
                        ins = three(out[:, 0:n], hi[:, k, t], lo[:, k, t], w_hi[:, s, w], w_lo[:, s, w],
                                    first and e == 0, last and e == len(ks) - 1)
                ins.then_inc(split_used, 1)

            def project(v, names, tiles=None, halves=(0, 1), ready=None):
                tiles = tiles or [(hT_hi, hT_lo, 0), (hT_hi, hT_lo, 1)]
                for n, half in enumerate(halves):
                    if ready:
                        ready(half)
                    if n == 0:
                        outs = [free(pe, name) for name in names]
                    unit(v + n, v + n + 1, [(*t, o) for t, o in zip(tiles, outs)], range(4 * half, 4 * half + 4), 512,
                         n == 0, n == 1)

            def input_ready(stage):
                return lambda half: [read_out(pe, (stage, 2 * half + e)) for e in range(2)]

            scaled = [0]

            def transpose_input(stage, src):
                scaled[0] += 1
                pe.wait_ge(sem("xn_a"), scaled[0])
                pe.wait_ge(sem("xn_v"), scaled[0])
                transposes(stage, src)

            def transposes(stage, src, n=4):
                for q in range(n):
                    b = free(pe, (stage, q))
                    for e in range(2):
                        for tb in range(TB):
                            ins = pe.transpose(b[:, e * T + tb * P:e * T + (tb + 1) * P],
                                               src[:, tb, (2 * q + e) * P:(2 * q + e + 1) * P], ident)
                    ins.then_inc(full_sem((stage, q)), 1)

            def mod_unit(m, col0):
                u = RAW_AT[("mod", m)]
                pe.wait_ge(raw_ready[u % RING], 16 * (u // RING + 1))
                b = bank[7]
                for e in range(2):
                    for k in range(KC):
                        ins = pe.matmul(b[:, col0 + 2 * e:col0 + 2 * e + 2],
                                        raw[:, u % RING, k * T + e * P:k * T + (e + 1) * P], silu_c[:, k, :],
                                        start=(k == 0), stop=(k == KC - 1))
                return ins

            pe.wait_ge(sem("fixed_loaded"), 16)
            transpose_input("memT", xn)
            for c in range(4):
                project(W_KV + 2 * c, [("kv", c, 0), ("kv", c, 1)], ready=input_ready("memT") if c == 0 else None)
            pe.wait_ge(sem("silu_c"), 1)
            for m in range(MOD_A):
                mod_unit(m, 4 * m).then_inc(mod_used, 1)
            read_out(pe, ("kv", 1, 0))
            read_out(pe, ("kv", 1, 1))
            transposes("keyT", mem_k)
            transpose_input("xT", xn)
            transpose_input("ctxT", rows)

            both = [(hT_hi, hT_lo, 0), (hT_hi, hT_lo, 1), (hcT_hi, hcT_lo, 0), (hcT_hi, hcT_lo, 1)]
            mods = [MOD_A]

            def mods_behind(j):
                for _ in range(IN_MODS[j]):
                    m = mods[0]
                    if m == MOD_A:
                        free(pe, "mod_b")
                    mod_unit(m, 4 * (m - MOD_A)).then_inc(mod_used, 1)
                    mods[0] += 1

            j = 0
            for part, units, tiles in [("kr", 2, both), ("vr", 2, both), ("kava", 1, both), ("qa", 2, both[:2]),
                                       ("qr", 2, both[:2]), ("gr", 2, both[:2])]:
                for e in range(units):
                    if j < 2:
                        for stage in ("xT", "ctxT"):
                            for q in range(2):
                                read_out(pe, (stage, 2 * j + q))
                    if e == 0:
                        outs = [free(pe, (part, t)) for t in range(len(tiles))]
                    ks, n = (range(4 * e, 4 * e + 4), 512) if units == 2 else (range(8), 256)
                    unit(W_IN + j, W_IN + j + 1, [(*t, o) for t, o in zip(tiles, outs)], ks, n, e == 0, e == units - 1)
                    mods_behind(j)
                    j += 1
            for q in range(4):
                if q % 2 == 0:
                    pe.wait_ge(sem("gain_diag"), q // 2 + 1)
                b = free(pe, ("gain_row", q))
                pe.matmul(b[:, :], ones, xn[:, q // 2, (q % 2) * 512:(q % 2 + 1) * 512], start=True, stop=True)\
                    .then_inc(full_sem(("gain_row", q)), 1)

            pe.wait_ge(sem("kr_done"), 1)
            read_out(pe, ("vr", 3))
            b = free(pe, "states")
            for fb in range(2):
                for h in range(HEADS):
                    o = b[64 * (h % 2):64 * (h % 2) + 64, fb * 256 + (h // 2) * HD:fb * 256 + (h // 2 + 1) * HD]
                    for jb in range(TB):
                        ins = pe.matmul(o, k_fb[:, fb, jb, h * HD:(h + 1) * HD], vr[:, 2 + jb, h * HD:(h + 1) * HD],
                                        start=(jb == 0), stop=(jb == 1))
            ins.then_inc(full_sem("states"), 1)
            pe.wait_ge(sem("rope_done"), 8)
            transposes("krT", krn, 2)
            b = free(pe, ("kaT", 0))
            for tile in range(4):
                ins = pe.transpose(b[:, tile * P:(tile + 1) * P], ka_all[:, tile, :], ident)
            ins.then_inc(full_sem(("kaT", 0)), 1)
            transposes("qaT", qan, 2)
            transposes("qrT", qrn, 2)
            for name, n in (("krT", 2), ("kaT", 1), ("qaT", 2), ("qrT", 2)):
                for q in range(n):
                    read_out(pe, (name, q))

            def scores(s):
                h, tb = s // 2, s % 2
                j, kv = h % GROUP, h // GROUP
                b = free(pe, ("scores", s))
                pe.matmul(b[:, :], qaT[64 * kv:64 * kv + 64, j, tb * P:(tb + 1) * P], kaT[64 * kv:64 * kv + 64, :],
                          start=True, stop=True).then_inc(full_sem(("scores", s)), 1)

            def weighted(s):
                h, tb = s // 2, s % 2
                kv = h // GROUP
                read_out(pe, ("probsT", s))
                b = free(pe, ("att", tb))
                for kb, tile in enumerate((2, 3, 0, 1)):
                    ins = pe.matmul(b[:, h * HD:(h + 1) * HD], probsT[:, s % 2, kb * P:(kb + 1) * P],
                                    kava[:, tile, P + kv * HD:P + (kv + 1) * HD], start=(kb == 0), stop=(kb == 3))
                ins.then_inc(sem("att_step"), 1)

            def retained(r):
                read_out(pe, ("ret_scores", r))
                pe.wait_ge(sem("q_decayed"), 2 * (r // 2) + 2)
                read_out(pe, "states")
                half = slice(64 * (r % 2), 64 * (r % 2) + 64)
                for ib in range(TB):
                    o = free(pe, ("ret", ib))[:, r * HD:(r + 1) * HD]
                    for jb in range(TB):
                        pe.matmul(o, ret_p[:, r % 2, jb * T + ib * P:jb * T + (ib + 1) * P], vr[:, jb, r * HD:(r + 1) * HD],
                                  start=(jb == 0), stop=False)
                    for fb in range(2):
                        ins = pe.matmul(o, q_decayed[half, fb, ib * P:(ib + 1) * P], state[half, fb, r // 2, :],
                                        start=False, stop=(fb == 1))
                ins.then_inc(sem("ret_step"), 1)

            scores(0)
            for s in range(2 * HEADS):
                if s + 1 < 2 * HEADS:
                    scores(s + 1)
                if s % 2 == 0:
                    r = s // 2
                    b = free(pe, ("ret_scores", r))
                    half = slice(64 * (r % 2), 64 * (r % 2) + 64)
                    for jb in range(TB):
                        ins = pe.matmul(b[:, jb * T:(jb + 1) * T], krT[half, r // 2, jb * P:(jb + 1) * P], qrT[half, r // 2, :],
                                        start=True, stop=True)
                    ins.then_inc(full_sem(("ret_scores", r)), 1)
                if s:
                    weighted(s - 1)
                read_out(pe, ("scores", s))
                b = free(pe, ("probsT", s))
                for kb in range(4):
                    ins = pe.transpose(b[:, kb * P:(kb + 1) * P], probs[:, s % 2, kb * P:(kb + 1) * P], ident)
                ins.then_inc(full_sem(("probsT", s)), 1)
                if s % 2 == 1:
                    retained(s // 2)
            weighted(2 * HEADS - 1)
            read_out(pe, ("att", 0))
            read_out(pe, ("att", 1))
            read_out(pe, ("ret", 0))
            read_out(pe, ("ret", 1))
            transposes("mixT", xn)
            for c in range(2):
                project(W_OUT + 2 * c, [("mix_out", tb, c) for tb in range(TB)], ready=input_ready("mixT") if c == 0 else None)

            def ffn(f, stage):
                up, dn = W_UP[f], W_DN[f]

                def up_chunk(c, ready, frees, inputs=None):
                    for half in range(2):
                        if inputs:
                            inputs(half)
                        if half == 0:
                            for tb in range(TB):
                                pe.wait_ge(bank_read[(c % 3) * 2 + tb], frees[tb])
                        unit(up + 2 * c + half, ready + half + 1,
                             [(hT_hi, hT_lo, tb, bank[(c % 3) * 2 + tb]) for tb in range(TB)],
                             range(4 * half, 4 * half + 4), 512, half == 0, half == 1)

                def gate_T(c, reads, before):
                    for tb in range(TB):
                        pe.wait_ge(bank_read[(c % 3) * 2 + tb], reads[tb])
                    pe.wait_ge(bank_read[6], before)
                    for e in range(2):
                        for tb in range(TB):
                            ins = pe.transpose(bank[6][:, e * T + tb * P:e * T + (tb + 1) * P],
                                               gate[:, c % 3, tb, e * P:(e + 1) * P], ident)
                    ins.then_inc(bank_full[6], 1)

                fills = lambda c: [plan.of[("up", f, c, tb)][1] for tb in range(TB)]
                g0 = plan.of[("gateT", f, 0)][1]
                up_chunk(0, up, fills(0), input_ready(stage))
                up_chunk(1, up + 2, fills(1))
                gate_T(0, [n + 1 for n in fills(0)], g0)
                with pe.Fori(0, 3) as i:
                    for j in range(3):
                        c = 2 + j
                        up_chunk(c, i * 6 + (up + 2 * c), [i + n for n in fills(c)])
                        gate_T(c - 1, [i + (n + 1) for n in fills(c - 1)], i * 3 + (g0 + c - 1))

                def down(k):
                    pe.wait_ge(split_ready, dn + k + 1)
                    pe.wait_ge(bank_read[6], g0 + k + 1)
                    s = (dn + k) % RING
                    for tb in range(TB):
                        t = slice(tb * P, (tb + 1) * P)
                        for e in range(2):
                            for half in range(2):
                                o = free(pe, ("down", f, tb, half)) if k == 0 and e == 0 else bank_of(("down", f, tb, half))
                                w = slice(e * D + half * 512, e * D + half * 512 + 512)
                                ins = three(o[:, :], gT_hi[:, 2 * k + e, t], gT_lo[:, 2 * k + e, t], w_hi[:, s, w], w_lo[:, s, w],
                                            k == 0 and e == 0, k == UP - 1 and e == 1)
                    ins.then_inc(split_used, 1)

                down(0)
                gate_T(UP - 1, [n + 1 for n in fills(UP - 1)], g0 + UP - 1)
                for k in range(1, UP):
                    down(k)

            transpose_input("ffn0T", xn)
            ffn(0, "ffn0T")
            transpose_input("ffn1T", xn)
            ffn(1, "ffn1T")
            transpose_input("mix2T", xn)

            z = lambda k, part: project(W_IN2 + 2 * k, [(part, 0), (part, 1)], ready=input_ready("mix2T") if k == 0 else None)
            z(0, "zf")
            z(1, "zq")
            z(2, "zi")
            read_out(pe, ("zq", 1))
            pe.wait_ge(sem("fgate"), 1)
            for name, src in (("hqT", hq), ("hkT", hk)):
                for blk in range(TB):
                    b = free(pe, (name, blk))
                    for h in range(HG_HEADS):
                        ins = pe.transpose(b[:, h * P:(h + 1) * P], src[:, blk, h * P:(h + 1) * P], ident)
                    ins.then_inc(full_sem((name, blk)), 1)

            def decay_sums(level):
                for blk in range(TB):
                    b = free(pe, ("decay", level, blk))
                    m = sums_r[:, level + blk if level == LEVELS else level, :]
                    for h in range(HG_HEADS):
                        o = b[:, h * P:(h + 1) * P]
                        pe.matmul(o, logf_hi[:, blk, h * P:(h + 1) * P], m, start=True, stop=False)
                        ins = pe.matmul(o, logf_lo[:, blk, h * P:(h + 1) * P], m, start=False, stop=True)
                    ins.then_inc(full_sem(("decay", level, blk)), 1)

            def pair_scores(level):
                pe.wait_ge(sem("level_decayed"), level + 1)
                buf = qk_dec[level % 2]
                if level == LEVELS:
                    b = free(pe, "cross")
                    for h in range(HG_HEADS):
                        ins = pe.matmul(b[:, h * P:(h + 1) * P], buf[:, h * P:(h + 1) * P],
                                        buf[:, 512 + h * P:512 + (h + 1) * P], start=True, stop=True)
                    ins.then_inc(full_sem("cross"), 1)
                    return
                for blk in range(TB):
                    b = free(pe, ("pairs", level, blk))
                    for h in range(HG_HEADS):
                        v = buf[:, blk * 512 + h * P:blk * 512 + (h + 1) * P]
                        ins = pe.matmul(b[:, h * P:(h + 1) * P], v, v, start=True, stop=True)
                    ins.then_inc(full_sem(("pairs", level, blk)), 1)

            pe.wait_ge(sem("sums_ready"), 1)
            pe.wait_ge(sem("logf_lo"), 1)
            decay_sums(0)
            for name in ("hqT", "hkT"):
                for q in range(2):
                    read_out(pe, (name, q))
            for blk in range(TB):
                b = free(pe, ("diag", blk))
                for h in range(HG_HEADS):
                    s = slice(blk * 512 + h * P, blk * 512 + (h + 1) * P)
                    ins = pe.matmul(b[:, h * P:(h + 1) * P], hkT[:, s], hqT[:, s], start=True, stop=True)
                ins.then_inc(full_sem(("diag", blk)), 1)
            parts = ["zc", "zu", "zb", "zg"]
            for step in range(8):
                k, half = step // 2, step % 2
                v = W_IN2 + 6 + step
                if half == 0:
                    outs = [free(pe, (parts[k], tb)) for tb in range(TB)]
                unit(v, v + 1, [(hT_hi, hT_lo, tb, outs[tb]) for tb in range(TB)], range(4 * half, 4 * half + 4), 512,
                     half == 0, half == 1)
                if step < LEVELS:
                    decay_sums(step + 1)
                    pair_scores(step)
            pair_scores(LEVELS)
            read_out(pe, ("zu", 1))
            read_out(pe, ("zb", 1))
            for name, src in (("uT", zc_sb), ("bT", zb_sb)):
                for j in range(2):
                    b = free(pe, f"{name}{j}")
                    for e in range(2):
                        for tb in range(TB):
                            ins = pe.transpose(b[:, e * T + tb * P:e * T + (tb + 1) * P],
                                               src[:, tb, (2 * j + e) * P:(2 * j + e + 1) * P], ident)
                    ins.then_inc(full_sem(f"{name}{j}"), 1)
            read_out(pe, ("pairs", LEVELS - 1, 0))
            read_out(pe, ("pairs", LEVELS - 1, 1))
            read_out(pe, "cross")
            for blk in range(TB):
                b = free(pe, ("hgrn", blk))
                for h in range(HG_HEADS):
                    d = slice(h * P, (h + 1) * P)
                    ins = pe.matmul(b[:, d], scT[:, blk * 512 + h * P:blk * 512 + (h + 1) * P], hv[:, blk, d],
                                    start=True, stop=(blk == 0))
                    if blk:
                        ins = pe.matmul(b[:, d], crossT[:, d], hv[:, 0, d], start=False, stop=True)
                ins.then_inc(full_sem(("hgrn", blk)), 1)
            pe.wait_ge(sem("hgrn_out"), TB)
            transposes("mix2oT", xn, 2)

            def mix2_ready(half):
                if half == 1:
                    pe.wait_ge(sem("conv_lo"), 2)
                else:
                    read_out(pe, ("mix2oT", 0))
                    read_out(pe, ("mix2oT", 1))

            for c in range(2):
                project(W_OUT2 + 2 * c, [("mix2_out", tb, c) for tb in range(TB)], halves=(1, 0), ready=mix2_ready)

            transpose_input("xattT", xn)
            for c in range(2):
                project(W_Q + 2 * c, [("mq", tb, c) for tb in range(TB)], ready=input_ready("xattT") if c == 0 else None)
            for tb in range(TB):
                for c in range(2):
                    read_out(pe, ("mq", tb, c))
            transposes("mqT", mq)
            for q in range(4):
                read_out(pe, ("mqT", q))

            def mem_scores(h):
                for tb in range(TB):
                    b = free(pe, ("mscores", h, tb))
                    for e in range(2):
                        ins = pe.matmul(b[:, 0:T], mqT[:, 2 * h + e, tb * P:(tb + 1) * P], memKT[:, 2 * h + e, :],
                                        start=(e == 0), stop=(e == 1))
                    ins.then_inc(full_sem(("mscores", h, tb)), 1)

            def mem_weighted(h):
                read_out(pe, ("mprobsT", h))
                for tb in range(TB):
                    b = free(pe, ("matt", h // 2, tb))
                    for mb in range(TB):
                        ins = pe.matmul(b[:, (h % 2) * MEM_HD:(h % 2 + 1) * MEM_HD],
                                        mprobsT[:, h % 2, (mb * TB + tb) * P:(mb * TB + tb + 1) * P],
                                        memV[:, mb, h * MEM_HD:(h + 1) * MEM_HD], start=(mb == 0), stop=(mb == 1))
                ins.then_inc(sem("matt_step"), 1)

            mem_scores(0)
            for h in range(MEM_HEADS):
                if h + 1 < MEM_HEADS:
                    mem_scores(h + 1)
                if h:
                    mem_weighted(h - 1)
                for tb in range(TB):
                    read_out(pe, ("mscores", h, tb))
                b = free(pe, ("mprobsT", h))
                for mb in range(TB):
                    for tb in range(TB):
                        ins = pe.transpose(b[:, (mb * TB + tb) * P:(mb * TB + tb + 1) * P], mprobs[:, tb, mb * P:(mb + 1) * P],
                                           ident)
                ins.then_inc(full_sem(("mprobsT", h)), 1)
            mem_weighted(MEM_HEADS - 1)
            for half in range(2):
                for tb in range(TB):
                    read_out(pe, ("matt", half, tb))
            transposes("mattT", xn)
            for c in range(2):
                project(W_O + 2 * c, [("mem_out", tb, c) for tb in range(TB)], ready=input_ready("mattT") if c == 0 else None)
            transpose_input("ffn2T", xn)
            ffn(2, "ffn2T")



def lay_out(a):
    f = lambda name: np.asarray(a[name])
    halves = lambda w: [w[512 * h:512 * h + 512].reshape(4, P, -1).transpose(1, 0, 2).reshape(P, UNIT) for h in range(2)]
    whole = lambda w: w.reshape(KC, P, 256).transpose(1, 0, 2).reshape(P, UNIT)

    def project(w, halves_order=(0, 1)):
        return [halves(w[:, c:c + 512])[h] for c in range(0, w.shape[1], 512) for h in halves_order]

    def swiglu(gate, up, down):
        out = []
        for c in range(0, FFN, 256):
            out += halves(np.concatenate([gate[:, c:c + 256], up[:, c:c + 256]], axis=1))
        return out + [down[r:r + 256].reshape(2, P, D).transpose(1, 0, 2).reshape(P, UNIT) for r in range(0, FFN, 256)]

    w_in, w_in2 = f("w_in")[0], f("w_in_2")[0]
    cut = lambda w, at: w[:, at:at + 512]
    kr, vr, qa, qr, gr = (cut(w_in, at) for at in (1280, 1792, 0, 768, 2304))
    w = project(f("w_kv_mem_2")[0])
    w += project(kr) + project(vr) + [whole(w_in[:, 512:768])] + project(qa) + project(qr) + project(gr)
    w += project(f("w_out")[0])
    w += swiglu(f("w_ffn_in")[0][:, :FFN], f("w_ffn_in")[0][:, FFN:], f("w_ffn_out")[0])
    w += swiglu(f("ffn1_gate_2")[0], f("ffn1_up_2")[0], f("ffn1_down_2")[0])
    for at in (512, 0, 1024, 2560, 3072, 2048, 1536):
        w += project(cut(w_in2, at))
    w += project(f("w_out_2")[0], (1, 0)) + project(f("w_q_mem_2")[0]) + project(f("w_o_mem_2")[0])
    w += swiglu(f("ffn2_gate_2")[0], f("ffn2_up_2")[0], f("ffn2_down_2")[0])
    mods = [whole(f("w_mod")[0][:, 256 * m:256 * m + 256]) for m in range(N_MOD)]
    units = {"w": w, "mod": mods}

    col = lambda v: v.reshape(-1, P).T
    everywhere = lambda v: np.broadcast_to(v.reshape(1, -1), (P, v.size))
    decay = np.stack([f("ret_decay_fwd")[0], f("ret_decay_bwd")[0]])
    pairs = np.concatenate([np.repeat(decay[:, e::2].reshape(1, -1), HD, axis=0) for e in range(2)], axis=0)
    small = {name: col(f(src)) for name, src in [
        ("g_pre_mix", "g_pre_mix"), ("g_post_mix", "g_post_mix"), ("g_pre_ffn", "g_pre_ffn"),
        ("g_post_ffn", "g_post_ffn"), ("b_mod", "b_mod"), ("ffn1_norm", "ffn1_norm_2"), ("mix_norm", "mix_norm_2"),
        ("xattn_norm", "xattn_norm_2"), ("mem_norm", "mem_norm_2"), ("ffn2_norm", "ffn2_norm_2")]}
    small["conv_w"] = f("conv_w_2")[0].reshape(4, P, 3).transpose(1, 0, 2).reshape(P, 12)
    small["cond"] = np.stack([f("c")[0], f("c_ctx")], axis=1).reshape(KC, P, 2).transpose(1, 0, 2).reshape(P, 16)
    small["decay_rows"] = everywhere(decay)
    small["decay_pairs"] = pairs
    small["qk_gain"] = everywhere(np.concatenate([f("q_norm_g")[0], f("k_norm_g")[0]]))
    tiles = lambda v: v[0].reshape(TB, P, D).transpose(1, 0, 2)
    fixed, const1, const2 = shape_constants()
    out = {
        "weights": np.stack([units[kind][n] for kind, n in STREAM]),
        "cols": np.concatenate([small[name] for name in COLS], axis=1),
        "x": tiles(f("x")), "ctx": tiles(f("ctx")), "mem": tiles(f("mem_2")),
        "fixed": fixed, "const1": const1, "const2": const2,
        "lb_param": f("lb_param_2").reshape(1, D), "hgrn_out_norm": f("hgrn_out_norm_2").reshape(1, 512),
        "final_norm": f("final_norm_2").reshape(1, D),
    }
    return {name: np.ascontiguousarray(v) for name, v in out.items()}


def kernel(**inputs):
    import concourse.bacc as _bacc
    from concourse.bass_utils import run_bass_kernel_spmd as _run

    nc = _bacc.Bacc("TRN2", target_bir_lowering=False, num_devices=1)
    arrays = {f"in_{name}": v for name, v in lay_out(inputs).items()}
    io = {name[3:]: nc.dram_tensor(name, v.shape, mybir.dt.from_np(v.dtype), kind="ExternalInput").ap()
          for name, v in arrays.items()}
    out = nc.dram_tensor("out", (T, D), F32, kind="ExternalOutput").ap()
    io["out"] = out.rearrange("(b p) d -> b p d", p=P)
    two_blocks_kernel(nc, io)
    r = _run(nc, [arrays], core_ids=[0])
    return r.results[0]["out"].reshape(1, T, D)
```

```python
from contextlib import ExitStack

import numpy as np

import concourse.bass as bass
from concourse import mybir

F32 = mybir.dt.float32
F32R = mybir.dt.float32r
I32 = mybir.dt.int32
ALU = mybir.AluOpType
ACT = mybir.ActivationFunctionType
AX = mybir.AxisListType

P = 128
T = 256
TB = T // P
D = 1024
KC = D // P
HD = 64
HEADS = 8
KV_HEADS = 2
GROUP = HEADS // KV_HEADS
PAIRS = HEADS // 2
FFN = 2816
UP = FFN // 256
HG_HEADS = 4
MEM_HEADS = 4
MEM_HD = D // MEM_HEADS
EPS = 1e-6
UNIT = 2048
RING = 3
LEVELS = 7

W_KV = 0
W_IN = W_KV + 8
W_OUT = W_IN + 11
W_UP = [W_OUT + 4, 0, 0]
W_DN = [W_UP[0] + 2 * UP, 0, 0]
W_UP[1] = W_DN[0] + UP
W_DN[1] = W_UP[1] + 2 * UP
W_IN2 = W_DN[1] + UP
W_OUT2 = W_IN2 + 14
W_Q = W_OUT2 + 4
W_O = W_Q + 4
W_UP[2] = W_O + 4
W_DN[2] = W_UP[2] + 2 * UP
N_W = W_DN[2] + UP
N_MOD = 24
MOD_A = 8

STREAM = [("w", W_KV)]
for _v in range(W_KV + 1, W_IN):
    STREAM += [("w", _v), ("mod", _v - W_KV - 1)]
STREAM.append(("mod", MOD_A - 1))
IN_MODS = [0, 2, 2, 2, 2, 2, 1, 1, 0, 0, 0]
_m = MOD_A
for _j in range(11):
    STREAM.append(("w", W_IN + _j))
    for _ in range(IN_MODS[_j]):
        STREAM.append(("mod", _m))
        _m += 1
STREAM += [("mod", m) for m in range(_m, N_MOD)]
STREAM += [("w", v) for v in range(W_OUT, N_W)]
MODS_IN = (MOD_A + sum(IN_MODS)) // 2
MOD_STEPS = {MODS_IN + n: 2 + 2 * n for n in range(N_MOD // 2 - MODS_IN)}
HEAD_UNITS = W_OUT + N_MOD
RAW_AT = {unit: u for u, unit in enumerate(STREAM)}

COLS = {}
_at = 0
for _name, _n in [("g_pre_mix", 8), ("g_post_mix", 8), ("g_pre_ffn", 8), ("g_post_ffn", 8), ("b_mod", 48),
                  ("ffn1_norm", 8), ("mix_norm", 8), ("xattn_norm", 8), ("mem_norm", 8), ("ffn2_norm", 8),
                  ("conv_w", 12), ("cond", 16), ("decay_rows", 16), ("decay_pairs", 8), ("qk_gain", 128)]:
    COLS[_name] = (_at, _at + _n)
    _at += _n
N_COLS = _at

CONST1 = {}
_at = 0
for _name, _n in [("fwd_dist", 384), ("bwd_dist", 384), ("from_start", T), ("to_end", T), ("ctx_dist", 4),
                  ("rope_cos", TB * HD), ("rope_sin", TB * HD)]:
    CONST1[_name] = (_at, _at + _n)
    _at += _n
N_CONST1 = _at


def shape_constants():
    i = np.arange(P, dtype=np.float32)
    ident = np.eye(P, dtype=np.float32)
    fixed = np.concatenate([ident, np.ones((P, P), np.float32)], axis=1)

    diff = i[None, :] - i[:, None]
    zero = np.zeros((P, P), np.float32)
    fwd = np.concatenate([zero, np.maximum(diff, 0), P + diff], axis=1)
    bwd = np.concatenate([P - diff, np.maximum(-diff, 0), zero], axis=1)
    t = np.arange(T, dtype=np.float32)
    rows = lambda a: np.broadcast_to(a, (P, a.shape[-1]))
    ctx_dist = np.stack([T - 1 - i, T - 1 - (i + P), i, i + P], axis=1)
    inv = (10000.0 ** (-np.arange(HD // 4, dtype=np.float32) / (HD // 4))).astype(np.float32)
    row, col = np.floor(t / 64), t % 64
    ang = np.concatenate([row[:, None] * inv, col[:, None] * inv], axis=1).astype(np.float32)
    cos, sin = np.cos(ang), np.sin(ang)
    tiles = lambda a: a.reshape(TB, P, HD).transpose(1, 0, 2).reshape(P, TB * HD)
    first = np.concatenate([fwd, bwd, rows(t + 1), rows(T - t), ctx_dist,
                            tiles(np.concatenate([cos, cos], 1)), tiles(np.concatenate([-sin, sin], 1))], axis=1)

    sums, masks = [], [ident]
    src, dst = np.arange(P)[:, None], np.arange(P)[None, :]
    for level in range(LEVELS):
        h = 1 << level
        seg_s, seg_t = src // (2 * h), dst // (2 * h)
        late_s, late_t = (src // h) % 2 == 1, (dst // h) % 2 == 1
        same = seg_s == seg_t
        sums.append(same & ((late_t & late_s & (src <= dst)) | (~late_t & ~late_s & (src > dst))))
        masks.append(same & ~late_s & late_t)
    sums += [src > dst, src <= dst]
    second = np.concatenate([m.astype(np.float32) for m in sums + masks], axis=1)
    return [np.ascontiguousarray(a, dtype=np.float32) for a in (fixed, first, second)]


class BankPlan:

    def __init__(self):
        self.fills = [0] * 8
        self.signals = [0] * 8
        self.of = {}

    def streamed(self, name, bank):
        self.of[name] = (bank, self.fills[bank], None)
        self.fills[bank] += 1

    def signalled(self, name, bank):
        self.of[name] = (bank, self.fills[bank], self.signals[bank])
        self.fills[bank] += 1
        self.signals[bank] += 1


FIRST_T = [(stage, 2 * half + e) for half in range(2) for stage in ("xT", "ctxT") for e in range(2)]


def plan_banks():
    plan = BankPlan()

    def transposes(stage, n):
        for q in range(n):
            plan.signalled((stage, q), 5 + q % 2)

    def ffn(f):
        for c in range(UP):
            for tb in range(TB):
                plan.streamed(("up", f, c, tb), (c % 3) * 2 + tb)
        for c in range(UP):
            plan.signalled(("gateT", f, c), 6)
        for tb in range(TB):
            for half in range(2):
                plan.streamed(("down", f, tb, half), tb * 2 + half)

    transposes("memT", 4)
    for c in range(4):
        for tb in range(TB):
            plan.streamed(("kv", c, tb), (c % 2) * 2 + tb)
    plan.streamed("mod_a", 7)
    transposes("keyT", 4)
    for n, name in enumerate(FIRST_T):
        plan.signalled(name, 4 + n % 4)
    for part, banks in [("kr", [0, 1, 2, 3]), ("vr", [4, 5, 6, 0]), ("kava", [1, 2, 3, 4]),
                        ("qa", [5, 6]), ("qr", [0, 1]), ("gr", [2, 3])]:
        for tile, bank in enumerate(banks):
            plan.streamed((part, tile), bank)
    plan.streamed("mod_b", 7)
    plan.signalled("states", 4)
    transposes("krT", 2)
    transposes("kaT", 1)
    transposes("qaT", 2)
    transposes("qrT", 2)
    for s in range(2 * HEADS):
        plan.signalled(("scores", s), s % 2)
        if s % 2 == 0:
            plan.signalled(("ret_scores", s // 2), 3)
        plan.signalled(("probsT", s), 2)
        for c, step in MOD_STEPS.items():
            if step == s:
                plan.signalled(("mod_col", c), 3)
    plan.streamed(("att", 0), 4)
    plan.streamed(("att", 1), 5)
    plan.streamed(("ret", 0), 6)
    plan.streamed(("ret", 1), 7)
    for c in range(2):
        for tb in range(TB):
            plan.streamed(("mix_out", tb, c), tb * 2 + c)
    for q in range(4):
        plan.signalled(("gain_row", q), 4 + q % 2)
    for q in range(2):
        plan.signalled(("mixT", q), 6 + q)
    transposes("ffn0T", 4)
    ffn(0)
    transposes("ffn1T", 4)
    ffn(1)
    transposes("mix2T", 4)
    for part, banks in [("zf", [0, 1]), ("zq", [2, 3]), ("zi", [0, 1]), ("zc", [2, 3]), ("zu", [0, 1]),
                        ("zb", [2, 3]), ("zg", [0, 1])]:
        for tb, bank in enumerate(banks):
            plan.streamed((part, tb), bank)
    transposes("hqT", 2)
    transposes("hkT", 2)
    for blk in range(TB):
        plan.signalled(("diag", blk), 5 + blk)
    for level in range(LEVELS):
        for blk in range(TB):
            plan.signalled(("decay", level, blk), [4, 7][blk])
            plan.signalled(("pairs", level, blk), 5 + blk)
    for blk in range(TB):
        plan.signalled(("decay", LEVELS, blk), [4, 7][blk])
    plan.signalled("cross", 5)
    plan.signalled("uT0", 6)
    plan.signalled("uT1", 5)
    plan.signalled("bT0", 6)
    plan.signalled("bT1", 5)
    for blk in range(TB):
        plan.signalled(("hgrn", blk), [4, 7][blk])
    plan.signalled(("mix2oT", 0), 6)
    plan.signalled(("mix2oT", 1), 5)
    for c in range(2):
        for tb in range(TB):
            plan.streamed(("mix2_out", tb, c), tb * 2 + c)
    transposes("xattT", 4)
    for c in range(2):
        for tb in range(TB):
            plan.streamed(("mq", tb, c), tb * 2 + c)
    transposes("mqT", 4)
    for h in range(MEM_HEADS):
        for tb in range(TB):
            plan.signalled(("mscores", h, tb), [4, 7][tb])
        plan.signalled(("mprobsT", h), 5 + h % 2)
    for half in range(2):
        for tb in range(TB):
            plan.streamed(("matt", half, tb), tb * 2 + half)
    transposes("mattT", 4)
    for c in range(2):
        for tb in range(TB):
            plan.streamed(("mem_out", tb, c), tb * 2 + c)
    transposes("ffn2T", 4)
    ffn(2)
    return plan


def two_blocks_kernel(nc, io):
    plan = plan_banks()
    sems = ExitStack()
    stack = ExitStack()
    named = {}

    def sem(name):
        if name not in named:
            named[name] = sems.enter_context(nc.semaphore(name))
        return named[name]

    with sems, stack:
        def sb(name, shape, dt=F32):
            return stack.enter_context(nc.sbuf_tensor(name, shape, dt))

        raw = sb("raw", [P, RING, UNIT])
        w_hi = sb("w_hi", [P, RING, UNIT], F32R)
        w_lo = sb("w_lo", [P, RING, UNIT], F32R)
        x = sb("x_res", [P, TB, D])
        hT_hi = sb("hT_hi", [P, KC, T], F32R)
        hT_lo = sb("hT_lo", [P, KC, T], F32R)
        xn = sb("xn", [P, TB, D])
        rows = sb("rows", [P, TB, D])
        memKT = sb("memKT", [P, KC, T])
        memV = sb("memV", [P, TB, D])
        fixed = sb("fixed", [P, 2 * P])
        cols = sb("cols", [P, N_COLS])
        eps = sb("eps", [P, 1])
        ssq = sb("ssq", [P, 2])
        rms = sb("rms", [P, 2])
        rstd = sb("rstd", [P, 2])
        silu_c = sb("silu_c", [P, KC, 2])
        mod = sb("mod", [P, 48, 2])
        a_mix = sb("a_mix", [P, KC, 2])
        a_ffn = sb("a_ffn", [P, KC])
        gain_col = sb("gain_col", [P, 2, KC])
        shifted_T = sb("shifted_T", [P, 2, 2 * T])
        ident = fixed[:, 0:P]
        ones = fixed[:, P:2 * P]

        def col(name, a=0, b=None):
            lo, hi = COLS[name]
            return cols[:, lo + a:(lo + b if b is not None else hi)]

        ARENA = 18440
        spot = ExitStack()
        hcT_hi = spot.enter_context(nc.sbuf_tensor("hcT_hi", [P, KC, T], F32R))
        hcT_lo = spot.enter_context(nc.sbuf_tensor("hcT_lo", [P, KC, T], F32R))
        spot.close()
        gT_hi = spot.enter_context(nc.sbuf_tensor("gT_hi", [P, 2 * UP, T], F32R))
        gT_lo = spot.enter_context(nc.sbuf_tensor("gT_lo", [P, 2 * UP, T], F32R))
        spot.close()
        logf_hi = spot.enter_context(nc.sbuf_tensor("logf_hi", [P, TB, 512], F32R))
        logf_lo = spot.enter_context(nc.sbuf_tensor("logf_lo", [P, TB, 512], F32R))
        sums_r = spot.enter_context(nc.sbuf_tensor("sums_r", [P, LEVELS + 2, P], F32R))
        spot.close()
        arena = sb("arena", [P, ARENA])

        def carve(start, *shape):
            n = int(np.prod(shape))
            assert start + n <= ARENA, (start, n)
            v = arena[:, start:start + n]
            if len(shape) == 2:
                return v.rearrange("p (a b) -> p a b", b=shape[1])
            if len(shape) == 3:
                return v.rearrange("p (a b c) -> p a b c", b=shape[1], c=shape[2])
            return v

        at = 4096
        qaT, kaT = carve(0, PAIRS, T), carve(1024, KV_HEADS, 4 * P)
        qrT = carve(2048, PAIRS, T)
        krT = xn[:].rearrange("p b d -> p (b d)").rearrange("p (h t) -> p h t", t=T)
        acc_a = carve(0, 2, 2, 512)
        const1 = carve(at, N_CONST1); at += N_CONST1
        vr = carve(at, 4, 512); ctx_in = carve(at, TB, D); at += 2048
        kava = carve(at, 4, 256); at += 1024
        staged = carve(at, 4, 512); mem_in = carve(at, TB, D)
        decay_arg, decay_mat = carve(at, 384), carve(at + 384, 384)
        q_dec = carve(at + 768, 2, T); q_decayed = carve(at + 1280, 2, T); at += 2048
        krn = carve(at, TB, 512); y_mix = carve(at, TB, D); at += 1024
        qrn = carve(at, TB, 512); at += 1024
        qan = carve(at, TB, 512); at += 1024
        gain_diag = [krn.rearrange("p a n -> p (a n)"), qan.rearrange("p a n -> p (a n)")]
        k_fb = carve(at, 2, TB, 512); mem_k = carve(at, TB, D)
        ret_p, probs = carve(at, 2, 2 * T), carve(at + 1024, 2, 512); at += 2048
        rope_a, rope_b = carve(at, 512), carve(at + 512, 512); probsT = carve(at, 2, 4 * P); at += 1024
        silu_gr = carve(at, TB, 512); tables = carve(at, 4, TB * HD); at += 1024
        ka_all = carve(at, 4, P); at += 512
        state = shifted_T[:].rearrange("p a (h c) -> p a h c", c=HD)
        ctx_decay = sb("ctx_decay", [P, 4, HEADS])
        lg_rows = sb("lg_rows", [P, 16])
        lg_pairs = sb("lg_pairs", [P, 8])
        head_ss = sb("head_ss", [P, 16])
        head_rms = sb("head_rms", [P, 16])
        head_rstd = sb("head_rstd", [P, 16])
        row_max = sb("row_max", [P, 16])
        row_sum = sb("row_sum", [P, 16])
        row_inv = sb("row_inv", [P, 16])

        def c1(name, a=0, b=None):
            lo, hi = CONST1[name]
            return const1[:, lo + a:(lo + b if b is not None else hi)]

        gate = carve(2 * 2 * UP * T, 3, TB, 256)
        y_ffn = carve(2 * 2 * UP * T + 3 * TB * 256, TB, D)

        at = 2048 + (LEVELS + 2) * P
        const2 = carve(at, (2 * LEVELS + 3) * P); at += (2 * LEVELS + 3) * P
        fgate = carve(at, TB, 512); at += 1024
        hk = carve(at, TB, 512); uT = carve(at, 4 * (T + 2)); at += 1032
        hq = carve(at, TB, 512); conv = carve(at, 4, T); at += 1024
        hv = carve(at, TB, 512); at += 1024
        zc_sb = carve(at, TB, 512); at += 1024
        zb_sb = carve(at, TB, 512); at += 1024
        silu_zg = carve(at, TB, 512); at += 1024
        hkT, hqT = carve(at, 8 * P), carve(at + 1024, 8 * P); at += 2048
        scT = carve(at, 8 * P); at += 1024
        crossT = carve(at, 4 * P); at += 512
        head_row = rows[:, 1, 0:512]
        lb_p = carve(at, 2, 512); lb = carve(at + 1024, 512); one_lb = carve(at + 1536, 512); at += 2048
        hgrn_sq = lb_p[:, 0, :]
        level_mask = const2[:, (LEVELS + 2) * P:].rearrange("p (l t) -> p l t", t=P)
        qk_dec = [xn[:, b, :] for b in range(2)]

        mq = carve(0, TB, D)
        mqT = carve(2048, KC, T)
        mprobs = carve(4096, 2, T)
        mprobsT = carve(4608, 2, 4 * P)

        bank = [stack.enter_context(nc.psum_tensor(f"bank{b}", [P, 512], F32)) for b in range(8)]
        bank_full = [sem(f"bank{b}_full") for b in range(8)]
        bank_read = [sem(f"bank{b}_read") for b in range(8)]
        raw_ready = [sem(f"raw_ready{s}") for s in range(RING)]
        mod_used = sem("mod_used")
        hi_ready = sem("hi_ready")
        split_ready = sem("split_ready")
        split_used = sem("split_used")

        def free(eng, name):
            b, k, _ = plan.of[name]
            if k:
                eng.wait_ge(bank_read[b], k)
            return bank[b]

        def filled(eng, name):
            b, _, s = plan.of[name]
            eng.wait_ge(bank_full[b], s + 1)
            return bank[b]

        def read_out(eng, name):
            b, k, _ = plan.of[name]
            eng.wait_ge(bank_read[b], k + 1)

        def bank_of(name):
            return bank[plan.of[name][0]]

        def full_sem(name):
            return bank_full[plan.of[name][0]]

        def read_sem(name):
            return bank_read[plan.of[name][0]]

        def raw_free(sp, u):
            kind, n = STREAM[u - RING]
            if kind == "w":
                sp.wait_ge(split_ready, n + 1)
            else:
                sp.wait_ge(mod_used, n + 1)

        acc_b = rows[:, 0, :].rearrange("p (a n) -> p a n", n=512)

        def heads_bc(ap, n, d):
            return ap.unsqueeze(2).to_broadcast([P, n, d])

        def over_heads(ap, n, d):
            return ap.unsqueeze(1).to_broadcast([P, n, d])

        def x_ready(n):
            return lambda eng: eng.wait_ge(sem("x_ready"), n)

        def x_added(name):
            return lambda eng: [read_out(eng, (*name, tb, c)) for tb in range(TB) for c in range(2)]

        shift_buf = lambda k: shifted_T[:, k % 2, :].rearrange("p (a t) -> p a t", t=T)

        block = stack.enter_context(nc.Block())

        @block.sync
        def _(sp):
            small = [(cols[:], io["cols"], "cols_loaded"), (mem_in, io["mem"], "mem_loaded"),
                     (fixed[:], io["fixed"], "fixed_loaded")]
            for dst, src, name in small:
                sp.dma_start(dst, src).then_inc(sem(name), 16)
            for u in range(HEAD_UNITS):
                if u >= RING:
                    raw_free(sp, u)
                sp.dma_start(raw[:, u % RING, :], io["weights"][u]).then_inc(raw_ready[u % RING], 16)
                for at_unit, dst, src, name in [(3, x[:], io["x"], "x_loaded"), (6, ctx_in, io["ctx"], "ctx_loaded"),
                                                (9, const1, io["const1"], "const1_loaded")]:
                    if u == at_unit:
                        sp.dma_start(dst, src).then_inc(sem(name), 16)
            first = len(STREAM) - HEAD_UNITS
            for u in range(HEAD_UNITS, HEAD_UNITS + RING):
                raw_free(sp, u)
                sp.dma_start(raw[:, u % RING, :], io["weights"][u]).then_inc(raw_ready[u % RING], 16)
            assert first % RING == 0
            with sp.Fori(0, first // RING - 1) as i:
                for j in range(RING):
                    u0 = HEAD_UNITS + RING + j
                    sp.wait_ge(split_ready, i * RING + (W_OUT + j + 1))
                    sp.dma_start(raw[:, u0 % RING, :], io["weights"][bass.ds(i * RING + u0, 1)].rearrange("a p n -> (a p) n"))\
                        .then_inc(raw_ready[u0 % RING], 16)
            for tb in range(TB):
                sp.wait_ge(sem("out_ready"), tb + 1)
                sp.dma_start(io["out"][tb], xn[:, tb, :]).then_inc(sem("stored"), 16)
            sp.wait_ge(sem("stored"), 16 * TB)

        @block.gpsimd
        def _(pool):
            def low_part(v_slot, u_slot, count):
                pool.wait_ge(hi_ready, count)
                pool.tensor_tensor(w_lo[:, v_slot, :], raw[:, u_slot, :], w_hi[:, v_slot, :].bitcast(F32),
                                   ALU.subtract).then_inc(split_ready, 1)

            for v in range(W_OUT):
                low_part(v % RING, RAW_AT[("w", v)] % RING, v + 1)
            with pool.Fori(0, (N_W - W_OUT) // RING) as i:
                for j in range(RING):
                    v0 = W_OUT + j
                    low_part(v0 % RING, RAW_AT[("w", v0)] % RING, i * RING + (v0 + 1))

        @block.scalar
        def _(act):
            chained = [0]

            def chain(ins):
                chained[0] += 1
                ins.then_inc(sem("act_chain"), 1)
                act.wait_ge(sem("act_chain"), chained[0])

            def high_part(v_slot, u_slot, loads, used, waits=True):
                act.wait_ge(raw_ready[u_slot], loads)
                if waits:
                    act.wait_ge(split_used, used)
                act.activation(w_hi[:, v_slot, :], raw[:, u_slot, :], ACT.Copy).then_inc(hi_ready, 1)

            split = [0]

            def split_to(n):
                while split[0] < min(n, N_W):
                    v = split[0]
                    u = RAW_AT[("w", v)]
                    high_part(v % RING, u % RING, 16 * (u // RING + 1), v - RING + 1, v >= RING)
                    split[0] += 1

            def split_behind(p):
                passed = RAW_AT[("w", p + 1)]
                reach = lambda v: all(STREAM[u][0] == "w" or u < passed for u in range(RAW_AT[("w", v)] - RING + 1))
                n = p + 1
                while n < min(p + 1 + RING, W_OUT) and reach(n):
                    n += 1
                split_to(n)

            def used(v):
                act.wait_ge(split_used, v + 1)

            norms = [0]

            def norm_stats(src, ready):
                ready(act)
                n = norms[0]
                norms[0] += 1
                if n:
                    act.wait_ge(sem("norm_rstd"), n)
                act.activation(xn_junk[0], src[:, 0, :], ACT.Square, accum_out=ssq[:, 0:1]).then_inc(sem("norm_ss_a"), 1)
                act.wait_ge(sem("norm_ss_a"), n + 1)
                act.wait_ge(sem("norm_ss_v"), n + 1)
                act.activation(rms[:, :], ssq[:, :], ACT.Sqrt, scale=1.0 / D, bias=eps[:, 0:1]).then_inc(sem("norm_rms"), 1)
                act.wait_ge(sem("norm_rstd"), n + 1)

            xn_junk = [rows[:, 0, :]]

            def norm_scale(src, dst):
                act.activation(dst[:, 0, :], src[:, 0, :], ACT.Copy, scale=rstd[:, 0:1]).then_inc(sem("xn_a"), 1)

            def split_T(stage, gain=None, shifted=False, hi=hT_hi, n=4, qs=None, first=0):
                for q in qs or range(n):
                    if shifted:
                        act.wait_ge(sem("full_T"), shifts[0] + 1)
                        act.activation(hi[:, 2 * q:2 * q + 2, :], shift_buf(shifts[0]), ACT.Copy).then_inc(sem("T_hi"), 1)
                        shifts[0] += 1
                        continue
                    b = filled(act, (stage, q))
                    if gain is None:
                        act.activation(hi[:, first + 2 * q:first + 2 * q + 2, :].rearrange("p a t -> p (a t)"), b[:, :], ACT.Copy)\
                            .then_inc(sem("T_hi"), 1)
                    else:
                        act.activation(hi[:, 2 * q, :], b[:, 0:T], ACT.Copy, scale=gain[:, 2 * q:2 * q + 1])
                        act.activation(hi[:, 2 * q + 1, :], b[:, T:2 * T], ACT.Copy, scale=gain[:, 2 * q + 1:2 * q + 2])\
                            .then_inc(sem("T_hi"), 1)

            shifts = [0]

            def copy_out(name, dst, func=ACT.Copy, n=512):
                act.activation(dst, bank_of(name)[:, 0:n], func).then_inc(read_sem(name), 1)

            act.wait_ge(sem("eps_set"), 1)
            act.wait_ge(sem("cols_loaded"), 16)
            act.activation(silu_c[:].rearrange("p k c -> p (k c)"), col("cond"), ACT.Silu).then_inc(sem("silu_c"), 1)
            act.activation(lg_rows[:, :], col("decay_rows"), ACT.Exp).then_inc(sem("lg_exp"), 1)
            act.activation(lg_pairs[:, :], col("decay_pairs"), ACT.Exp).then_inc(sem("lg_exp"), 1)
            norm_stats(mem_in, lambda e: e.wait_ge(sem("mem_loaded"), 16))
            norm_scale(mem_in, xn)
            split_to(1)
            split_T("memT", col("mem_norm"))
            split_to(3)
            norm_stats(x, lambda e: e.wait_ge(sem("x_loaded"), 16))
            filled(act, ("memT", 3))
            norm_scale(x, xn)
            for c in range(4):
                split_behind(W_KV + 2 * c)
                if c < 3:
                    split_behind(W_KV + 2 * c + 1)
                used(W_KV + 2 * c + 1)
                for tb in range(TB):
                    dst = (mem_k if c < 2 else memV)[:, tb, (c % 2) * 512:(c % 2 + 1) * 512]
                    copy_out(("kv", c, tb), dst)
                if c == 0:
                    norm_stats(ctx_in, lambda e: e.wait_ge(sem("ctx_loaded"), 16))
                    norm_scale(ctx_in, rows)
                if c == 2:
                    act.wait_ge(sem("lg_neg"), 2)
                    act.wait_ge(sem("const1_loaded"), 16)
                    for fb in range(2):
                        for jb in range(TB):
                            a = act.activation(ctx_decay[:, 2 * fb + jb, :], lg_rows[:, 8 * fb:8 * fb + 8], ACT.Exp,
                                               scale=c1("ctx_dist", 2 * fb + jb, 2 * fb + jb + 1))
                            a.then_inc(sem("ctx_decay"), 1)
            split_to(W_IN + 1)
            for q in range(4):
                b = filled(act, ("keyT", q))
                act.activation(memKT[:, 2 * q:2 * q + 2, :].rearrange("p a t -> p (a t)"), b[:, :], ACT.Copy)\
                    .then_inc(read_sem(("keyT", q)), 1)
            for n in range(4):
                if n == 2:
                    split_to(W_IN + 2)
                split_T(None, shifted=True, hi=[hT_hi, hcT_hi][n % 2], qs=[2 * (n // 2), 2 * (n // 2) + 1])

            for part, v, n in [("kr", 0, 2), ("vr", 2, 2), ("kava", 4, 1), ("qa", 5, 2), ("qr", 7, 2), ("gr", 9, 2)]:
                split_behind(W_IN + v + n - 1)
                used(W_IN + v + n - 1)
                if part == "kr":
                    for tile in range(4):
                        copy_out((part, tile), staged[:, tile, :])
                elif part == "vr":
                    for tile in range(4):
                        copy_out((part, tile), vr[:, tile, :])
                elif part == "kava":
                    for tile in range(4):
                        copy_out((part, tile), kava[:, tile, :], n=256)
                    act.wait_ge(sem("ka_ss"), 1)
                    act.activation(head_rms[:, 0:8], head_ss[:, 0:8], ACT.Sqrt, scale=1.0 / HD, bias=eps[:, 0:1])\
                        .then_inc(sem("ka_rms"), 1)
                elif part == "qa":
                    act.wait_ge(sem("kr_done"), 1)
                    for tb in range(TB):
                        copy_out((part, tb), staged[:, tb, :])
                    act.wait_ge(sem("qa_ss"), 1)
                    act.activation(head_rms[:, :], head_ss[:, :], ACT.Sqrt, scale=1.0 / HD, bias=eps[:, 0:1])\
                        .then_inc(sem("qa_rms"), 1)
                elif part == "qr":
                    for tb in range(TB):
                        copy_out((part, tb), staged[:, 2 + tb, :])
                else:
                    act.wait_ge(sem("rope_done"), 6)
                    for tb in range(TB):
                        copy_out((part, tb), silu_gr[:, tb, :], ACT.Silu)
            for q in range(2):
                b = filled(act, ("krT", q))
                for e in range(2):
                    half = slice(64 * e, 64 * e + 64)
                    ins = act.activation(krT.rearrange("p (n e) t -> p n e t", e=2)[half, 2 * q:2 * q + 2, e, :],
                                         b[half, :].rearrange("p (n t) -> p n t", t=T), ACT.Copy)
                ins.then_inc(read_sem(("krT", q)), 1)
            b = filled(act, ("kaT", 0))
            for e in range(2):
                half = slice(64 * e, 64 * e + 64)
                ins = act.activation(kaT[half, e, :], b[half, :], ACT.Copy)
            ins.then_inc(read_sem(("kaT", 0)), 1)
            for name, dst in [("qaT", qaT), ("qrT", qrT)]:
                for q in range(2):
                    b = filled(act, (name, q))
                    act.activation(dst[:, 2 * q:2 * q + 2, :].rearrange("p a t -> p (a t)"), b[:, :], ACT.Copy)\
                        .then_inc(read_sem((name, q)), 1)

            def attention_probs(s):
                act.wait_ge(sem("neg_max"), s + 1)
                if s >= 2:
                    filled(act, ("probsT", s - 2))
                act.activation(probs[:, s % 2, :], bank_of(("scores", s))[:, :], ACT.Exp, scale=HD ** -0.5,
                               bias=row_max[:, s:s + 1], accum_out=row_sum[:, s:s + 1]).then_inc(read_sem(("scores", s)), 1)

            attention_probs(0)
            for s in range(2 * HEADS):
                r = s // 2
                if s + 1 < 2 * HEADS:
                    attention_probs(s + 1)
                if s == 2 * HEADS - 3:
                    split_to(W_OUT + RING)
                if s % 2 == 0:
                    act.wait_ge(sem("decay_arg"), r + 1)
                    if r:
                        read_out(act, ("ret_scores", r - 1))
                    act.activation(decay_mat, decay_arg, ACT.Exp).then_inc(sem("decay_mat"), 1)
                    if r % 2 == 0:
                        if r:
                            act.wait_ge(sem("q_decayed"), r)
                        act.activation(q_dec[:, 0, :], c1("from_start"), ACT.Exp, scale=lg_pairs[:, r // 2:r // 2 + 1])
                        act.activation(q_dec[:, 1, :], c1("to_end"), ACT.Exp, scale=lg_pairs[:, 4 + r // 2:5 + r // 2])\
                            .then_inc(sem("q_dec"), 1)
                b = filled(act, ("probsT", s))
                if s >= 2:
                    act.wait_ge(sem("att_step"), s - 1)
                act.activation(probsT[:, s % 2, :], b[:, :], ACT.Copy).then_inc(read_sem(("probsT", s)), 1)
            act.wait_ge(sem("att_step"), 2 * HEADS)
            for tb in range(TB):
                act.activation(hT_hi[:, 0:4, tb * P:(tb + 1) * P], bank_of(("att", tb))[:, :].rearrange("p (a t) -> p a t", t=P),
                               ACT.Copy).then_inc(sem("T_hi"), 1)
            for tb in range(TB):
                act.wait_ge(sem("ret_centred"), tb + 1)
                act.activation(probs[:, tb, :], xn[:, tb, 512:1024], ACT.Square).then_inc(sem("ret_sq"), 1)
            act.wait_ge(sem("ret_var"), 1)
            act.activation(head_rms[:, :], head_ss[:, :], ACT.Sqrt, scale=1.0 / HD, bias=eps[:, 0:1])\
                .then_inc(sem("ret_rms"), 1)
            split_to(W_OUT + 4)
            for q in range(4):
                b = filled(act, ("gain_row", q))
                act.activation(rows[:, q // 2, (q % 2) * 512:(q % 2 + 1) * 512], b[:, :], ACT.Copy)\
                    .then_inc(read_sem(("gain_row", q)), 1)
            split_T("mixT", n=2, first=4)

            def post_norm(y, name, last):
                used(last)
                for c in range(2):
                    copy_out((*name, 0, c), y[:, 0, c * 512:(c + 1) * 512])
                read_out(act, (*name, 0, 0))
                read_out(act, (*name, 0, 1))
                norm_stats(y, lambda e: None)

            xn_junk[0] = xn[:, 0, :]
            post_norm(y_mix, ("mix_out",), W_OUT + 3)
            split_to(W_OUT + 4 + RING)

            def ffn(f):
                up, dn = W_UP[f], W_DN[f]

                def silu_gate(c, before, i=None):
                    act.wait_ge(split_used, before)
                    for tb in range(TB):
                        act.activation(gate[:, c % 3, tb, :], bank[(c % 3) * 2 + tb][:, 0:256], ACT.Silu)\
                            .then_inc(sem("gate_silu"), 1)

                g0 = plan.of[("gateT", f, 0)][2]

                def gate_hi(c, full, at):
                    act.wait_ge(bank_full[6], full)
                    act.activation(gT_hi[:, at, :] if isinstance(at, slice) else gT_hi[:, bass.ds(at, 2), :],
                                   bank[6][:, :].rearrange("p (a t) -> p a t", t=T), ACT.Copy).then_inc(sem("gateT_hi"), 1)

                split_to(up + RING)
                for c in range(2):
                    split_to(up + 2 * c + 5)
                    silu_gate(c, up + 2 * c + 2)
                    if c:
                        gate_hi(0, g0 + 1, slice(0, 2))
                v0 = split[0]
                u0 = RAW_AT[("w", v0)]
                assert v0 == up + 7
                with act.Fori(0, 3) as i:
                    for j in range(3):
                        for e in range(2):
                            k = 2 * j + e
                            high_part((v0 + k) % RING, (u0 + k) % RING, i * 32 + 16 * ((u0 + k) // RING + 1),
                                      i * 6 + (v0 + k - RING + 1))
                        c = 2 + j
                        silu_gate(c, i * 6 + (up + 2 * c + 2))
                        gate_hi(c - 1, i * 3 + (g0 + c), i * 6 + 2 * (c - 1))
                split[0] += 18
                split_to(dn + 1 + RING)
                gate_hi(UP - 1, g0 + UP, slice(2 * UP - 2, 2 * UP))
                split_to(dn + UP)

            def pre_norm(stage, ready, gain=None, shifted=False):
                norm_stats(x, ready)
                norm_scale(x, xn)
                split_T(stage, gain, shifted)

            pre_norm("ffn0T", x_ready(1), shifted=True)
            ffn(0)
            post_norm(y_ffn, ("down", 0), W_DN[0] + UP - 1)
            split_to(W_UP[1] + RING)
            pre_norm("ffn1T", x_ready(2), col("ffn1_norm"))
            act.dma_start(rows[:, 0, :], io["final_norm"].to_broadcast([P, D])).then_inc(sem("final_loaded"), 16)
            ffn(1)
            used(W_DN[1] + UP - 1)
            for dst, src, name in [(const2, io["const2"], "const2_loaded"),
                                   (lb_p.rearrange("p a n -> p (a n)"), io["lb_param"].to_broadcast([P, D]), "lb_loaded"),
                                   (head_row, io["hgrn_out_norm"].to_broadcast([P, 512]), "head_row_loaded")]:
                act.dma_start(dst, src).then_inc(sem(name), 16)
            pre_norm("mix2T", x_added(("down", 1)), col("mix_norm"))
            split_to(W_IN2 + RING)

            act.wait_ge(sem("const2_loaded"), 16)
            act.activation(sums_r[:].rearrange("p l t -> p (l t)"), const2[:, 0:(LEVELS + 2) * P], ACT.Copy)\
                .then_inc(sem("sums_ready"), 1)
            act.wait_ge(sem("lb_diff"), 1)
            act.activation(lb_p[:].rearrange("p a n -> p (a n)"), lb_p[:].rearrange("p a n -> p (a n)"), ACT.Exp)\
                .then_inc(sem("lb_exp"), 1)

            def streamed_out(k, part, dst, func=ACT.Copy):
                split_to(W_IN2 + 2 * k + 2 + RING)
                used(W_IN2 + 2 * k + 1)
                for tb in range(TB):
                    copy_out((part, tb), dst[:, tb, :], func)

            def level_decays(level):
                for blk in range(TB):
                    b = filled(act, ("decay", level, blk))
                    if blk == 0 and level >= 2:
                        filled(act, ("pairs", level - 2, 1))
                    act.activation(qk_dec[level % 2][:, blk * 512:(blk + 1) * 512], b[:, :], ACT.Exp)\
                        .then_inc(read_sem(("decay", level, blk)), 1)

            streamed_out(0, "zf", fgate, ACT.Sigmoid)
            act.wait_ge(sem("fgate"), 1)
            streamed_out(1, "zq", hq, ACT.Silu)
            act.activation(fgate[:].rearrange("p a n -> p (a n)"), fgate[:].rearrange("p a n -> p (a n)"), ACT.Ln)\
                .then_inc(sem("logf"), 1)
            act.wait_ge(sem("logf"), 1)
            act.activation(logf_hi[:].rearrange("p a n -> p (a n)"), fgate[:].rearrange("p a n -> p (a n)"), ACT.Copy)\
                .then_inc(sem("logf_hi"), 1)
            streamed_out(2, "zi", hv)
            for q in range(2):
                b = filled(act, ("hqT", q))
                act.activation(hqT[:, q * 512:(q + 1) * 512], b[:, :], ACT.Copy, scale=P ** -0.5)\
                    .then_inc(read_sem(("hqT", q)), 1)
            for q in range(2):
                b = filled(act, ("hkT", q))
                act.activation(hkT[:, q * 512:(q + 1) * 512], b[:, :], ACT.Copy).then_inc(read_sem(("hkT", q)), 1)
            for step in range(8):
                split_to(W_IN2 + 6 + step + RING)
                level_decays(step)
                if step == 1:
                    streamed_out(3, "zc", zc_sb)
                if step == 3:
                    split_to(W_IN2 + 10 + RING)
                if step == 5:
                    streamed_out(5, "zb", zb_sb)
            streamed_out(6, "zg", silu_zg, ACT.Silu)
            for j in range(2):
                b = filled(act, f"uT{j}")
                act.activation(uT.rearrange("p (c t) -> p c t", t=T + 2)[:, 2 * j:2 * j + 2, 2:T + 2],
                               b[:, :].rearrange("p (c t) -> p c t", t=T), ACT.Copy).then_inc(read_sem(f"uT{j}"), 1)
            for j in range(2):
                read_out(act, f"bT{j}")
                act.activation(hT_hi[:, 4 + 2 * j:6 + 2 * j, :], conv[:, 2 * j:2 * j + 2, :], ACT.Copy)\
                    .then_inc(sem("conv_hi"), 1)
            for blk in range(TB):
                b = filled(act, ("hgrn", blk))
                if blk:
                    act.wait_ge(sem("hgrn_ss"), blk)
                act.activation(hgrn_sq, b[:, :], ACT.Square).then_inc(sem("hgrn_sq"), 1)
            act.wait_ge(sem("hgrn_ss"), TB)
            act.activation(head_rms[:, 0:8], head_ss[:, 0:8], ACT.Sqrt, scale=1.0 / P, bias=eps[:, 0:1])\
                .then_inc(sem("hgrn_rms"), 1)
            split_T("mix2oT", n=2)
            split_to(W_OUT2 + 4 + RING)
            pre_norm("xattT", x_added(("mix2_out",)), col("xattn_norm"))

            split_to(W_Q + 4)
            used(W_Q + 3)
            for c in range(2):
                for tb in range(TB):
                    copy_out(("mq", tb, c), mq[:, tb, c * 512:(c + 1) * 512])
            for q in range(4):
                b = filled(act, ("mqT", q))
                act.activation(mqT[:, 2 * q:2 * q + 2, :].rearrange("p a t -> p (a t)"), b[:, :], ACT.Copy)\
                    .then_inc(read_sem(("mqT", q)), 1)
            split_to(W_O + RING)
            for h in range(MEM_HEADS):
                for tb in range(TB):
                    s = TB * h + tb
                    act.wait_ge(sem("neg_max"), 16 + s + 1)
                    if h:
                        filled(act, ("mprobsT", h - 1))
                    act.activation(mprobs[:, tb, :], bank_of(("mscores", h, tb))[:, 0:T], ACT.Exp, scale=MEM_HD ** -0.5,
                                   bias=row_max[:, s:s + 1], accum_out=row_sum[:, s:s + 1])\
                        .then_inc(read_sem(("mscores", h, tb)), 1)
                b = filled(act, ("mprobsT", h))
                if h >= 2:
                    act.wait_ge(sem("matt_step"), h - 1)
                act.activation(mprobsT[:, h % 2, :], b[:, :], ACT.Copy).then_inc(read_sem(("mprobsT", h)), 1)
            split_T("mattT")
            split_to(W_O + 4 + RING)
            pre_norm("ffn2T", x_added(("mem_out",)), col("ffn2_norm"))
            ffn(2)
            norm_stats(x, x_added(("down", 2)))

        @block.vector
        def _(dve):
            chained = [0]

            def chain(ins):
                chained[0] += 1
                ins.then_inc(sem("dve_chain"), 1)
                dve.wait_ge(sem("dve_chain"), chained[0])

            norms = [0]
            junk = [rows[:, 1, :]]

            def norm_stats(src, ready):
                ready(dve)
                n = norms[0]
                norms[0] += 1
                dve.tensor_tensor_reduce(out=junk[0], in0=src[:, 1, :], in1=src[:, 1, :], scale=1.0, scalar=0.0,
                                         op0=ALU.mult, op1=ALU.add, accum_out=ssq[:, 1:2]).then_inc(sem("norm_ss_v"), 1)
                dve.wait_ge(sem("norm_rms"), n + 1)
                dve.reciprocal(rstd[:, :], rms[:, :]).then_inc(sem("norm_rstd"), 1)
                dve.wait_ge(sem("norm_rstd"), n + 1)

            def norm_scale(src, dst):
                dve.tensor_scalar(dst[:, 1, :], src[:, 1, :], rstd[:, 1:2], None, ALU.mult).then_inc(sem("xn_v"), 1)

            hi_seen = [0]
            shifts = [0]

            def split_T(stage, gain=None, shift=None, hi=hT_hi, lo=hT_lo, n=4, qs=None, first=0):
                for q in qs or range(n):
                    name = (stage, q)
                    if shift is not None:
                        a, s = shift
                        b = filled(dve, name)
                        buf = shift_buf(shifts[0])
                        for e in range(2):
                            k = 2 * q + e
                            ins = dve.tensor_scalar(buf[:, e, :], b[:, e * T:(e + 1) * T], a[:, k:k + 1], s[:, k:k + 1],
                                                    ALU.mult, ALU.add)
                        ins.then_inc(sem("full_T"), 1)
                        shifts[0] += 1
                        hi_seen[0] += 1
                        dve.wait_ge(sem("T_hi"), hi_seen[0])
                        dve.tensor_tensor(lo[:, 2 * q:2 * q + 2, :], buf, hi[:, 2 * q:2 * q + 2, :].bitcast(F32), ALU.subtract)\
                            .then_inc(read_sem(name), 1)
                        continue
                    hi_seen[0] += 1
                    dve.wait_ge(sem("T_hi"), hi_seen[0])
                    b = bank_of(name)
                    if gain is None:
                        k = slice(first + 2 * q, first + 2 * q + 2)
                        dve.tensor_tensor(lo[:, k, :], b[:, :].rearrange("p (a t) -> p a t", t=T),
                                          hi[:, k, :].bitcast(F32), ALU.subtract).then_inc(read_sem(name), 1)
                    else:
                        for e in range(2):
                            k = 2 * q + e
                            ins = dve.scalar_tensor_tensor(out=lo[:, k, :], in0=b[:, e * T:(e + 1) * T],
                                                           scalar=gain[:, k:k + 1], in1=hi[:, k, :].bitcast(F32),
                                                           op0=ALU.mult, op1=ALU.subtract)
                        ins.then_inc(read_sem(name), 1)

            ropes = [0]

            def rope(src, cos, sin, dst, n):
                v = src.rearrange("p (h d) -> p h d", d=HD)
                a = rope_a[:, 0:n * HD].rearrange("p (h d) -> p h d", d=HD)
                b = rope_b[:, 0:n * HD].rearrange("p (h d) -> p h d", d=HD)
                dve.tensor_tensor(a, v, over_heads(cos, n, HD), ALU.mult)
                dve.tensor_tensor(b[:, :, 0:HD // 2], v[:, :, HD // 2:HD], over_heads(sin[:, 0:HD // 2], n, HD // 2), ALU.mult)
                chain(dve.tensor_tensor(b[:, :, HD // 2:HD], v[:, :, 0:HD // 2], over_heads(sin[:, HD // 2:HD], n, HD // 2),
                                        ALU.mult))
                if len(dst.shape) == 4:
                    a = a.rearrange("p (k j) d -> p k j d", k=KV_HEADS)
                    b = b.rearrange("p (k j) d -> p k j d", k=KV_HEADS)
                dve.tensor_tensor(dst, a, b, ALU.add).then_inc(sem("rope_done"), 1)
                ropes[0] += 1
                dve.wait_ge(sem("rope_done"), ropes[0])

            heads = lambda ap: ap.rearrange("p (h d) -> p h d", d=HD)

            dve.memset(eps[:, :], EPS).then_inc(sem("eps_set"), 1)
            dve.wait_ge(sem("fixed_loaded"), 16)
            norm_stats(mem_in, lambda e: e.wait_ge(sem("mem_loaded"), 16))
            norm_scale(mem_in, xn)
            dve.wait_ge(sem("cols_loaded"), 16)
            split_T("memT", col("mem_norm"))
            dve.wait_ge(sem("lg_exp"), 2)
            dve.tensor_scalar(lg_rows[:, :], lg_rows[:, :], -1.0, None, ALU.mult).then_inc(sem("lg_neg"), 1)
            dve.tensor_scalar(lg_pairs[:, :], lg_pairs[:, :], -1.0, None, ALU.mult).then_inc(sem("lg_neg"), 1)
            def weigh_mod(m):
                u, c, half = RAW_AT[("mod", m)], m // 2, m % 2
                dve.wait_ge(raw_ready[u % RING], 16 * (u // RING + 1))
                if half == 0 and (2 <= c < MOD_A // 2 or c >= MOD_A // 2 + 2):
                    if c - 2 in MOD_STEPS:
                        filled(dve, ("mod_col", c - 2))
                    else:
                        dve.wait_ge(sem("mod_col"), c - 1)
                for k in range(4):
                    w = raw[:, u % RING, k * 512:(k + 1) * 512]
                    for cond in range(2 if m < MOD_A else 1):
                        acc = acc_a[:, c % 2, cond, :] if m < MOD_A else acc_b[:, c % 2, :]
                        s = silu_c[:, 4 * half + k, cond:cond + 1]
                        if half == 0 and k == 0:
                            ins = dve.tensor_scalar(acc, w, s, None, ALU.mult)
                        else:
                            ins = dve.scalar_tensor_tensor(out=acc, in0=w, scalar=s, in1=acc, op0=ALU.mult, op1=ALU.add)
                    if k < 3:
                        chain(ins)
                ins.then_inc(mod_used, 1)
                dve.wait_ge(mod_used, m + 1)

            dve.wait_ge(sem("silu_c"), 1)
            weigh_mod(0)
            weigh_mod(1)
            norm_stats(x, lambda e: e.wait_ge(sem("x_loaded"), 16))
            filled(dve, ("memT", 3))
            norm_scale(x, xn)
            weigh_mod(2)
            norm_stats(ctx_in, lambda e: e.wait_ge(sem("ctx_loaded"), 16))
            norm_scale(ctx_in, rows)
            for m in range(3, MOD_A):
                weigh_mod(m)
            dve.wait_ge(sem("const1_loaded"), 16)
            half = HD // 2
            for n, base in ((0, 0), (1, HD)):
                g = col("qk_gain", base, base + HD)
                cs, sn = (tables[:, 2 * n + e, :].rearrange("p (b d) -> p b d", d=HD) for e in range(2))
                cos_t = c1("rope_cos").rearrange("p (b d) -> p b d", d=HD)
                sin_t = c1("rope_sin").rearrange("p (b d) -> p b d", d=HD)
                dve.tensor_tensor(cs, cos_t, over_heads(g, TB, HD), ALU.mult)
                dve.tensor_tensor(sn[:, :, 0:half], sin_t[:, :, 0:half], over_heads(g[:, half:HD], TB, half), ALU.mult)
                chain(dve.tensor_tensor(sn[:, :, half:HD], sin_t[:, :, half:HD], over_heads(g[:, 0:half], TB, half), ALU.mult))
            dve.wait_ge(sem("ctx_decay"), 4)
            chain(dve.tensor_scalar(ctx_decay[:], ctx_decay[:], HD ** -0.5, None, ALU.mult))

            dve.wait_ge(sem("mod_col"), MOD_A // 2)
            b = bank_of("mod_a")
            chain(dve.tensor_tensor(mod[:, 0:16, :], b[:, 0:32].rearrange("p (j c) -> p j c", c=2),
                                    heads_bc(col("b_mod", 0, 16), 16, 2), ALU.add))
            chain(dve.tensor_scalar(a_mix[:], mod[:, 8:16, :], 1.0, None, ALU.add))
            dve.tensor_tensor(a_mix[:], a_mix[:], heads_bc(col("g_pre_mix"), 8, 2), ALU.mult).then_inc(read_sem("mod_a"), 1)
            read_out(dve, "mod_a")
            for n in range(4):
                cond = n % 2
                split_T(("xT", "ctxT")[cond], shift=(a_mix[:, :, cond], mod[:, 0:8, cond]), hi=[hT_hi, hcT_hi][cond],
                        lo=[hT_lo, hcT_lo][cond], qs=[2 * (n // 2), 2 * (n // 2) + 1])

            read_out(dve, ("ctxT", 3))
            filled(dve, ("ctxT", 3))
            for m in range(MOD_A, MOD_A + 4):
                weigh_mod(m)
            for e in range(2):
                other = slice(64 * (1 - e), 64 * (1 - e) + 64)
                dve.memset(state.rearrange("p a (n e) c -> p a n e c", e=2)[other, :, :, e, :], 0.0)
                dve.memset(krT.rearrange("p (n e) t -> p n e t", e=2)[other, :, e, :], 0.0)

            read_out(dve, ("kr", 1))
            for tb in range(TB):
                rope(staged[:, tb, :], c1("rope_cos", tb * HD, (tb + 1) * HD), c1("rope_sin", tb * HD, (tb + 1) * HD),
                     heads(krn[:, tb, :]), HEADS)
            read_out(dve, ("kr", 3))
            for fb in range(2):
                for jb in range(TB):
                    ins = dve.tensor_tensor(heads(k_fb[:, fb, jb, :]), heads(staged[:, 2 + jb, :]),
                                            heads_bc(ctx_decay[:, 2 * fb + jb, :], HEADS, HD), ALU.mult)
            ins.then_inc(sem("kr_done"), 1)
            for m in range(MOD_A + 4, MOD_A + 10):
                weigh_mod(m)
            read_out(dve, ("kava", 3))
            sq = rope_a.rearrange("p (a b) -> p a b", b=P)
            chain(dve.tensor_tensor(sq, kava[:, :, 0:P], kava[:, :, 0:P], ALU.mult))
            dve.reduce_sum(head_ss[:, 0:8], rope_a.rearrange("p (h d) -> p h d", d=HD), AX.X).then_inc(sem("ka_ss"), 1)
            dve.wait_ge(sem("ka_rms"), 1)
            chain(dve.reciprocal(head_rstd[:, 0:8], head_rms[:, 0:8]))
            for tile in range(4):
                ins = dve.tensor_tensor(heads(kava[:, tile, 0:P]), heads(kava[:, tile, 0:P]),
                                        heads_bc(head_rstd[:, 2 * tile:2 * tile + 2], 2, HD), ALU.mult)
            chain(ins)
            for tile in range(2):
                dve.tensor_tensor(heads(ka_all[:, tile, :]), heads(kava[:, 2 + tile, 0:P]),
                                  over_heads(col("qk_gain", HD, 2 * HD), KV_HEADS, HD), ALU.mult)
                rope(kava[:, tile, 0:P], tables[:, 2, tile * HD:(tile + 1) * HD], tables[:, 3, tile * HD:(tile + 1) * HD],
                     heads(ka_all[:, 2 + tile, :]), KV_HEADS)
            for m in range(MOD_A + 10, 2 * MODS_IN):
                weigh_mod(m)
            for e in range(2):
                other = slice(64 * (1 - e), 64 * (1 - e) + 64)
                ins = dve.memset(kaT[other, e, :], 0.0)
            ins.then_inc(sem("keys_padded"), 1)
            read_out(dve, ("qa", 1))
            for tb in range(TB):
                chain(dve.tensor_tensor(rope_a, staged[:, tb, :], staged[:, tb, :], ALU.mult))
                ins = dve.reduce_sum(head_ss[:, tb * 8:tb * 8 + 8], heads(rope_a), AX.X)
                if tb == 0:
                    chain(ins)
            ins.then_inc(sem("qa_ss"), 1)
            dve.wait_ge(sem("qa_rms"), 1)
            chain(dve.reciprocal(head_rstd[:, :], head_rms[:, :]))
            for tb in range(TB):
                ins = dve.tensor_tensor(heads(staged[:, tb, :]), heads(staged[:, tb, :]),
                                        heads_bc(head_rstd[:, tb * 8:tb * 8 + 8], HEADS, HD), ALU.mult)
            chain(ins)
            for tb in range(TB):
                rope(staged[:, tb, :], tables[:, 0, tb * HD:(tb + 1) * HD], tables[:, 1, tb * HD:(tb + 1) * HD],
                     qan[:, tb, :].rearrange("p (j k d) -> p k j d", k=KV_HEADS, d=HD), HEADS)
            read_out(dve, ("qr", 1))
            for tb in range(TB):
                rope(staged[:, 2 + tb, :], c1("rope_cos", tb * HD, (tb + 1) * HD), c1("rope_sin", tb * HD, (tb + 1) * HD),
                     heads(qrn[:, tb, :]), HEADS)

            b = filled(dve, "states")
            for e in range(2):
                half = slice(64 * e, 64 * e + 64)
                ins = dve.tensor_copy(state.rearrange("p a (n e) c -> p a n e c", e=2)[half, :, :, e, :],
                                      b[half, :].rearrange("p (a n c) -> p a n c", a=2, c=HD))
            ins.then_inc(read_sem("states"), 1)

            def decay_of(r):
                if r:
                    dve.wait_ge(sem("decay_mat"), r)
                chain(dve.tensor_scalar(decay_arg, c1("fwd_dist"), lg_rows[:, r:r + 1], None, ALU.mult))
                dve.scalar_tensor_tensor(out=decay_arg, in0=c1("bwd_dist"), scalar=lg_rows[:, 8 + r:9 + r], in1=decay_arg,
                                         op0=ALU.mult, op1=ALU.add).then_inc(sem("decay_arg"), 1)

            def negative_max(s, name, n, scale):
                b = filled(dve, name)
                chain(dve.reduce_max(row_max[:, s:s + 1], b[:, 0:n], AX.X))
                dve.tensor_scalar(row_max[:, s:s + 1], row_max[:, s:s + 1], -scale, None, ALU.mult).then_inc(sem("neg_max"), 1)

            def normalise(s):
                read_out(dve, ("scores", s))
                chain(dve.reciprocal(row_inv[:, s:s + 1], row_sum[:, s:s + 1]))
                dve.tensor_scalar(probs[:, s % 2, :], probs[:, s % 2, :], row_inv[:, s:s + 1], None, ALU.mult)\
                    .then_inc(sem("probs_ready"), 1)

            def mod_column(cs, name):
                b = bank_of(name)
                ins = dve.tensor_tensor(mod[:, 4 * cs[0]:4 * cs[-1] + 4, 0], b[:, 0:4 * len(cs)],
                                        col("b_mod", 4 * cs[0], 4 * cs[-1] + 4), ALU.add)
                ins.then_inc(read_sem(name), 1)
                read_out(dve, name)

            dve.wait_ge(sem("mod_col"), MODS_IN)
            mod_column(list(range(MOD_A // 2, MODS_IN)), "mod_b")

            decay_of(0)
            negative_max(0, ("scores", 0), 512, HD ** -0.5)
            for s in range(2 * HEADS):
                r = s // 2
                if s + 1 < 2 * HEADS:
                    negative_max(s + 1, ("scores", s + 1), 512, HD ** -0.5)
                normalise(s)
                if s % 2 == 0:
                    dve.wait_ge(sem("decay_mat"), r + 1)
                    chain(dve.tensor_tensor(decay_mat[:, P:2 * P], decay_mat[:, P:2 * P], ident, ALU.add))
                    b = filled(dve, ("ret_scores", r))
                    if r >= 2:
                        dve.wait_ge(sem("ret_step"), r - 1)
                    for jb in range(TB):
                        ins = dve.scalar_tensor_tensor(out=ret_p[:, r % 2, jb * T:(jb + 1) * T], in0=b[:, jb * T:(jb + 1) * T],
                                                       scalar=HD ** -0.5, in1=decay_mat[:, (1 - jb) * P:(3 - jb) * P],
                                                       op0=ALU.mult, op1=ALU.mult)
                    ins.then_inc(read_sem(("ret_scores", r)), 1)
                    if r % 2 == 0:
                        dve.wait_ge(sem("q_dec"), r // 2 + 1)
                        read_out(dve, ("qrT", 1))
                        if r:
                            dve.wait_ge(sem("ret_step"), r)
                        for fb in range(2):
                            dve.tensor_tensor(q_decayed[:, fb, :], qrT[:, r // 2, :], q_dec[:, fb, :], ALU.mult)\
                                .then_inc(sem("q_decayed"), 1)
                    if r < HEADS - 1:
                        decay_of(r + 1)
                for c, step in MOD_STEPS.items():
                    if s in (step - 2, step - 1):
                        weigh_mod(2 * c + s - step + 2)
                    elif step == s:
                        filled(dve, ("mod_col", c))
                        mod_column([c], ("mod_col", c))
            dve.tensor_tensor(gain_col[:, 0, :], mod[:, 16:24, 0], col("g_post_mix"), ALU.mult)
            chain(dve.tensor_tensor(gain_col[:, 1, :], mod[:, 40:48, 0], col("g_post_ffn"), ALU.mult))
            for g in range(2):
                dve.tensor_tensor(gain_diag[g].rearrange("p (k t) -> p k t", t=P), over_heads(ident, KC, P),
                                  heads_bc(gain_col[:, g, :], KC, P), ALU.mult).then_inc(sem("gain_diag"), 1)
            chain(dve.tensor_scalar(a_ffn[:, :], mod[:, 32:40, 0], 1.0, None, ALU.add))
            chain(dve.tensor_tensor(a_ffn[:, :], a_ffn[:, :], col("g_pre_ffn"), ALU.mult))
            for tb in range(TB):
                hi_seen[0] += 1
                dve.wait_ge(sem("T_hi"), hi_seen[0])
                t = slice(tb * P, (tb + 1) * P)
                dve.tensor_tensor(hT_lo[:, 0:4, t], bank_of(("att", tb))[:, :].rearrange("p (a t) -> p a t", t=P),
                                  hT_hi[:, 0:4, t].bitcast(F32), ALU.subtract).then_inc(read_sem(("att", tb)), 1)
            dve.wait_ge(sem("ret_step"), HEADS)
            for tb in range(TB):
                b = bank_of(("ret", tb))
                chain(dve.reduce_sum(row_max[:, tb * 8:tb * 8 + 8], heads(b[:, :]), AX.X))
                chain(dve.tensor_scalar(row_max[:, tb * 8:tb * 8 + 8], row_max[:, tb * 8:tb * 8 + 8], -1.0 / HD, None, ALU.mult))
                ins = dve.tensor_tensor(heads(xn[:, tb, 512:1024]), heads(b[:, :]),
                                        heads_bc(row_max[:, tb * 8:tb * 8 + 8], HEADS, HD), ALU.add)
                ins.then_inc(sem("ret_centred"), 1)
            for tb in range(TB):
                dve.wait_ge(sem("ret_sq"), tb + 1)
                ins = dve.reduce_sum(head_ss[:, tb * 8:tb * 8 + 8], heads(probs[:, tb, :]), AX.X)
            ins.then_inc(sem("ret_var"), 1)
            dve.wait_ge(sem("ret_rms"), 1)
            chain(dve.reciprocal(head_rstd[:, :], head_rms[:, :]))
            for tb in range(TB):
                v = xn[:, tb, 512:1024]
                chain(dve.tensor_tensor(heads(v), heads(v), heads_bc(head_rstd[:, tb * 8:tb * 8 + 8], HEADS, HD), ALU.mult))
                dve.tensor_tensor(v, v, silu_gr[:, tb, :], ALU.mult).then_inc(read_sem(("ret", tb)), 1)
            split_T("mixT", n=2, first=4)

            def post_norm(y, name, last, g):
                dve.wait_ge(split_used, last + 1)
                for c in range(2):
                    dve.tensor_copy(y[:, 1, c * 512:(c + 1) * 512], bank_of((*name, 1, c))[:, :])\
                        .then_inc(read_sem((*name, 1, c)), 1)
                read_out(dve, (*name, 1, 0))
                read_out(dve, (*name, 1, 1))
                norm_stats(y, lambda e: None)
                for tb in range(TB):
                    ins = dve.scalar_tensor_tensor(out=y[:, tb, :], in0=y[:, tb, :], scalar=rstd[:, tb:tb + 1],
                                                   in1=rows[:, g, :], op0=ALU.mult, op1=ALU.mult)
                chain(ins)
                for tb in range(TB):
                    ins = dve.tensor_tensor(x[:, tb, :], x[:, tb, :], y[:, tb, :], ALU.add)
                ins.then_inc(sem("x_ready"), 1)

            junk[0] = xn[:, 1, :]

            def pre_norm(stage, ready, gain=None, shift=None):
                norm_stats(x, ready)
                norm_scale(x, xn)
                split_T(stage, gain, shift)

            def add_to_x(name, last, scale=None):
                dve.wait_ge(split_used, last + 1)
                for c in range(2):
                    for tb in range(TB):
                        key = (*name, tb, c)
                        xs = x[:, tb, c * 512:(c + 1) * 512]
                        dve.scalar_tensor_tensor(out=xs, in0=bank_of(key)[:, :], scalar=1.0 if scale is None else scale,
                                                 in1=xs, op0=ALU.mult, op1=ALU.add).then_inc(read_sem(key), 1)

            def ffn(f):
                silu0 = 2 * UP * f

                def gated(c, silus):
                    for tb in range(TB):
                        dve.wait_ge(sem("gate_silu"), silus + tb + 1)
                        b = (c % 3) * 2 + tb
                        dve.tensor_tensor(gate[:, c % 3, tb, :], gate[:, c % 3, tb, :], bank[b][:, 256:512], ALU.mult)\
                            .then_inc(bank_read[b], 1)

                def gate_lo(his, at):
                    dve.wait_ge(sem("gateT_hi"), his)
                    s = at if isinstance(at, slice) else bass.ds(at, 2)
                    dve.tensor_tensor(gT_lo[:, s, :], bank[6][:, :].rearrange("p (a t) -> p a t", t=T),
                                      gT_hi[:, s, :].bitcast(F32), ALU.subtract).then_inc(bank_read[6], 1)

                gated(0, silu0)
                gated(1, silu0 + 2)
                gate_lo(UP * f + 1, slice(0, 2))
                with dve.Fori(0, 3) as i:
                    for j in range(3):
                        c = 2 + j
                        gated(c, i * 6 + (silu0 + 2 * c))
                        gate_lo(i * 3 + (UP * f + c), i * 6 + 2 * (c - 1))
                gate_lo(UP * (f + 1), slice(2 * UP - 2, 2 * UP))

            post_norm(y_mix, ("mix_out",), W_OUT + 3, 0)
            pre_norm("ffn0T", x_ready(1), shift=(a_ffn, mod[:, 24:32, 0]))
            ffn(0)
            post_norm(y_ffn, ("down", 0), W_DN[0] + UP - 1, 1)
            pre_norm("ffn1T", x_ready(2), col("ffn1_norm"))
            ffn(1)
            add_to_x(("down", 1), W_DN[1] + UP - 1, 0.5)
            pre_norm("mix2T", x_added(("down", 1)), col("mix_norm"))

            dve.wait_ge(sem("lb_loaded"), 16)
            chain(dve.tensor_tensor(lb, lb_p[:, 0, :], lb_p[:, 1, :], ALU.max))
            dve.tensor_tensor(lb_p[:], lb_p[:], over_heads(lb, 2, 512), ALU.subtract).then_inc(sem("lb_diff"), 1)
            dve.wait_ge(sem("lb_exp"), 1)
            chain(dve.tensor_tensor(lb, lb_p[:, 0, :], lb_p[:, 1, :], ALU.add))
            chain(dve.reciprocal(lb, lb))
            chain(dve.tensor_tensor(lb, lb, lb_p[:, 0, :], ALU.mult))
            chain(dve.tensor_scalar(one_lb, lb, -1.0, 1.0, ALU.mult, ALU.add))
            chain(dve.memset(scT, 0.0))
            read_out(dve, ("zf", 1))
            chain(dve.tensor_tensor(fgate[:], fgate[:], over_heads(one_lb, TB, 512), ALU.mult))
            chain(dve.tensor_tensor(fgate[:], fgate[:], over_heads(lb, TB, 512), ALU.add))
            dve.tensor_scalar(hk[:], fgate[:], -1.0, 1.0, ALU.mult, ALU.add).then_inc(sem("fgate"), 1)
            dve.wait_ge(sem("logf_hi"), 1)
            dve.tensor_tensor(logf_lo[:], fgate[:], logf_hi[:].bitcast(F32), ALU.subtract).then_inc(sem("logf_lo"), 1)

            mask = lambda n: over_heads(level_mask[:, n, :], 4, P).bitcast(I32)
            sc = lambda blk: scT[:, blk * 512:(blk + 1) * 512].rearrange("p (h t) -> p h t", t=P)

            def keep_pairs(level, name):
                for blk in range(TB):
                    b = filled(dve, (*name, blk))
                    dve.copy_predicated(sc(blk), mask(level + 1), b[:, :].rearrange("p (h t) -> p h t", t=P))\
                        .then_inc(read_sem((*name, blk)), 1)

            def decayed(level):
                buf = qk_dec[level % 2]
                for late, other in ((1, hqT), (0, hkT)):
                    h = 1 << level
                    v = buf.rearrange("p (n two h) -> p n two h", two=2, h=h)[:, :, late, :] if level < LEVELS else \
                        buf[:, late * 512:late * 512 + 512]
                    o = other.rearrange("p (n two h) -> p n two h", two=2, h=h)[:, :, late, :] if level < LEVELS else \
                        other[:, late * 512:late * 512 + 512]
                    ins = dve.tensor_tensor(v, v, o, ALU.mult)
                ins.then_inc(sem("level_decayed"), 1)

            dve.wait_ge(sem("const2_loaded"), 16)
            read_out(dve, ("hkT", 0))
            read_out(dve, ("hkT", 1))
            keep_pairs(-1, ("diag",))
            for level in range(LEVELS + 1):
                read_out(dve, ("decay", level, 0))
                read_out(dve, ("decay", level, 1))
                decayed(level)
                if level:
                    keep_pairs(level - 1, ("pairs", level - 1))
                if level == 4:
                    dve.wait_ge(split_used, W_IN2 + 10)
                    read_out(dve, ("zc", 1))
                    for tb in range(TB):
                        dve.tensor_tensor(zc_sb[:, tb, :], zc_sb[:, tb, :], bank_of(("zu", tb))[:, :], ALU.mult)\
                            .then_inc(read_sem(("zu", tb)), 1)
            b = filled(dve, "cross")
            dve.tensor_copy(crossT, b[:, :]).then_inc(read_sem("cross"), 1)
            u3 = uT.rearrange("p (c t) -> p c t", t=T + 2)
            dve.memset(u3[:, :, 0:2], 0.0).then_inc(sem("u_pad"), 1)
            read_out(dve, "uT0")
            read_out(dve, "uT1")
            dve.wait_ge(sem("u_pad"), 1)
            taps = lambda c, j: col("conv_w", 3 * c + j, 3 * c + j + 1)
            for c in range(4):
                ins = dve.tensor_scalar(conv[:, c, :], u3[:, c, 2:T + 2], taps(c, 2), None, ALU.mult)
            chain(ins)
            for j in (1, 0):
                for c in range(4):
                    ins = dve.scalar_tensor_tensor(out=conv[:, c, :], in0=u3[:, c, j:T + j], scalar=taps(c, j),
                                                   in1=conv[:, c, :], op0=ALU.mult, op1=ALU.add)
                chain(ins)
            for j in range(2):
                b = filled(dve, f"bT{j}")
                dve.tensor_tensor(conv[:, 2 * j:2 * j + 2, :], conv[:, 2 * j:2 * j + 2, :],
                                  b[:, :].rearrange("p (c t) -> p c t", t=T), ALU.mult).then_inc(read_sem(f"bT{j}"), 1)
            for j in range(2):
                dve.wait_ge(sem("conv_hi"), j + 1)
                dve.tensor_tensor(hT_lo[:, 4 + 2 * j:6 + 2 * j, :], conv[:, 2 * j:2 * j + 2, :],
                                  hT_hi[:, 4 + 2 * j:6 + 2 * j, :].bitcast(F32), ALU.subtract).then_inc(sem("conv_lo"), 1)
            read_out(dve, ("zg", 1))
            dve.wait_ge(sem("head_row_loaded"), 16)
            chain(dve.tensor_tensor(silu_zg[:], silu_zg[:], over_heads(head_row, TB, 512), ALU.mult))
            for blk in range(TB):
                dve.wait_ge(sem("hgrn_sq"), blk + 1)
                dve.reduce_sum(head_ss[:, 4 * blk:4 * blk + 4], hgrn_sq.rearrange("p (h d) -> p h d", d=P), AX.X)\
                    .then_inc(sem("hgrn_ss"), 1)
            dve.wait_ge(sem("hgrn_rms"), 1)
            chain(dve.reciprocal(head_rstd[:, 0:8], head_rms[:, 0:8]))
            for blk in range(TB):
                b = bank_of(("hgrn", blk))
                v = xn[:, blk, 0:512]
                dve.tensor_tensor(v.rearrange("p (h d) -> p h d", d=P), b[:, :].rearrange("p (h d) -> p h d", d=P),
                                  heads_bc(head_rstd[:, 4 * blk:4 * blk + 4], 4, P), ALU.mult)\
                    .then_inc(read_sem(("hgrn", blk)), 1)
                read_out(dve, ("hgrn", blk))
                dve.tensor_tensor(v, v, silu_zg[:, blk, :], ALU.mult).then_inc(sem("hgrn_out"), 1)
            split_T("mix2oT", n=2)
            add_to_x(("mix2_out",), W_OUT2 + 3)
            pre_norm("xattT", x_added(("mix2_out",)), col("xattn_norm"))

            for h in range(MEM_HEADS):
                for tb in range(TB):
                    negative_max(TB * h + tb, ("mscores", h, tb), T, MEM_HD ** -0.5)
            for tb in range(TB):
                read_out(dve, ("mscores", MEM_HEADS - 1, tb))
            chain(dve.reciprocal(row_inv[:, 0:8], row_sum[:, 0:8]))
            inv = row_inv[:, 0:8].rearrange("p (h b) -> p h b", b=TB)
            for h2 in range(2):
                dve.wait_ge(sem("matt_step"), 2 * h2 + 2)
                for tb in range(TB):
                    b = bank_of(("matt", h2, tb))
                    dve.tensor_tensor(xn[:, tb, h2 * 512:(h2 + 1) * 512].rearrange("p (h d) -> p h d", d=MEM_HD),
                                      b[:, :].rearrange("p (h d) -> p h d", d=MEM_HD),
                                      heads_bc(inv[:, 2 * h2:2 * h2 + 2, tb], 2, MEM_HD), ALU.mult)\
                        .then_inc(read_sem(("matt", h2, tb)), 1)
            split_T("mattT")
            add_to_x(("mem_out",), W_O + 3)
            pre_norm("ffn2T", x_added(("mem_out",)), col("ffn2_norm"))
            ffn(2)
            add_to_x(("down", 2), W_DN[2] + UP - 1, 0.5)

            norm_stats(x, x_added(("down", 2)))
            dve.wait_ge(sem("final_loaded"), 16)
            for tb in range(TB):
                dve.scalar_tensor_tensor(out=xn[:, tb, :], in0=x[:, tb, :], scalar=rstd[:, tb:tb + 1], in1=rows[:, 0, :],
                                         op0=ALU.mult, op1=ALU.mult).then_inc(sem("out_ready"), 1)

        @block.tensor
        def _(pe):
            def three(out, hi, lo, rhi, rlo, start, stop):
                pe.matmul(out, hi, rhi, start=start, stop=False)
                pe.matmul(out, hi, rlo, start=False, stop=False)
                return pe.matmul(out, lo, rhi, start=False, stop=stop)

            def unit(v, ready, tiles, ks, n, first, last, slot=None):
                pe.wait_ge(split_ready, ready)
                s = v % RING
                for hi, lo, tb, out in tiles:
                    for e, k in enumerate(ks):
                        t = slice(tb * P, (tb + 1) * P)
                        w = slice(e * n, (e + 1) * n)
                        ins = three(out[:, 0:n], hi[:, k, t], lo[:, k, t], w_hi[:, s, w], w_lo[:, s, w],
                                    first and e == 0, last and e == len(ks) - 1)
                ins.then_inc(split_used, 1)

            def project(v, names, tiles=None, halves=(0, 1), ready=None):
                tiles = tiles or [(hT_hi, hT_lo, 0), (hT_hi, hT_lo, 1)]
                for n, half in enumerate(halves):
                    if ready:
                        ready(half)
                    if n == 0:
                        outs = [free(pe, name) for name in names]
                    unit(v + n, v + n + 1, [(*t, o) for t, o in zip(tiles, outs)], range(4 * half, 4 * half + 4), 512,
                         n == 0, n == 1)

            def input_ready(stage):
                return lambda half: [read_out(pe, (stage, 2 * half + e)) for e in range(2)]

            scaled = [0]

            def transpose_input(stage, src):
                scaled[0] += 1
                pe.wait_ge(sem("xn_a"), scaled[0])
                pe.wait_ge(sem("xn_v"), scaled[0])
                transposes(stage, src)

            def transposes(stage, src, n=4):
                for q in range(n):
                    b = free(pe, (stage, q))
                    for e in range(2):
                        for tb in range(TB):
                            ins = pe.transpose(b[:, e * T + tb * P:e * T + (tb + 1) * P],
                                               src[:, tb, (2 * q + e) * P:(2 * q + e + 1) * P], ident)
                    ins.then_inc(full_sem((stage, q)), 1)

            def mod_columns(name, c, accs, col0=0):
                b = bank_of(name)
                for e in range(4):
                    for cond, acc in enumerate(accs):
                        ins = pe.matmul(b[:, col0 + len(accs) * e + cond:col0 + len(accs) * e + cond + 1],
                                        acc[:, e * P:(e + 1) * P], ones[:, 0:1], start=True, stop=True)
                return ins

            def mod_columns_a(c):
                pe.wait_ge(mod_used, 2 * c + 2)
                mod_columns("mod_a", c, [acc_a[:, c % 2, cond, :] for cond in range(2)], 8 * c).then_inc(sem("mod_col"), 1)

            def mod_columns_b(c):
                pe.wait_ge(mod_used, 2 * c + 2)
                if c in MOD_STEPS:
                    free(pe, ("mod_col", c))
                    mod_columns(("mod_col", c), c, [acc_b[:, c % 2, :]]).then_inc(full_sem(("mod_col", c)), 1)
                else:
                    mod_columns("mod_b", c, [acc_b[:, c % 2, :]], 4 * (c - 4)).then_inc(sem("mod_col"), 1)

            pe.wait_ge(sem("fixed_loaded"), 16)
            transpose_input("memT", xn)
            for c in range(4):
                project(W_KV + 2 * c, [("kv", c, 0), ("kv", c, 1)], ready=input_ready("memT") if c == 0 else None)
                if c:
                    mod_columns_a(c - 1)
            read_out(pe, ("kv", 1, 0))
            read_out(pe, ("kv", 1, 1))
            transposes("keyT", mem_k)
            mod_columns_a(3)
            pe.wait_ge(sem("xn_a"), 3)
            pe.wait_ge(sem("xn_v"), 3)
            scaled[0] += 2

            def first_transposes(names):
                for stage, q in names:
                    b = free(pe, (stage, q))
                    for e in range(2):
                        for tb in range(TB):
                            ins = pe.transpose(b[:, e * T + tb * P:e * T + (tb + 1) * P],
                                               (xn if stage == "xT" else rows)[:, tb, (2 * q + e) * P:(2 * q + e + 1) * P], ident)
                    ins.then_inc(full_sem((stage, q)), 1)

            first_transposes(FIRST_T)

            both = [(hT_hi, hT_lo, 0), (hT_hi, hT_lo, 1), (hcT_hi, hcT_lo, 0), (hcT_hi, hcT_lo, 1)]
            j = 0
            for part, units, tiles in [("kr", 2, both), ("vr", 2, both), ("kava", 1, both), ("qa", 2, both[:2]),
                                       ("qr", 2, both[:2]), ("gr", 2, both[:2])]:
                for e in range(units):
                    if j < 2:
                        for stage in ("xT", "ctxT"):
                            for q in range(2):
                                read_out(pe, (stage, 2 * j + q))
                    if e == 0:
                        outs = [free(pe, (part, t)) for t in range(len(tiles))]
                    if j == 2:
                        free(pe, "mod_b")
                    if 3 <= j < 8:
                        mod_columns_b(MOD_A // 2 + j - 3)
                    ks, n = (range(4 * e, 4 * e + 4), 512) if units == 2 else (range(8), 256)
                    unit(W_IN + j, W_IN + j + 1, [(*t, o) for t, o in zip(tiles, outs)], ks, n, e == 0, e == units - 1)
                    j += 1
            mod_columns_b(MODS_IN - 1)

            pe.wait_ge(sem("kr_done"), 1)
            read_out(pe, ("vr", 3))
            b = free(pe, "states")
            for fb in range(2):
                for h in range(HEADS):
                    o = b[64 * (h % 2):64 * (h % 2) + 64, fb * 256 + (h // 2) * HD:fb * 256 + (h // 2 + 1) * HD]
                    for jb in range(TB):
                        ins = pe.matmul(o, k_fb[:, fb, jb, h * HD:(h + 1) * HD], vr[:, 2 + jb, h * HD:(h + 1) * HD],
                                        start=(jb == 0), stop=(jb == 1))
            ins.then_inc(full_sem("states"), 1)
            pe.wait_ge(sem("rope_done"), 8)
            transposes("krT", krn, 2)
            b = free(pe, ("kaT", 0))
            for tile in range(4):
                ins = pe.transpose(b[:, tile * P:(tile + 1) * P], ka_all[:, tile, :], ident)
            ins.then_inc(full_sem(("kaT", 0)), 1)
            transposes("qaT", qan, 2)
            transposes("qrT", qrn, 2)
            for name, n in (("krT", 2), ("kaT", 1), ("qaT", 2), ("qrT", 2)):
                for q in range(n):
                    read_out(pe, (name, q))

            pe.wait_ge(sem("keys_padded"), 1)

            def scores(s):
                h, tb = s // 2, s % 2
                j, kv = h % GROUP, h // GROUP
                b = free(pe, ("scores", s))
                pe.matmul(b[:, :], qaT[:, j, tb * P:(tb + 1) * P], kaT[:, kv, :],
                          start=True, stop=True).then_inc(full_sem(("scores", s)), 1)

            def weighted(s):
                h, tb = s // 2, s % 2
                kv = h // GROUP
                read_out(pe, ("probsT", s))
                j = h % GROUP
                b = free(pe, ("att", tb))
                for kb, tile in enumerate((2, 3, 0, 1)):
                    ins = pe.matmul(b[kv * HD:(kv + 1) * HD, j * P:(j + 1) * P], kava[:, tile, P + kv * HD:P + (kv + 1) * HD],
                                    probsT[:, s % 2, kb * P:(kb + 1) * P], start=(kb == 0), stop=(kb == 3))
                ins.then_inc(sem("att_step"), 1)

            def retained(r):
                read_out(pe, ("ret_scores", r))
                pe.wait_ge(sem("q_decayed"), 2 * (r // 2) + 2)
                read_out(pe, "states")
                for ib in range(TB):
                    o = free(pe, ("ret", ib))[:, r * HD:(r + 1) * HD]
                    for jb in range(TB):
                        pe.matmul(o, ret_p[:, r % 2, jb * T + ib * P:jb * T + (ib + 1) * P], vr[:, jb, r * HD:(r + 1) * HD],
                                  start=(jb == 0), stop=False)
                    for fb in range(2):
                        ins = pe.matmul(o, q_decayed[:, fb, ib * P:(ib + 1) * P], state[:, fb, r, :],
                                        start=False, stop=(fb == 1))
                ins.then_inc(sem("ret_step"), 1)

            scores(0)
            for s in range(2 * HEADS):
                if s + 1 < 2 * HEADS:
                    scores(s + 1)
                if s % 2 == 0:
                    r = s // 2
                    b = free(pe, ("ret_scores", r))
                    for jb in range(TB):
                        ins = pe.matmul(b[:, jb * T:(jb + 1) * T], krT[:, r, jb * P:(jb + 1) * P], qrT[:, r // 2, :],
                                        start=True, stop=True)
                    ins.then_inc(full_sem(("ret_scores", r)), 1)
                if s:
                    weighted(s - 1)
                pe.wait_ge(sem("probs_ready"), s + 1)
                b = free(pe, ("probsT", s))
                for kb in range(4):
                    ins = pe.transpose(b[:, kb * P:(kb + 1) * P], probs[:, s % 2, kb * P:(kb + 1) * P], ident)
                ins.then_inc(full_sem(("probsT", s)), 1)
                if s % 2 == 1:
                    retained(s // 2)
                for c, step in MOD_STEPS.items():
                    if step == s:
                        mod_columns_b(c)
            weighted(2 * HEADS - 1)
            read_out(pe, ("att", 0))
            read_out(pe, ("att", 1))

            def mix_out(half):
                for c in range(2):
                    v = W_OUT + 2 * half + c
                    outs = [(free(pe, ("mix_out", tb, c)) if half == 0 else bank_of(("mix_out", tb, c))) for tb in range(TB)]
                    unit(v, v + 1, [(hT_hi, hT_lo, tb, outs[tb]) for tb in range(TB)], range(4 * half, 4 * half + 4), 512,
                         half == 0, half == 1)

            mix_out(0)
            for q in range(4):
                if q % 2 == 0:
                    pe.wait_ge(sem("gain_diag"), q // 2 + 1)
                b = free(pe, ("gain_row", q))
                pe.matmul(b[:, :], ones, gain_diag[q // 2][:, (q % 2) * 512:(q % 2 + 1) * 512], start=True, stop=True)\
                    .then_inc(full_sem(("gain_row", q)), 1)

            for q in range(2):
                read_out(pe, ("ret", q))
            for q in range(2):
                b = free(pe, ("mixT", q))
                for e in range(2):
                    for tb in range(TB):
                        k = 4 + 2 * q + e
                        ins = pe.transpose(b[:, e * T + tb * P:e * T + (tb + 1) * P], xn[:, tb, k * P:(k + 1) * P], ident)
                ins.then_inc(full_sem(("mixT", q)), 1)
            for q in range(2):
                read_out(pe, ("mixT", q))
            mix_out(1)

            def ffn(f, stage):
                up, dn = W_UP[f], W_DN[f]

                def up_chunk(c, ready, frees, inputs=None):
                    for half in range(2):
                        if inputs:
                            inputs(half)
                        if half == 0:
                            for tb in range(TB):
                                pe.wait_ge(bank_read[(c % 3) * 2 + tb], frees[tb])
                        unit(up + 2 * c + half, ready + half + 1,
                             [(hT_hi, hT_lo, tb, bank[(c % 3) * 2 + tb]) for tb in range(TB)],
                             range(4 * half, 4 * half + 4), 512, half == 0, half == 1)

                def gate_T(c, reads, before):
                    for tb in range(TB):
                        pe.wait_ge(bank_read[(c % 3) * 2 + tb], reads[tb])
                    pe.wait_ge(bank_read[6], before)
                    for e in range(2):
                        for tb in range(TB):
                            ins = pe.transpose(bank[6][:, e * T + tb * P:e * T + (tb + 1) * P],
                                               gate[:, c % 3, tb, e * P:(e + 1) * P], ident)
                    ins.then_inc(bank_full[6], 1)

                fills = lambda c: [plan.of[("up", f, c, tb)][1] for tb in range(TB)]
                g0 = plan.of[("gateT", f, 0)][1]
                up_chunk(0, up, fills(0), input_ready(stage))
                up_chunk(1, up + 2, fills(1))
                gate_T(0, [n + 1 for n in fills(0)], g0)
                with pe.Fori(0, 3) as i:
                    for j in range(3):
                        c = 2 + j
                        up_chunk(c, i * 6 + (up + 2 * c), [i + n for n in fills(c)])
                        gate_T(c - 1, [i + (n + 1) for n in fills(c - 1)], i * 3 + (g0 + c - 1))

                def down(k):
                    pe.wait_ge(split_ready, dn + k + 1)
                    pe.wait_ge(bank_read[6], g0 + k + 1)
                    s = (dn + k) % RING
                    for tb in range(TB):
                        t = slice(tb * P, (tb + 1) * P)
                        for e in range(2):
                            for half in range(2):
                                o = free(pe, ("down", f, tb, half)) if k == 0 and e == 0 else bank_of(("down", f, tb, half))
                                w = slice(e * D + half * 512, e * D + half * 512 + 512)
                                ins = three(o[:, :], gT_hi[:, 2 * k + e, t], gT_lo[:, 2 * k + e, t], w_hi[:, s, w], w_lo[:, s, w],
                                            k == 0 and e == 0, k == UP - 1 and e == 1)
                    ins.then_inc(split_used, 1)

                down(0)
                gate_T(UP - 1, [n + 1 for n in fills(UP - 1)], g0 + UP - 1)
                for k in range(1, UP):
                    down(k)

            transpose_input("ffn0T", xn)
            ffn(0, "ffn0T")
            transpose_input("ffn1T", xn)
            ffn(1, "ffn1T")
            transpose_input("mix2T", xn)

            z = lambda k, part: project(W_IN2 + 2 * k, [(part, 0), (part, 1)], ready=input_ready("mix2T") if k == 0 else None)
            z(0, "zf")
            z(1, "zq")
            z(2, "zi")
            read_out(pe, ("zq", 1))
            pe.wait_ge(sem("fgate"), 1)
            for name, src in (("hqT", hq), ("hkT", hk)):
                for blk in range(TB):
                    b = free(pe, (name, blk))
                    for h in range(HG_HEADS):
                        ins = pe.transpose(b[:, h * P:(h + 1) * P], src[:, blk, h * P:(h + 1) * P], ident)
                    ins.then_inc(full_sem((name, blk)), 1)

            def decay_sums(level):
                for blk in range(TB):
                    b = free(pe, ("decay", level, blk))
                    m = sums_r[:, level + blk if level == LEVELS else level, :]
                    for h in range(HG_HEADS):
                        o = b[:, h * P:(h + 1) * P]
                        pe.matmul(o, logf_hi[:, blk, h * P:(h + 1) * P], m, start=True, stop=False)
                        ins = pe.matmul(o, logf_lo[:, blk, h * P:(h + 1) * P], m, start=False, stop=True)
                    ins.then_inc(full_sem(("decay", level, blk)), 1)

            def pair_scores(level):
                pe.wait_ge(sem("level_decayed"), level + 1)
                buf = qk_dec[level % 2]
                if level == LEVELS:
                    b = free(pe, "cross")
                    for h in range(HG_HEADS):
                        ins = pe.matmul(b[:, h * P:(h + 1) * P], buf[:, h * P:(h + 1) * P],
                                        buf[:, 512 + h * P:512 + (h + 1) * P], start=True, stop=True)
                    ins.then_inc(full_sem("cross"), 1)
                    return
                for blk in range(TB):
                    b = free(pe, ("pairs", level, blk))
                    for h in range(HG_HEADS):
                        v = buf[:, blk * 512 + h * P:blk * 512 + (h + 1) * P]
                        ins = pe.matmul(b[:, h * P:(h + 1) * P], v, v, start=True, stop=True)
                    ins.then_inc(full_sem(("pairs", level, blk)), 1)

            pe.wait_ge(sem("sums_ready"), 1)
            pe.wait_ge(sem("logf_lo"), 1)
            decay_sums(0)
            for name in ("hqT", "hkT"):
                for q in range(2):
                    read_out(pe, (name, q))
            for blk in range(TB):
                b = free(pe, ("diag", blk))
                for h in range(HG_HEADS):
                    s = slice(blk * 512 + h * P, blk * 512 + (h + 1) * P)
                    ins = pe.matmul(b[:, h * P:(h + 1) * P], hkT[:, s], hqT[:, s], start=True, stop=True)
                ins.then_inc(full_sem(("diag", blk)), 1)
            parts = ["zc", "zu", "zb", "zg"]
            for step in range(8):
                k, half = step // 2, step % 2
                v = W_IN2 + 6 + step
                if half == 0:
                    outs = [free(pe, (parts[k], tb)) for tb in range(TB)]
                unit(v, v + 1, [(hT_hi, hT_lo, tb, outs[tb]) for tb in range(TB)], range(4 * half, 4 * half + 4), 512,
                     half == 0, half == 1)
                if step < LEVELS:
                    decay_sums(step + 1)
                    pair_scores(step)
            pair_scores(LEVELS)
            read_out(pe, ("zu", 1))
            read_out(pe, ("zb", 1))
            for name, src in (("uT", zc_sb), ("bT", zb_sb)):
                for j in range(2):
                    b = free(pe, f"{name}{j}")
                    for e in range(2):
                        for tb in range(TB):
                            ins = pe.transpose(b[:, e * T + tb * P:e * T + (tb + 1) * P],
                                               src[:, tb, (2 * j + e) * P:(2 * j + e + 1) * P], ident)
                    ins.then_inc(full_sem(f"{name}{j}"), 1)
            read_out(pe, ("pairs", LEVELS - 1, 0))
            read_out(pe, ("pairs", LEVELS - 1, 1))
            read_out(pe, "cross")
            for blk in range(TB):
                b = free(pe, ("hgrn", blk))
                for h in range(HG_HEADS):
                    d = slice(h * P, (h + 1) * P)
                    ins = pe.matmul(b[:, d], scT[:, blk * 512 + h * P:blk * 512 + (h + 1) * P], hv[:, blk, d],
                                    start=True, stop=(blk == 0))
                    if blk:
                        ins = pe.matmul(b[:, d], crossT[:, d], hv[:, 0, d], start=False, stop=True)
                ins.then_inc(full_sem(("hgrn", blk)), 1)
            pe.wait_ge(sem("hgrn_out"), TB)
            transposes("mix2oT", xn, 2)

            def mix2_ready(half):
                if half == 1:
                    pe.wait_ge(sem("conv_lo"), 2)
                else:
                    read_out(pe, ("mix2oT", 0))
                    read_out(pe, ("mix2oT", 1))

            for c in range(2):
                project(W_OUT2 + 2 * c, [("mix2_out", tb, c) for tb in range(TB)], halves=(1, 0), ready=mix2_ready)

            transpose_input("xattT", xn)
            for c in range(2):
                project(W_Q + 2 * c, [("mq", tb, c) for tb in range(TB)], ready=input_ready("xattT") if c == 0 else None)
            for tb in range(TB):
                for c in range(2):
                    read_out(pe, ("mq", tb, c))
            transposes("mqT", mq)
            for q in range(4):
                read_out(pe, ("mqT", q))

            def mem_scores(h):
                for tb in range(TB):
                    b = free(pe, ("mscores", h, tb))
                    for e in range(2):
                        ins = pe.matmul(b[:, 0:T], mqT[:, 2 * h + e, tb * P:(tb + 1) * P], memKT[:, 2 * h + e, :],
                                        start=(e == 0), stop=(e == 1))
                    ins.then_inc(full_sem(("mscores", h, tb)), 1)

            def mem_weighted(h):
                read_out(pe, ("mprobsT", h))
                for tb in range(TB):
                    b = free(pe, ("matt", h // 2, tb))
                    for mb in range(TB):
                        ins = pe.matmul(b[:, (h % 2) * MEM_HD:(h % 2 + 1) * MEM_HD],
                                        mprobsT[:, h % 2, (mb * TB + tb) * P:(mb * TB + tb + 1) * P],
                                        memV[:, mb, h * MEM_HD:(h + 1) * MEM_HD], start=(mb == 0), stop=(mb == 1))
                ins.then_inc(sem("matt_step"), 1)

            mem_scores(0)
            for h in range(MEM_HEADS):
                if h + 1 < MEM_HEADS:
                    mem_scores(h + 1)
                if h:
                    mem_weighted(h - 1)
                for tb in range(TB):
                    read_out(pe, ("mscores", h, tb))
                b = free(pe, ("mprobsT", h))
                for mb in range(TB):
                    for tb in range(TB):
                        ins = pe.transpose(b[:, (mb * TB + tb) * P:(mb * TB + tb + 1) * P], mprobs[:, tb, mb * P:(mb + 1) * P],
                                           ident)
                ins.then_inc(full_sem(("mprobsT", h)), 1)
            mem_weighted(MEM_HEADS - 1)
            for half in range(2):
                for tb in range(TB):
                    read_out(pe, ("matt", half, tb))
            transposes("mattT", xn)
            for c in range(2):
                project(W_O + 2 * c, [("mem_out", tb, c) for tb in range(TB)], ready=input_ready("mattT") if c == 0 else None)
            transpose_input("ffn2T", xn)
            ffn(2, "ffn2T")



def lay_out(a):
    f = lambda name: np.asarray(a[name])
    halves = lambda w: [w[512 * h:512 * h + 512].reshape(4, P, -1).transpose(1, 0, 2).reshape(P, UNIT) for h in range(2)]
    whole = lambda w: w.reshape(KC, P, 256).transpose(1, 0, 2).reshape(P, UNIT)

    def project(w, halves_order=(0, 1)):
        return [halves(w[:, c:c + 512])[h] for c in range(0, w.shape[1], 512) for h in halves_order]

    def swiglu(gate, up, down):
        out = []
        for c in range(0, FFN, 256):
            out += halves(np.concatenate([gate[:, c:c + 256], up[:, c:c + 256]], axis=1))
        return out + [down[r:r + 256].reshape(2, P, D).transpose(1, 0, 2).reshape(P, UNIT) for r in range(0, FFN, 256)]

    w_in, w_in2 = f("w_in")[0], f("w_in_2")[0]
    cut = lambda w, at: w[:, at:at + 512]
    kr, vr, qa, qr, gr = (cut(w_in, at) for at in (1280, 1792, 0, 768, 2304))
    w = project(f("w_kv_mem_2")[0])
    w += project(kr) + project(vr) + [whole(w_in[:, 512:768])] + project(qa) + project(qr) + project(gr)
    w_out = f("w_out")[0]
    w_out = np.concatenate([w_out[:512].reshape(KV_HEADS, GROUP, HD, D).transpose(1, 0, 2, 3).reshape(512, D), w_out[512:]])
    w += [halves(w_out[:, c:c + 512])[h] for h in range(2) for c in range(0, D, 512)]
    w += swiglu(f("w_ffn_in")[0][:, :FFN], f("w_ffn_in")[0][:, FFN:], f("w_ffn_out")[0])
    w += swiglu(f("ffn1_gate_2")[0], f("ffn1_up_2")[0], f("ffn1_down_2")[0])
    for at in (512, 0, 1024, 2560, 3072, 2048, 1536):
        w += project(cut(w_in2, at))
    w += project(f("w_out_2")[0], (1, 0)) + project(f("w_q_mem_2")[0]) + project(f("w_o_mem_2")[0])
    w += swiglu(f("ffn2_gate_2")[0], f("ffn2_up_2")[0], f("ffn2_down_2")[0])
    mods = project(f("w_mod")[0])
    units = {"w": w, "mod": mods}

    col = lambda v: v.reshape(-1, P).T
    everywhere = lambda v: np.broadcast_to(v.reshape(1, -1), (P, v.size))
    decay = np.stack([f("ret_decay_fwd")[0], f("ret_decay_bwd")[0]])
    pairs = np.concatenate([np.repeat(decay[:, e::2].reshape(1, -1), HD, axis=0) for e in range(2)], axis=0)
    small = {name: col(f(src)) for name, src in [
        ("g_pre_mix", "g_pre_mix"), ("g_post_mix", "g_post_mix"), ("g_pre_ffn", "g_pre_ffn"),
        ("g_post_ffn", "g_post_ffn"), ("b_mod", "b_mod"), ("ffn1_norm", "ffn1_norm_2"), ("mix_norm", "mix_norm_2"),
        ("xattn_norm", "xattn_norm_2"), ("mem_norm", "mem_norm_2"), ("ffn2_norm", "ffn2_norm_2")]}
    small["conv_w"] = f("conv_w_2")[0].reshape(4, P, 3).transpose(1, 0, 2).reshape(P, 12)
    small["cond"] = np.stack([f("c")[0], f("c_ctx")], axis=1).reshape(KC, P, 2).transpose(1, 0, 2).reshape(P, 16)
    small["decay_rows"] = everywhere(decay)
    small["decay_pairs"] = pairs
    small["qk_gain"] = everywhere(np.concatenate([f("q_norm_g")[0], f("k_norm_g")[0]]))
    tiles = lambda v: v[0].reshape(TB, P, D).transpose(1, 0, 2)
    fixed, const1, const2 = shape_constants()
    out = {
        "weights": np.stack([units[kind][n] for kind, n in STREAM]),
        "cols": np.concatenate([small[name] for name in COLS], axis=1),
        "x": tiles(f("x")), "ctx": tiles(f("ctx")), "mem": tiles(f("mem_2")),
        "fixed": fixed, "const1": const1, "const2": const2,
        "lb_param": f("lb_param_2").reshape(1, D), "hgrn_out_norm": f("hgrn_out_norm_2").reshape(1, 512),
        "final_norm": f("final_norm_2").reshape(1, D),
    }
    return {name: np.ascontiguousarray(v) for name, v in out.items()}


def kernel(**inputs):
    import concourse.bacc as _bacc
    from concourse.bass_utils import run_bass_kernel_spmd as _run

    nc = _bacc.Bacc("TRN2", target_bir_lowering=False, num_devices=1)
    arrays = {f"in_{name}": v for name, v in lay_out(inputs).items()}
    io = {name[3:]: nc.dram_tensor(name, v.shape, mybir.dt.from_np(v.dtype), kind="ExternalInput").ap()
          for name, v in arrays.items()}
    out = nc.dram_tensor("out", (T, D), F32, kind="ExternalOutput").ap()
    io["out"] = out.rearrange("(b p) d -> b p d", p=P)
    two_blocks_kernel(nc, io)
    r = _run(nc, [arrays], core_ids=[0])
    return r.results[0]["out"].reshape(1, T, D)
```

```python
from contextlib import ExitStack

import numpy as np

import concourse.bass as bass
from concourse import mybir

F32 = mybir.dt.float32
F32R = mybir.dt.float32r
I32 = mybir.dt.int32
ALU = mybir.AluOpType
ACT = mybir.ActivationFunctionType
AX = mybir.AxisListType

P = 128
T = 256
TB = T // P
D = 1024
KC = D // P
HD = 64
HEADS = 8
KV_HEADS = 2
GROUP = HEADS // KV_HEADS
PAIRS = HEADS // 2
FFN = 2816
UP = FFN // 256
HG_HEADS = 4
MEM_HEADS = 4
MEM_HD = D // MEM_HEADS
EPS = 1e-6
UNIT = 2048
RING = 3
LEVELS = 7

W_KV = 0
W_IN = W_KV + 8
W_OUT = W_IN + 11
W_UP = [W_OUT + 4, 0, 0]
W_DN = [W_UP[0] + 2 * UP, 0, 0]
W_UP[1] = W_DN[0] + UP
W_DN[1] = W_UP[1] + 2 * UP
W_IN2 = W_DN[1] + UP
W_OUT2 = W_IN2 + 14
W_Q = W_OUT2 + 4
W_O = W_Q + 4
W_UP[2] = W_O + 4
W_DN[2] = W_UP[2] + 2 * UP
N_W = W_DN[2] + UP
N_MOD = 24
MOD_A = 8

STREAM = [("w", W_KV)]
for _v in range(W_KV + 1, W_IN):
    STREAM += [("w", _v), ("mod", _v - W_KV - 1)]
STREAM.append(("mod", MOD_A - 1))
IN_MODS = [0, 2, 2, 2, 2, 0, 0, 0, 0, 0, 0]
_m = MOD_A
for _j in range(11):
    STREAM.append(("w", W_IN + _j))
    for _ in range(IN_MODS[_j]):
        STREAM.append(("mod", _m))
        _m += 1
LATE_MODS = 4
STREAM += [("mod", m) for m in range(_m, N_MOD - LATE_MODS)]
STREAM += [("w", W_OUT), ("w", W_OUT + 1), ("mod", N_MOD - 4), ("mod", N_MOD - 3), ("w", W_OUT + 2),
           ("mod", N_MOD - 2), ("mod", N_MOD - 1)]
W_REG = W_OUT + RING
STREAM += [("w", v) for v in range(W_REG, N_W)]
HEAD_UNITS = W_REG + N_MOD
RAW_AT = {unit: u for u, unit in enumerate(STREAM)}

MODS_IN = (MOD_A + sum(IN_MODS)) // 2
MOD_STEPS = {MODS_IN: 6, MODS_IN + 1: 12}
WEIGH_STEPS = {2: 2 * MODS_IN, 4: 2 * MODS_IN + 1, 8: 2 * MODS_IN + 2, 10: 2 * MODS_IN + 3}
UNIT_STEPS = {5: 9, 11: 10}
SPLIT_STEPS = {0: W_IN + 10, 15: W_OUT}
QR_STEP, GR_STEP = 6, 13
WEIGH_HEADS = {2: N_MOD - 4, 3: N_MOD - 3, 5: N_MOD - 2, 6: N_MOD - 1}

COLS = {}
_at = 0
for _name, _n in [("g_pre_mix", 8), ("g_post_mix", 8), ("g_pre_ffn", 8), ("g_post_ffn", 8), ("b_mod", 48),
                  ("ffn1_norm", 8), ("mix_norm", 8), ("xattn_norm", 8), ("mem_norm", 8), ("ffn2_norm", 8),
                  ("conv_w", 12), ("cond", 16), ("decay_rows", 16), ("decay_pairs", 8), ("qk_gain", 128)]:
    COLS[_name] = (_at, _at + _n)
    _at += _n
N_COLS = _at

CONST1 = {}
_at = 0
for _name, _n in [("fwd_dist", 384), ("bwd_dist", 384), ("from_start", T), ("to_end", T), ("ctx_dist", 4),
                  ("rope_cos", TB * HD), ("rope_sin", TB * HD)]:
    CONST1[_name] = (_at, _at + _n)
    _at += _n
N_CONST1 = _at


def shape_constants():
    i = np.arange(P, dtype=np.float32)
    ident = np.eye(P, dtype=np.float32)
    fixed = np.concatenate([ident, np.ones((P, P), np.float32)], axis=1)

    diff = i[None, :] - i[:, None]
    zero = np.zeros((P, P), np.float32)
    fwd = np.concatenate([zero, np.maximum(diff, 0), P + diff], axis=1)
    bwd = np.concatenate([P - diff, np.maximum(-diff, 0), zero], axis=1)
    t = np.arange(T, dtype=np.float32)
    rows = lambda a: np.broadcast_to(a, (P, a.shape[-1]))
    ctx_dist = np.stack([T - 1 - i, T - 1 - (i + P), i, i + P], axis=1)
    inv = (10000.0 ** (-np.arange(HD // 4, dtype=np.float32) / (HD // 4))).astype(np.float32)
    row, col = np.floor(t / 64), t % 64
    ang = np.concatenate([row[:, None] * inv, col[:, None] * inv], axis=1).astype(np.float32)
    cos, sin = np.cos(ang), np.sin(ang)
    tiles = lambda a: a.reshape(TB, P, HD).transpose(1, 0, 2).reshape(P, TB * HD)
    first = np.concatenate([fwd, bwd, rows(t + 1), rows(T - t), ctx_dist,
                            tiles(np.concatenate([cos, cos], 1)), tiles(np.concatenate([-sin, sin], 1))], axis=1)

    sums, masks = [], [ident]
    src, dst = np.arange(P)[:, None], np.arange(P)[None, :]
    for level in range(LEVELS):
        h = 1 << level
        seg_s, seg_t = src // (2 * h), dst // (2 * h)
        late_s, late_t = (src // h) % 2 == 1, (dst // h) % 2 == 1
        same = seg_s == seg_t
        sums.append(same & ((late_t & late_s & (src <= dst)) | (~late_t & ~late_s & (src > dst))))
        masks.append(same & ~late_s & late_t)
    sums += [src > dst, src <= dst]
    second = np.concatenate([m.astype(np.float32) for m in sums + masks], axis=1)
    return [np.ascontiguousarray(a, dtype=np.float32) for a in (fixed, first, second)]


class BankPlan:

    def __init__(self):
        self.fills = [0] * 8
        self.signals = [0] * 8
        self.of = {}

    def streamed(self, name, bank):
        self.of[name] = (bank, self.fills[bank], None)
        self.fills[bank] += 1

    def signalled(self, name, bank):
        self.of[name] = (bank, self.fills[bank], self.signals[bank])
        self.fills[bank] += 1
        self.signals[bank] += 1


FIRST_T = [(stage, 2 * half + e) for half in range(2) for stage in ("xT", "ctxT") for e in range(2)]


def plan_banks():
    plan = BankPlan()

    def transposes(stage, n):
        for q in range(n):
            plan.signalled((stage, q), 5 + q % 2)

    def ffn(f):
        for c in range(UP):
            for tb in range(TB):
                plan.streamed(("up", f, c, tb), (c % 3) * 2 + tb)
        for c in range(UP):
            plan.signalled(("gateT", f, c), 6)
        for tb in range(TB):
            for half in range(2):
                plan.streamed(("down", f, tb, half), tb * 2 + half)

    def four_transposes(stage):
        for q in range(4):
            plan.signalled((stage, q), 4 + q)

    four_transposes("memT")
    for c in range(4):
        for tb in range(TB):
            plan.streamed(("kv", c, tb), (c % 2) * 2 + tb)
    plan.streamed("mod_a", 7)
    transposes("keyT", 4)
    for n, name in enumerate(FIRST_T):
        plan.signalled(name, 4 + n % 4)
    for part, banks in [("kr", [0, 1, 2, 3]), ("vr", [4, 5, 6, 0]), ("kava", [1, 2, 3, 4]),
                        ("qa", [5, 6]), ("qr", [0, 1])]:
        for tile, bank in enumerate(banks):
            plan.streamed((part, tile), bank)
    plan.streamed("mod_b", 7)
    plan.signalled("states", 4)
    transposes("krT", 2)
    transposes("kaT", 1)
    transposes("qaT", 2)
    for s in range(2 * HEADS):
        plan.signalled(("scores", s), s % 2)
        if UNIT_STEPS.get(s) == 9:
            for tb in range(TB):
                plan.streamed(("gr", tb), 6 + tb)
        plan.signalled(("probsT", s), 2)
        for c, step in MOD_STEPS.items():
            if step == s:
                plan.signalled(("mod_col", c), 3)
    for q in range(2):
        plan.signalled(("qrT", q), 3)
    plan.streamed(("att", 0), 4)
    plan.streamed(("att", 1), 5)
    plan.streamed(("ret", 0), 6)
    plan.streamed(("ret", 1), 7)
    for r in range(HEADS):
        plan.signalled(("ret_scores", r), 1 + 2 * (r % 2))
    plan.signalled(("mod_col", N_MOD // 2 - 2), 4)
    plan.signalled(("mod_col", N_MOD // 2 - 1), 5)
    for c in range(2):
        for tb in range(TB):
            plan.streamed(("mix_out", tb, c), tb * 2 + c)
    for q in range(4):
        plan.signalled(("gain_row", q), 4 + q % 2)
    for q in range(2):
        plan.signalled(("mixT", q), 6 + q)
    four_transposes("ffn0T")
    ffn(0)
    four_transposes("ffn1T")
    ffn(1)
    four_transposes("mix2T")
    for part, banks in [("zf", [0, 1]), ("zq", [2, 3]), ("zi", [0, 1]), ("zc", [2, 3]), ("zu", [0, 1]),
                        ("zb", [2, 3]), ("zg", [0, 1])]:
        for tb, bank in enumerate(banks):
            plan.streamed((part, tb), bank)
    transposes("hqT", 2)
    transposes("hkT", 2)
    for blk in range(TB):
        plan.signalled(("diag", blk), 5 + blk)
    for level in range(LEVELS):
        for blk in range(TB):
            plan.signalled(("decay", level, blk), [4, 7][blk])
            plan.signalled(("pairs", level, blk), 5 + blk)
        for step, name in ((LEVELS - 2, "uT"), (LEVELS - 1, "bT")):
            if level == step:
                plan.signalled(f"{name}0", 6)
                plan.signalled(f"{name}1", 5)
    for blk in range(TB):
        plan.signalled(("decay", LEVELS, blk), [4, 7][blk])
    plan.signalled("cross", 5)
    for blk in range(TB):
        plan.signalled(("hgrn", blk), [4, 7][blk])
    plan.signalled(("mix2oT", 0), 6)
    plan.signalled(("mix2oT", 1), 5)
    for c in range(2):
        for tb in range(TB):
            plan.streamed(("mix2_out", tb, c), tb * 2 + c)
    four_transposes("xattT")
    for c in range(2):
        for tb in range(TB):
            plan.streamed(("mq", tb, c), tb * 2 + c)
    transposes("mqT", 4)
    for h in range(MEM_HEADS):
        for tb in range(TB):
            plan.signalled(("mscores", h, tb), [4, 7][tb])
        plan.signalled(("mprobsT", h), 5 + h % 2)
    for half in range(2):
        for tb in range(TB):
            plan.streamed(("matt", half, tb), tb * 2 + half)
    transposes("mattT", 4)
    for c in range(2):
        for tb in range(TB):
            plan.streamed(("mem_out", tb, c), tb * 2 + c)
    four_transposes("ffn2T")
    ffn(2)
    return plan


def two_blocks_kernel(nc, io):
    plan = plan_banks()
    sems = ExitStack()
    stack = ExitStack()
    named = {}

    def sem(name):
        if name not in named:
            named[name] = sems.enter_context(nc.semaphore(name))
        return named[name]

    with sems, stack:
        def sb(name, shape, dt=F32):
            return stack.enter_context(nc.sbuf_tensor(name, shape, dt))

        raw = sb("raw", [P, RING, UNIT])
        w_hi = sb("w_hi", [P, RING, UNIT], F32R)
        w_lo = sb("w_lo", [P, RING, UNIT], F32R)
        x = sb("x_res", [P, TB, D])
        hT_hi = sb("hT_hi", [P, KC, T], F32R)
        hT_lo = sb("hT_lo", [P, KC, T], F32R)
        xn = sb("xn", [P, TB, D])
        rows = sb("rows", [P, TB, D])
        memKT = sb("memKT", [P, KC, T])
        memV = sb("memV", [P, TB, D])
        fixed = sb("fixed", [P, 2 * P])
        cols = sb("cols", [P, N_COLS])
        eps = sb("eps", [P, 1])
        ssq = sb("ssq", [P, 2])
        warm = sb("warm", [P, 8])
        half_ss = sb("half_ss", [P, 2, TB])
        half_mean = sb("half_mean", [P, TB])
        rms = sb("rms", [P, 2])
        rstd = sb("rstd", [P, 2])
        rstd_mem = sb("rstd_mem", [P, 2])
        silu_c = sb("silu_c", [P, KC, 2])
        mod = sb("mod", [P, 48, 2])
        a_mix = sb("a_mix", [P, KC, 2])
        a_ffn = sb("a_ffn", [P, KC])
        gain_col = sb("gain_col", [P, 2, KC])
        shifted_T = sb("shifted_T", [P, 2, 2 * T])
        ident = fixed[:, 0:P]
        ones = fixed[:, P:2 * P]

        def col(name, a=0, b=None):
            lo, hi = COLS[name]
            return cols[:, lo + a:(lo + b if b is not None else hi)]

        ARENA = 18440
        spot = ExitStack()
        hcT_hi = spot.enter_context(nc.sbuf_tensor("hcT_hi", [P, KC, T], F32R))
        hcT_lo = spot.enter_context(nc.sbuf_tensor("hcT_lo", [P, KC, T], F32R))
        spot.close()
        gT_hi = spot.enter_context(nc.sbuf_tensor("gT_hi", [P, 2 * UP, T], F32R))
        gT_lo = spot.enter_context(nc.sbuf_tensor("gT_lo", [P, 2 * UP, T], F32R))
        spot.close()
        logf_hi = spot.enter_context(nc.sbuf_tensor("logf_hi", [P, TB, 512], F32R))
        logf_lo = spot.enter_context(nc.sbuf_tensor("logf_lo", [P, TB, 512], F32R))
        sums_r = spot.enter_context(nc.sbuf_tensor("sums_r", [P, LEVELS + 2, P], F32R))
        spot.close()
        arena = sb("arena", [P, ARENA])

        def carve(start, *shape):
            n = int(np.prod(shape))
            assert start + n <= ARENA, (start, n)
            v = arena[:, start:start + n]
            if len(shape) == 2:
                return v.rearrange("p (a b) -> p a b", b=shape[1])
            if len(shape) == 3:
                return v.rearrange("p (a b c) -> p a b c", b=shape[1], c=shape[2])
            return v

        at = 4096
        qaT, kaT = carve(0, PAIRS, T), carve(1024, KV_HEADS, 4 * P)
        qrT = carve(2048, PAIRS, T)
        krT = xn[:].rearrange("p b d -> p (b d)").rearrange("p (h t) -> p h t", t=T)
        acc_a = carve(0, 2, 2, 512)
        const1 = carve(at, N_CONST1); at += N_CONST1
        vr = carve(at, 4, 512); ctx_in = carve(at, TB, D); at += 2048
        kava = carve(at, 4, 256); at += 1024
        staged = carve(at, 4, 512); mem_in = carve(at, TB, D)
        decay_arg, decay_mat = carve(at, 384), carve(at + 384, 384)
        decay_mats = [decay_mat]
        q_dec = carve(at + 768, 2, T); q_decayed = carve(at + 1280, 2, T); at += 2048
        krn = carve(at, TB, 512); y_mix = carve(at, TB, D); at += 1024
        qrn = carve(at, TB, 512); at += 1024
        qan = carve(at, TB, 512); at += 1024
        k_fb = carve(at, 2, TB, 512); mem_k = carve(at, TB, D)
        ret_p, probs = carve(at, 2, 2 * T), carve(at + 1024, 2, 512); at += 2048
        gain_diag = [ret_p.rearrange("p a n -> p (a n)"), qan.rearrange("p a n -> p (a n)")]
        decay_mats.append(probs[:, 0, 0:384])
        rope_a, rope_b = carve(at, 512), carve(at + 512, 512); probsT = carve(at, 2, 4 * P); at += 1024
        silu_gr = carve(at, TB, 512); tables = carve(at, 4, TB * HD); at += 1024
        ka_all = carve(at, 4, P); at += 512
        state = shifted_T[:].rearrange("p a (h c) -> p a h c", c=HD)
        ctx_decay = sb("ctx_decay", [P, 4, HEADS])
        lg_rows = sb("lg_rows", [P, 16])
        lg_pairs = sb("lg_pairs", [P, 8])
        head_ss = sb("head_ss", [P, 16])
        head_rms = sb("head_rms", [P, 16])
        head_rstd = sb("head_rstd", [P, 16])
        row_max = sb("row_max", [P, 16])
        row_sum = sb("row_sum", [P, 16])
        row_inv = sb("row_inv", [P, 16])

        def c1(name, a=0, b=None):
            lo, hi = CONST1[name]
            return const1[:, lo + a:(lo + b if b is not None else hi)]

        gate = carve(2 * 2 * UP * T, 3, TB, 256)
        y_ffn = carve(2 * 2 * UP * T + 3 * TB * 256, TB, D)

        at = 2048 + (LEVELS + 2) * P
        const2 = carve(at, (2 * LEVELS + 3) * P); at += (2 * LEVELS + 3) * P
        fgate = carve(at, TB, 512); at += 1024
        hk = carve(at, TB, 512); uT = carve(at, 4 * (T + 2)); at += 1032
        hq = carve(at, TB, 512); conv = carve(at, 4, T); at += 1024
        hv = carve(at, TB, 512); at += 1024
        zc_sb = carve(at, TB, 512); at += 1024
        zb_sb = carve(at, TB, 512); at += 1024
        silu_zg = carve(at, TB, 512); at += 1024
        hkT, hqT = carve(at, 8 * P), carve(at + 1024, 8 * P); at += 2048
        scT = carve(at, 8 * P); at += 1024
        crossT = carve(at, 4 * P); at += 512
        head_row = rows[:, 1, 0:512]
        lb_p = carve(at, 2, 512); lb = carve(at + 1024, 512); one_lb = carve(at + 1536, 512); at += 2048
        hgrn_sq = lb_p[:, 0, :]
        level_mask = const2[:, (LEVELS + 2) * P:].rearrange("p (l t) -> p l t", t=P)
        qk_dec = [xn[:, b, :] for b in range(2)]

        mq = carve(0, TB, D)
        mqT = carve(2048, KC, T)
        mprobs = carve(4096, 2, T)
        mprobsT = carve(4608, 2, 4 * P)

        bank = [stack.enter_context(nc.psum_tensor(f"bank{b}", [P, 512], F32)) for b in range(8)]
        bank_full = [sem(f"bank{b}_full") for b in range(8)]
        bank_read = [sem(f"bank{b}_read") for b in range(8)]
        raw_ready = [sem(f"raw_ready{s}") for s in range(RING)]
        mod_used = sem("mod_used")
        hi_ready = sem("hi_ready")
        split_ready = sem("split_ready")
        split_used = sem("split_used")

        def free(eng, name):
            b, k, _ = plan.of[name]
            if k:
                eng.wait_ge(bank_read[b], k)
            return bank[b]

        def filled(eng, name):
            b, _, s = plan.of[name]
            eng.wait_ge(bank_full[b], s + 1)
            return bank[b]

        def read_out(eng, name):
            b, k, _ = plan.of[name]
            eng.wait_ge(bank_read[b], k + 1)

        def bank_of(name):
            return bank[plan.of[name][0]]

        def full_sem(name):
            return bank_full[plan.of[name][0]]

        def read_sem(name):
            return bank_read[plan.of[name][0]]

        def raw_free(sp, u):
            kind, n = STREAM[u - RING]
            if kind == "w":
                sp.wait_ge(split_ready, n + 1)
            else:
                sp.wait_ge(mod_used, n + 1)

        acc_b = rows[:, 0, :].rearrange("p (a n) -> p a n", n=512)

        def heads_bc(ap, n, d):
            return ap.unsqueeze(2).to_broadcast([P, n, d])

        def over_heads(ap, n, d):
            return ap.unsqueeze(1).to_broadcast([P, n, d])

        def product_done(eng, name, c):
            if name[0] == "down" and c == 0:
                eng.wait_ge(sem("down_half"), name[1] + 1)
                return
            last = {"mix_out": W_OUT + 2, "mix2_out": W_OUT2 + 2, "mem_out": W_O + 1}
            step = {"mix_out": 1, "mix2_out": 1, "mem_out": 2}
            unit = W_DN[name[1]] + UP - 1 if name[0] == "down" else last[name[0]] + step[name[0]] * c
            eng.wait_ge(split_used, unit + 1)

        def x_added(name, tb):
            return lambda eng: [read_out(eng, (*name, tb, c)) for c in range(2)]

        shift_buf = lambda k: shifted_T[:, k % 2, :].rearrange("p (a t) -> p a t", t=T)

        block = stack.enter_context(nc.Block())

        @block.sync
        def _(sp):
            small = [(fixed[:], io["fixed"], "fixed_loaded"), (cols[:], io["cols"], "cols_loaded"),
                     (mem_in, io["mem"], "mem_loaded")]
            for u in range(HEAD_UNITS):
                if u == 1:
                    for dst, src, name in small:
                        sp.dma_start(dst, src).then_inc(sem(name), 16)
                if u >= RING:
                    raw_free(sp, u)
                sp.dma_start(raw[:, u % RING, :], io["weights"][u]).then_inc(raw_ready[u % RING], 16)
                for at_unit, dst, src, name in [(4, x[:], io["x"], "x_loaded"), (7, ctx_in, io["ctx"], "ctx_loaded"),
                                                (9, const1, io["const1"], "const1_loaded")]:
                    if u == at_unit:
                        sp.dma_start(dst, src).then_inc(sem(name), 16)
            first = len(STREAM) - HEAD_UNITS
            for u in range(HEAD_UNITS, HEAD_UNITS + RING):
                raw_free(sp, u)
                sp.dma_start(raw[:, u % RING, :], io["weights"][u]).then_inc(raw_ready[u % RING], 16)
            assert first % RING == 0
            with sp.Fori(0, first // RING - 1) as i:
                for j in range(RING):
                    u0 = HEAD_UNITS + RING + j
                    sp.wait_ge(split_ready, i * RING + (W_REG + j + 1))
                    sp.dma_start(raw[:, u0 % RING, :], io["weights"][bass.ds(i * RING + u0, 1)].rearrange("a p n -> (a p) n"))\
                        .then_inc(raw_ready[u0 % RING], 16)
            for tb in range(TB):
                sp.wait_ge(sem("out_ready"), tb + 1)
                sp.dma_start(io["out"][tb], xn[:, tb, :]).then_inc(sem("stored"), 16)
            sp.wait_ge(sem("stored"), 16 * TB)

        @block.gpsimd
        def _(pool):
            def low_part(v_slot, u_slot, count):
                pool.wait_ge(hi_ready, count)
                pool.tensor_tensor(w_lo[:, v_slot, :], raw[:, u_slot, :], w_hi[:, v_slot, :].bitcast(F32),
                                   ALU.subtract).then_inc(split_ready, 1)

            for v in range(W_REG):
                low_part(v % RING, RAW_AT[("w", v)] % RING, v + 1)
            with pool.Fori(0, (N_W - W_REG) // RING) as i:
                for j in range(RING):
                    v0 = W_REG + j
                    low_part(v0 % RING, RAW_AT[("w", v0)] % RING, i * RING + (v0 + 1))

        @block.scalar
        def _(act):
            def high_part(v_slot, u_slot, loads, used, waits=True):
                act.wait_ge(raw_ready[u_slot], loads)
                if waits:
                    act.wait_ge(split_used, used)
                act.activation(w_hi[:, v_slot, :], raw[:, u_slot, :], ACT.Copy).then_inc(hi_ready, 1)

            split = [0]

            def split_to(n):
                while split[0] < min(n, N_W):
                    v = split[0]
                    u = RAW_AT[("w", v)]
                    high_part(v % RING, u % RING, 16 * (u // RING + 1), v - RING + 1, v >= RING)
                    split[0] += 1

            def split_behind(p):
                passed = RAW_AT[("w", p + 1)]
                reach = lambda v: all(STREAM[u][0] == "w" or u < passed for u in range(RAW_AT[("w", v)] - RING + 1))
                n = p + 1
                while n < min(p + 1 + RING, W_IN + 8) and reach(n):
                    n += 1
                split_to(n)

            def used(v):
                act.wait_ge(split_used, v + 1)

            tables_loaded = [0]

            def load_table(func):
                n = tables_loaded[0]
                tables_loaded[0] += 1
                act.activation(warm[:, n:n + 1], eps[:, 0:1], func)

            norms = [0]

            def norm_stats(src, ready):
                ready(act)
                n = norms[0]
                norms[0] += 1
                if n:
                    act.wait_ge(sem("norm_rstd"), n)
                act.activation(squares_out[0], src[:, 0, :], ACT.Square, accum_out=ssq[:, 0:1]).then_inc(sem("norm_ss_a"), 1)
                act.wait_ge(sem("norm_ss_a"), n + 1)
                act.wait_ge(sem("norm_ss_v"), n + 1)
                act.activation(rms[:, :], ssq[:, :], ACT.Sqrt, scale=1.0 / D, bias=eps[:, 0:1]).then_inc(sem("norm_rms"), 1)
                act.wait_ge(sem("norm_rstd"), n + 1)

            squares_out = [rows[:, 0, :]]

            def norm_scale(src, dst):
                act.activation(dst[:, 0, :], src[:, 0, :], ACT.Copy, scale=rstd[:, 0:1]).then_inc(sem("xn_a"), 1)

            def split_T(stage, gain=None, shifted=False, hi=hT_hi, n=4, qs=None, first=0):
                for q in qs or range(n):
                    if shifted:
                        act.wait_ge(sem("full_T"), shifts[0] + 1)
                        act.activation(hi[:, 2 * q:2 * q + 2, :], shift_buf(shifts[0]), ACT.Copy).then_inc(sem("T_hi"), 1)
                        shifts[0] += 1
                        continue
                    b = filled(act, (stage, q))
                    if gain is None:
                        act.activation(hi[:, first + 2 * q:first + 2 * q + 2, :].rearrange("p a t -> p (a t)"), b[:, :], ACT.Copy)\
                            .then_inc(sem("T_hi"), 1)
                    else:
                        act.activation(hi[:, 2 * q, :], b[:, 0:T], ACT.Copy, scale=gain[:, 2 * q:2 * q + 1])
                        act.activation(hi[:, 2 * q + 1, :], b[:, T:2 * T], ACT.Copy, scale=gain[:, 2 * q + 1:2 * q + 2])\
                            .then_inc(sem("T_hi"), 1)

            shifts = [0]

            def copy_out(name, dst, func=ACT.Copy, n=512, scale=1.0):
                act.activation(dst, bank_of(name)[:, 0:n], func, scale=scale).then_inc(read_sem(name), 1)

            split_to(1)
            act.wait_ge(sem("eps_set"), 1)
            act.wait_ge(sem("cols_loaded"), 16)
            act.activation(silu_c[:].rearrange("p k c -> p (k c)"), col("cond"), ACT.Silu).then_inc(sem("silu_c"), 1)
            act.activation(lg_rows[:, :], col("decay_rows"), ACT.Exp).then_inc(sem("lg_exp"), 1)
            act.activation(lg_pairs[:, :], col("decay_pairs"), ACT.Exp).then_inc(sem("lg_exp"), 1)
            split_T("memT", col("mem_norm"))
            split_to(2)
            norm_stats(mem_in, lambda e: e.wait_ge(sem("mem_loaded"), 16))
            split_to(4)
            norm_stats(x, lambda e: e.wait_ge(sem("x_loaded"), 16))
            norm_scale(x, xn)
            act.wait_ge(sem("rstd_mem"), 1)
            for c in range(4):
                split_behind(W_KV + 2 * c)
                if c < 3:
                    split_behind(W_KV + 2 * c + 1)
                used(W_KV + 2 * c + 1)
                for tb in range(TB):
                    dst = (mem_k if c < 2 else memV)[:, tb, (c % 2) * 512:(c % 2 + 1) * 512]
                    copy_out(("kv", c, tb), dst, scale=rstd_mem[:, tb:tb + 1])
                if c == 0:
                    norm_stats(ctx_in, lambda e: e.wait_ge(sem("ctx_loaded"), 16))
                    norm_scale(ctx_in, rows)
                if c == 2:
                    act.wait_ge(sem("lg_neg"), 2)
                    act.wait_ge(sem("const1_loaded"), 16)
                    for fb in range(2):
                        for jb in range(TB):
                            a = act.activation(ctx_decay[:, 2 * fb + jb, :], lg_rows[:, 8 * fb:8 * fb + 8], ACT.Exp,
                                               scale=c1("ctx_dist", 2 * fb + jb, 2 * fb + jb + 1))
                            a.then_inc(sem("ctx_decay"), 1)
            split_to(W_IN + 1)
            for q in range(4):
                b = filled(act, ("keyT", q))
                act.activation(memKT[:, 2 * q:2 * q + 2, :].rearrange("p a t -> p (a t)"), b[:, :], ACT.Copy)\
                    .then_inc(read_sem(("keyT", q)), 1)
            for n in range(4):
                if n == 2:
                    split_to(W_IN + 2)
                split_T(None, shifted=True, hi=[hT_hi, hcT_hi][n % 2], qs=[2 * (n // 2), 2 * (n // 2) + 1])

            for part, v, n in [("kr", 0, 2), ("vr", 2, 2), ("kava", 4, 1), ("qa", 5, 2), ("qr", 7, 2)]:
                split_to(W_IN + {"kr": 4, "vr": 5, "kava": 6, "qa": 8, "qr": 9}[part])
                used(W_IN + v + n - 1)
                if part == "kr":
                    for tile in range(4):
                        copy_out((part, tile), staged[:, tile, :])
                elif part == "vr":
                    for tile in range(4):
                        copy_out((part, tile), vr[:, tile, :])
                elif part == "kava":
                    for tile in range(4):
                        copy_out((part, tile), kava[:, tile, :], n=256)
                    act.wait_ge(sem("ka_ss"), 1)
                    act.activation(head_rms[:, 0:8], head_ss[:, 0:8], ACT.Sqrt, scale=1.0 / HD, bias=eps[:, 0:1])\
                        .then_inc(sem("ka_rms"), 1)
                elif part == "qr":
                    for tb in range(TB):
                        copy_out((part, tb), staged[:, 2 + tb, :])
                else:
                    act.wait_ge(sem("kr_done"), 1)
                    for tb in range(TB):
                        copy_out((part, tb), staged[:, tb, :])
                    act.wait_ge(sem("qa_ss"), 1)
                    act.activation(head_rms[:, :], head_ss[:, :], ACT.Sqrt, scale=1.0 / HD, bias=eps[:, 0:1])\
                        .then_inc(sem("qa_rms"), 1)
            for q in range(2):
                b = filled(act, ("krT", q))
                for e in range(2):
                    half = slice(64 * e, 64 * e + 64)
                    ins = act.activation(krT.rearrange("p (n e) t -> p n e t", e=2)[half, 2 * q:2 * q + 2, e, :],
                                         b[half, :].rearrange("p (n t) -> p n t", t=T), ACT.Copy)
                ins.then_inc(read_sem(("krT", q)), 1)
            b = filled(act, ("kaT", 0))
            for e in range(2):
                half = slice(64 * e, 64 * e + 64)
                ins = act.activation(kaT[half, e, :], b[half, :], ACT.Copy)
            ins.then_inc(read_sem(("kaT", 0)), 1)

            def queries_out(name, dst, qs=(0, 1)):
                for q in qs:
                    b = filled(act, (name, q))
                    act.activation(dst[:, 2 * q:2 * q + 2, :].rearrange("p a t -> p (a t)"), b[:, :], ACT.Copy)\
                        .then_inc(read_sem((name, q)), 1)

            queries_out("qaT", qaT)
            split_to(W_IN + 10)

            def attention_probs(s):
                act.wait_ge(sem("neg_max"), s + 1)
                if s >= 2:
                    filled(act, ("probsT", s - 2))
                act.activation(probs[:, s % 2, :], bank_of(("scores", s))[:, :], ACT.Exp, scale=HD ** -0.5,
                               bias=row_max[:, s:s + 1], accum_out=row_sum[:, s:s + 1]).then_inc(read_sem(("scores", s)), 1)

            def decays(r):
                act.wait_ge(sem("decay_arg"), r + 1)
                if r >= 2:
                    read_out(act, ("ret_scores", r - 2))
                act.activation(decay_mats[r % 2], decay_arg, ACT.Exp).then_inc(sem("decay_mat"), 1)

            def query_decays(r):
                if r:
                    act.wait_ge(sem("q_decayed"), r)
                act.activation(q_dec[:, 0, :], c1("from_start"), ACT.Exp, scale=lg_pairs[:, r // 2:r // 2 + 1])
                act.activation(q_dec[:, 1, :], c1("to_end"), ACT.Exp, scale=lg_pairs[:, 4 + r // 2:5 + r // 2])\
                    .then_inc(sem("q_dec"), 1)

            attention_probs(0)
            attention_probs(1)
            for s in range(2 * HEADS):
                b = filled(act, ("probsT", s))
                if s >= 2:
                    act.wait_ge(sem("att_step"), s - 1)
                act.activation(probsT[:, s % 2, :], b[:, :], ACT.Copy).then_inc(read_sem(("probsT", s)), 1)
                if s + 2 < 2 * HEADS:
                    attention_probs(s + 2)
                if s in SPLIT_STEPS:
                    split_to(SPLIT_STEPS[s] + 1)
                if s == GR_STEP:
                    act.wait_ge(sem("rope_done"), 6)
                    used(W_IN + 10)
                    for tb in range(TB):
                        copy_out(("gr", tb), silu_gr[:, tb, :])
                if s >= 2 * HEADS - 2:
                    queries_out("qrT", qrT, [s - (2 * HEADS - 2)])
                if s == 2 * HEADS - 2:
                    decays(0)

            query_decays(0)
            filled(act, ("probsT", 2 * HEADS - 1))
            decays(1)
            act.wait_ge(sem("att_step"), 2 * HEADS)
            for tb in range(TB):
                act.activation(hT_hi[:, 0:4, tb * P:(tb + 1) * P], bank_of(("att", tb))[:, :].rearrange("p (a t) -> p a t", t=P),
                               ACT.Copy).then_inc(sem("T_hi"), 1)
            for r in range(2, HEADS):
                decays(r)
                if r % 2 == 0:
                    query_decays(r)
                if r in (3, 5):
                    split_to(W_OUT + (r + 1) // 2)
            act.activation(silu_gr[:].rearrange("p a n -> p (a n)"), silu_gr[:].rearrange("p a n -> p (a n)"), ACT.Silu)\
                .then_inc(sem("silu_gr"), 1)
            load_table(ACT.Sqrt)
            for tb in range(TB):
                act.wait_ge(sem("ret_centred"), tb + 1)
                act.activation(probs[:, tb, :], xn[:, tb, 512:1024], ACT.Square).then_inc(sem("ret_sq"), 1)
            act.wait_ge(sem("ret_var"), 1)
            act.activation(head_rms[:, :], head_ss[:, :], ACT.Sqrt, scale=1.0 / HD, bias=eps[:, 0:1])\
                .then_inc(sem("ret_rms"), 1)
            split_to(W_OUT + 4)
            split_T("mixT", n=2, first=4)
            for q in range(4):
                b = filled(act, ("gain_row", q))
                act.activation(rows[:, q // 2, (q % 2) * 512:(q % 2 + 1) * 512], b[:, :], ACT.Copy)\
                    .then_inc(read_sem(("gain_row", q)), 1)

            def post_norm(name, g):
                n = norms[0]
                norms[0] += 1
                for c in range(2):
                    product_done(act, name, c)
                    act.activation(xn[:, 0, c * 512:(c + 1) * 512], bank_of((*name, 0, c))[:, :], ACT.Square,
                                   accum_out=half_ss[:, c, 0:1]).then_inc(sem("tile0_squared"), 1)
                    act.wait_ge(sem("y_gained"), 4 * g + 2 * c + 1)
                    act.activation(xn[:, 1, c * 512:(c + 1) * 512], bank_of((*name, 1, c))[:, :], ACT.Square,
                                   accum_out=half_ss[:, c, 1:2]).then_inc(sem("norm_ss_a" if c else "half_ss_ready"), 1)
                act.wait_ge(sem("norm_ss_a"), n + 1)
                act.wait_ge(sem("norm_ss_v"), n + 1)
                for tb in range(TB):
                    ins = act.activation(rms[:, tb:tb + 1], half_ss[:, 1, tb:tb + 1], ACT.Sqrt, scale=1.0 / D,
                                         bias=half_mean[:, tb:tb + 1])
                ins.then_inc(sem("norm_rms"), 1)
                act.wait_ge(sem("norm_rstd"), n + 1)

            squares_out[0] = xn[:, 0, :]
            post_norm(("mix_out",), 0)
            split_to(W_OUT + 4 + 1)

            def ffn(f):
                up, dn = W_UP[f], W_DN[f]

                def silu_gate(c, before):
                    act.wait_ge(split_used, before)
                    for tb in range(TB):
                        act.activation(gate[:, c % 3, tb, :], bank[(c % 3) * 2 + tb][:, 0:256], ACT.Silu,
                                       scale=rstd[:, tb:tb + 1] if f else 1.0)\
                            .then_inc(sem("gate_silu"), 1)

                g0 = plan.of[("gateT", f, 0)][2]

                def gate_hi(c, full, at):
                    act.wait_ge(bank_full[6], full)
                    act.activation(gT_hi[:, at, :] if isinstance(at, slice) else gT_hi[:, bass.ds(at, 2), :],
                                   bank[6][:, :].rearrange("p (a t) -> p a t", t=T), ACT.Copy).then_inc(sem("gateT_hi"), 1)

                split_to(up + RING)
                for c in range(2):
                    split_to(up + 2 * c + 5)
                    silu_gate(c, up + 2 * c + 2)
                    if c:
                        gate_hi(0, g0 + 1, slice(0, 2))
                v0 = split[0]
                u0 = RAW_AT[("w", v0)]
                assert v0 == up + 7
                with act.Fori(0, 3) as i:
                    for j in range(3):
                        for e in range(2):
                            k = 2 * j + e
                            high_part((v0 + k) % RING, (u0 + k) % RING, i * 32 + 16 * ((u0 + k) // RING + 1),
                                      i * 6 + (v0 + k - RING + 1))
                        c = 2 + j
                        silu_gate(c, i * 6 + (up + 2 * c + 2))
                        gate_hi(c - 1, i * 3 + (g0 + c), i * 6 + 2 * (c - 1))
                split[0] += 18
                split_to(dn + 1 + RING)
                gate_hi(UP - 1, g0 + UP, slice(2 * UP - 2, 2 * UP))
                load_table(ACT.Sqrt)
                split_to(dn + UP)

            def pre_norm(stage, ready, gain, following):
                split_to(following + 2)
                split_T(stage, gain)
                norm_stats(x, ready)
                split_to(following + 3)

            norm_stats(x, x_added(("mix_out",), 0))
            norm_scale(x, xn)
            split_to(W_OUT + 4 + 2)
            split_T("ffn0T", shifted=True)
            ffn(0)
            split_to(W_UP[1] + 2)
            post_norm(("down", 0), 1)
            pre_norm("ffn1T", x_added(("down", 0), 0), col("ffn1_norm"), W_UP[1])
            act.dma_start(rows[:, 0, :], io["final_norm"].to_broadcast([P, D])).then_inc(sem("final_loaded"), 16)
            ffn(1)
            split_to(W_IN2 + 2)
            used(W_DN[1] + UP - 1)
            for dst, src, name in [(const2, io["const2"], "const2_loaded"),
                                   (lb_p.rearrange("p a n -> p (a n)"), io["lb_param"].to_broadcast([P, D]), "lb_loaded"),
                                   (head_row, io["hgrn_out_norm"].to_broadcast([P, 512]), "head_row_loaded")]:
                act.dma_start(dst, src).then_inc(sem(name), 16)
            pre_norm("mix2T", x_added(("down", 1), 0), col("mix_norm"), W_IN2)

            act.wait_ge(sem("const2_loaded"), 16)
            act.activation(sums_r[:].rearrange("p l t -> p (l t)"), const2[:, 0:(LEVELS + 2) * P], ACT.Copy)\
                .then_inc(sem("sums_ready"), 1)
            act.wait_ge(sem("lb_diff"), 1)
            act.activation(lb_p[:].rearrange("p a n -> p (a n)"), lb_p[:].rearrange("p a n -> p (a n)"), ACT.Exp)\
                .then_inc(sem("lb_exp"), 1)

            def streamed_out(k, part, dst, func=ACT.Copy):
                split_to(W_IN2 + 2 * k + 2 + RING)
                used(W_IN2 + 2 * k + 1)
                for tb in range(TB):
                    copy_out((part, tb), dst[:, tb, :], func, scale=rstd[:, tb:tb + 1])

            def level_decays(level):
                for blk in range(TB):
                    b = filled(act, ("decay", level, blk))
                    if blk == 0 and level >= 2:
                        filled(act, ("pairs", level - 2, 1))
                    act.activation(qk_dec[level % 2][:, blk * 512:(blk + 1) * 512], b[:, :], ACT.Exp)\
                        .then_inc(read_sem(("decay", level, blk)), 1)

            streamed_out(0, "zf", fgate, ACT.Sigmoid)
            act.wait_ge(sem("fgate"), 1)
            streamed_out(1, "zq", hq, ACT.Silu)
            act.activation(fgate[:].rearrange("p a n -> p (a n)"), fgate[:].rearrange("p a n -> p (a n)"), ACT.Ln)\
                .then_inc(sem("logf"), 1)
            act.wait_ge(sem("logf"), 1)
            act.activation(logf_hi[:].rearrange("p a n -> p (a n)"), fgate[:].rearrange("p a n -> p (a n)"), ACT.Copy)\
                .then_inc(sem("logf_hi"), 1)
            for q in range(2):
                b = filled(act, ("hqT", q))
                act.activation(hqT[:, q * 512:(q + 1) * 512], b[:, :], ACT.Copy, scale=P ** -0.5)\
                    .then_inc(read_sem(("hqT", q)), 1)
            for q in range(2):
                b = filled(act, ("hkT", q))
                act.activation(hkT[:, q * 512:(q + 1) * 512], b[:, :], ACT.Copy).then_inc(read_sem(("hkT", q)), 1)
            streamed_out(2, "zi", hv)
            for step in range(8):
                if step < LEVELS:
                    split_to(W_IN2 + 6 + step + RING)
                level_decays(step)
                if step == 1:
                    streamed_out(3, "zc", zc_sb)
                if step == 3:
                    split_to(W_IN2 + 10 + RING)
                if step == 5:
                    streamed_out(5, "zb", zb_sb)
                if step == LEVELS - 1:
                    for j in range(2):
                        b = filled(act, f"uT{j}")
                        act.activation(uT.rearrange("p (c t) -> p c t", t=T + 2)[:, 2 * j:2 * j + 2, 2:T + 2],
                                       b[:, :].rearrange("p (c t) -> p c t", t=T), ACT.Copy).then_inc(read_sem(f"uT{j}"), 1)
            load_table(ACT.Silu)
            streamed_out(6, "zg", silu_zg, ACT.Silu)
            for j in range(2):
                read_out(act, f"bT{j}")
                act.activation(hT_hi[:, 4 + 2 * j:6 + 2 * j, :], conv[:, 2 * j:2 * j + 2, :], ACT.Copy)\
                    .then_inc(sem("conv_hi"), 1)
            load_table(ACT.Sqrt)
            for blk in range(TB):
                b = filled(act, ("hgrn", blk))
                if blk:
                    act.wait_ge(sem("hgrn_ss"), blk)
                act.activation(hgrn_sq, b[:, :], ACT.Square).then_inc(sem("hgrn_sq"), 1)
            act.wait_ge(sem("hgrn_ss"), TB)
            act.activation(head_rms[:, 0:8], head_ss[:, 0:8], ACT.Sqrt, scale=1.0 / P, bias=eps[:, 0:1])\
                .then_inc(sem("hgrn_rms"), 1)
            split_T("mix2oT", n=2)
            pre_norm("xattT", x_added(("mix2_out",), 0), col("xattn_norm"), W_OUT2 + 4)

            load_table(ACT.Exp)
            split_to(W_Q + 4)
            for c in range(2):
                if c:
                    split_to(W_O + 2)
                used(W_Q + 2 * c + 1)
                for tb in range(TB):
                    copy_out(("mq", tb, c), mq[:, tb, c * 512:(c + 1) * 512], scale=rstd[:, tb:tb + 1])
                for q in (2 * c, 2 * c + 1):
                    b = filled(act, ("mqT", q))
                    act.activation(mqT[:, 2 * q:2 * q + 2, :].rearrange("p a t -> p (a t)"), b[:, :], ACT.Copy)\
                        .then_inc(read_sem(("mqT", q)), 1)
            for h in range(MEM_HEADS):
                for tb in range(TB):
                    s = TB * h + tb
                    act.wait_ge(sem("neg_max"), 16 + s + 1)
                    if h:
                        filled(act, ("mprobsT", h - 1))
                    act.activation(mprobs[:, tb, :], bank_of(("mscores", h, tb))[:, 0:T], ACT.Exp, scale=MEM_HD ** -0.5,
                                   bias=row_max[:, s:s + 1], accum_out=row_sum[:, s:s + 1])\
                        .then_inc(read_sem(("mscores", h, tb)), 1)
                b = filled(act, ("mprobsT", h))
                if h >= 2:
                    act.wait_ge(sem("matt_step"), h - 1)
                act.activation(mprobsT[:, h % 2, :], b[:, :], ACT.Copy).then_inc(read_sem(("mprobsT", h)), 1)
                if h == 0:
                    split_to(W_O + 3)
            split_T("mattT")
            pre_norm("ffn2T", x_added(("mem_out",), 0), col("ffn2_norm"), W_O + 4)
            ffn(2)
            norm_stats(x, x_added(("down", 2), 0))

        @block.vector
        def _(dve):
            chained = [0]

            def chain(ins):
                chained[0] += 1
                ins.then_inc(sem("dve_chain"), 1)
                dve.wait_ge(sem("dve_chain"), chained[0])

            norms = [0]
            squares_out = [rows[:, 1, :]]

            def norm_stats(src, ready):
                ready(dve)
                n = norms[0]
                norms[0] += 1
                dve.tensor_tensor_reduce(out=squares_out[0], in0=src[:, 1, :], in1=src[:, 1, :], scale=1.0, scalar=0.0,
                                         op0=ALU.mult, op1=ALU.add, accum_out=ssq[:, 1:2]).then_inc(sem("norm_ss_v"), 1)
                dve.wait_ge(sem("norm_rms"), n + 1)
                dve.reciprocal(rstd[:, :], rms[:, :]).then_inc(sem("norm_rstd"), 1)
                dve.wait_ge(sem("norm_rstd"), n + 1)

            def norm_scale(src, dst):
                dve.tensor_scalar(dst[:, 1, :], src[:, 1, :], rstd[:, 1:2], None, ALU.mult).then_inc(sem("xn_v"), 1)

            hi_seen = [0]
            shifts = [0]
            shifted_names = []

            def shifted_T_parts(parts):
                def whole(name, shift, hi, lo):
                    a, s = shift
                    b = filled(dve, name)
                    buf = shift_buf(shifts[0])
                    if shifts[0] >= 2:
                        read_out(dve, shifted_names[shifts[0] - 2])
                    for e in range(2):
                        k = 2 * name[1] + e
                        ins = dve.tensor_scalar(buf[:, e, :], b[:, e * T:(e + 1) * T], a[:, k:k + 1], s[:, k:k + 1],
                                                ALU.mult, ALU.add)
                    ins.then_inc(sem("full_T"), 1)
                    shifted_names.append(name)
                    shifts[0] += 1

                def low(n, name, shift, hi, lo):
                    hi_seen[0] += 1
                    dve.wait_ge(sem("T_hi"), hi_seen[0])
                    k = slice(2 * name[1], 2 * name[1] + 2)
                    dve.tensor_tensor(lo[:, k, :], shift_buf(n), hi[:, k, :].bitcast(F32), ALU.subtract)\
                        .then_inc(read_sem(name), 1)

                first = shifts[0]
                for n, part in enumerate(parts):
                    whole(*part)
                    if n:
                        low(first + n - 1, *parts[n - 1])
                low(first + len(parts) - 1, *parts[-1])

            def split_T(stage, gain=None, shift=None, hi=hT_hi, lo=hT_lo, n=4, first=0):
                if shift is not None:
                    shifted_T_parts([((stage, q), shift, hi, lo) for q in range(n)])
                    return
                for q in range(n):
                    name = (stage, q)
                    hi_seen[0] += 1
                    dve.wait_ge(sem("T_hi"), hi_seen[0])
                    b = bank_of(name)
                    if gain is None:
                        k = slice(first + 2 * q, first + 2 * q + 2)
                        dve.tensor_tensor(lo[:, k, :], b[:, :].rearrange("p (a t) -> p a t", t=T),
                                          hi[:, k, :].bitcast(F32), ALU.subtract).then_inc(read_sem(name), 1)
                    else:
                        for e in range(2):
                            k = 2 * q + e
                            ins = dve.scalar_tensor_tensor(out=lo[:, k, :], in0=b[:, e * T:(e + 1) * T],
                                                           scalar=gain[:, k:k + 1], in1=hi[:, k, :].bitcast(F32),
                                                           op0=ALU.mult, op1=ALU.subtract)
                        ins.then_inc(read_sem(name), 1)

            ropes = [0]

            def rope(src, cos, sin, dst, n, scratch=(rope_a, rope_b)):
                v = src.rearrange("p (h d) -> p h d", d=HD)
                a, b = (t[:, 0:n * HD].rearrange("p (h d) -> p h d", d=HD) for t in scratch)
                dve.tensor_tensor(a, v, over_heads(cos, n, HD), ALU.mult)
                dve.tensor_tensor(b[:, :, 0:HD // 2], v[:, :, HD // 2:HD], over_heads(sin[:, 0:HD // 2], n, HD // 2), ALU.mult)
                chain(dve.tensor_tensor(b[:, :, HD // 2:HD], v[:, :, 0:HD // 2], over_heads(sin[:, HD // 2:HD], n, HD // 2),
                                        ALU.mult))
                if len(dst.shape) == 4:
                    a = a.rearrange("p (k j) d -> p k j d", k=KV_HEADS)
                    b = b.rearrange("p (k j) d -> p k j d", k=KV_HEADS)
                dve.tensor_tensor(dst, a, b, ALU.add).then_inc(sem("rope_done"), 1)
                ropes[0] += 1
                dve.wait_ge(sem("rope_done"), ropes[0])

            heads = lambda ap: ap.rearrange("p (h d) -> p h d", d=HD)

            dve.memset(eps[:, :], EPS).then_inc(sem("eps_set"), 1)
            dve.wait_ge(sem("fixed_loaded"), 16)
            dve.wait_ge(sem("cols_loaded"), 16)
            split_T("memT", col("mem_norm"))
            norm_stats(mem_in, lambda e: e.wait_ge(sem("mem_loaded"), 16))
            dve.tensor_copy(rstd_mem[:, :], rstd[:, :]).then_inc(sem("rstd_mem"), 1)
            dve.wait_ge(sem("lg_exp"), 2)
            dve.tensor_scalar(lg_rows[:, :], lg_rows[:, :], -1.0, None, ALU.mult).then_inc(sem("lg_neg"), 1)
            dve.tensor_scalar(lg_pairs[:, :], lg_pairs[:, :], -1.0, None, ALU.mult).then_inc(sem("lg_neg"), 1)
            def weigh_mod(m):
                u, c, half = RAW_AT[("mod", m)], m // 2, m % 2
                dve.wait_ge(raw_ready[u % RING], 16 * (u // RING + 1))
                if half == 0 and (2 <= c < MOD_A // 2 or c >= MOD_A // 2 + 2):
                    if c - 2 >= MODS_IN:
                        filled(dve, ("mod_col", c - 2))
                    else:
                        dve.wait_ge(sem("mod_col"), c - 1)
                for k in range(4):
                    w = raw[:, u % RING, k * 512:(k + 1) * 512]
                    for cond in range(2 if m < MOD_A else 1):
                        acc = acc_a[:, c % 2, cond, :] if m < MOD_A else acc_b[:, c % 2, :]
                        s = silu_c[:, 4 * half + k, cond:cond + 1]
                        if half == 0 and k == 0:
                            ins = dve.tensor_scalar(acc, w, s, None, ALU.mult)
                        else:
                            ins = dve.scalar_tensor_tensor(out=acc, in0=w, scalar=s, in1=acc, op0=ALU.mult, op1=ALU.add)
                    if k < 3:
                        chain(ins)
                ins.then_inc(mod_used, 1)
                dve.wait_ge(mod_used, m + 1)

            dve.wait_ge(sem("silu_c"), 1)
            weigh_mod(0)
            weigh_mod(1)
            norm_stats(x, lambda e: e.wait_ge(sem("x_loaded"), 16))
            norm_scale(x, xn)
            weigh_mod(2)
            norm_stats(ctx_in, lambda e: e.wait_ge(sem("ctx_loaded"), 16))
            norm_scale(ctx_in, rows)
            for m in range(3, MOD_A):
                weigh_mod(m)
            dve.wait_ge(sem("const1_loaded"), 16)
            half = HD // 2
            for n, base in ((0, 0), (1, HD)):
                g = col("qk_gain", base, base + HD)
                cs, sn = (tables[:, 2 * n + e, :].rearrange("p (b d) -> p b d", d=HD) for e in range(2))
                cos_t = c1("rope_cos").rearrange("p (b d) -> p b d", d=HD)
                sin_t = c1("rope_sin").rearrange("p (b d) -> p b d", d=HD)
                dve.tensor_tensor(cs, cos_t, over_heads(g, TB, HD), ALU.mult)
                dve.tensor_tensor(sn[:, :, 0:half], sin_t[:, :, 0:half], over_heads(g[:, half:HD], TB, half), ALU.mult)
                chain(dve.tensor_tensor(sn[:, :, half:HD], sin_t[:, :, half:HD], over_heads(g[:, 0:half], TB, half), ALU.mult))
            dve.wait_ge(sem("ctx_decay"), 4)
            chain(dve.tensor_scalar(ctx_decay[:], ctx_decay[:], HD ** -0.5, None, ALU.mult))

            dve.wait_ge(sem("mod_col"), MOD_A // 2)
            b = bank_of("mod_a")
            chain(dve.tensor_tensor(mod[:, 0:16, :], b[:, 0:32].rearrange("p (j c) -> p j c", c=2),
                                    heads_bc(col("b_mod", 0, 16), 16, 2), ALU.add))
            chain(dve.tensor_scalar(a_mix[:], mod[:, 8:16, :], 1.0, None, ALU.add))
            dve.tensor_tensor(a_mix[:], a_mix[:], heads_bc(col("g_pre_mix"), 8, 2), ALU.mult).then_inc(read_sem("mod_a"), 1)
            read_out(dve, "mod_a")
            sides = {"xT": ((a_mix[:, :, 0], mod[:, 0:8, 0]), hT_hi, hT_lo), "ctxT": ((a_mix[:, :, 1], mod[:, 0:8, 1]), hcT_hi, hcT_lo)}
            shifted_T_parts([(name, *sides[name[0]]) for name in FIRST_T])

            read_out(dve, ("ctxT", 3))
            filled(dve, ("ctxT", 3))
            weighed = [MOD_A]

            def weigh_behind(j):
                while weighed[0] < MOD_A + sum(IN_MODS[:j + 1]):
                    weigh_mod(weighed[0])
                    weighed[0] += 1

            weigh_behind(2)
            for e in range(2):
                other = slice(64 * (1 - e), 64 * (1 - e) + 64)
                dve.memset(state.rearrange("p a (n e) c -> p a n e c", e=2)[other, :, :, e, :], 0.0)
                dve.memset(krT.rearrange("p (n e) t -> p n e t", e=2)[other, :, e, :], 0.0)

            read_out(dve, ("kr", 1))
            for tb in range(TB):
                rope(staged[:, tb, :], c1("rope_cos", tb * HD, (tb + 1) * HD), c1("rope_sin", tb * HD, (tb + 1) * HD),
                     heads(krn[:, tb, :]), HEADS)
            read_out(dve, ("kr", 3))
            for fb in range(2):
                for jb in range(TB):
                    ins = dve.tensor_tensor(heads(k_fb[:, fb, jb, :]), heads(staged[:, 2 + jb, :]),
                                            heads_bc(ctx_decay[:, 2 * fb + jb, :], HEADS, HD), ALU.mult)
            ins.then_inc(sem("kr_done"), 1)
            weigh_behind(4)
            read_out(dve, ("kava", 3))
            sq = rope_a.rearrange("p (a b) -> p a b", b=P)
            chain(dve.tensor_tensor(sq, kava[:, :, 0:P], kava[:, :, 0:P], ALU.mult))
            dve.reduce_sum(head_ss[:, 0:8], rope_a.rearrange("p (h d) -> p h d", d=HD), AX.X).then_inc(sem("ka_ss"), 1)
            dve.wait_ge(sem("ka_rms"), 1)
            chain(dve.reciprocal(head_rstd[:, 0:8], head_rms[:, 0:8]))
            for tile in range(4):
                ins = dve.tensor_tensor(heads(kava[:, tile, 0:P]), heads(kava[:, tile, 0:P]),
                                        heads_bc(head_rstd[:, 2 * tile:2 * tile + 2], 2, HD), ALU.mult)
            chain(ins)
            for tile in range(2):
                dve.tensor_tensor(heads(ka_all[:, tile, :]), heads(kava[:, 2 + tile, 0:P]),
                                  over_heads(col("qk_gain", HD, 2 * HD), KV_HEADS, HD), ALU.mult)
                rope(kava[:, tile, 0:P], tables[:, 2, tile * HD:(tile + 1) * HD], tables[:, 3, tile * HD:(tile + 1) * HD],
                     heads(ka_all[:, 2 + tile, :]), KV_HEADS)
            for e in range(2):
                other = slice(64 * (1 - e), 64 * (1 - e) + 64)
                ins = dve.memset(kaT[other, e, :], 0.0)
            ins.then_inc(sem("keys_padded"), 1)
            read_out(dve, ("qa", 1))
            for tb in range(TB):
                chain(dve.tensor_tensor(rope_a, staged[:, tb, :], staged[:, tb, :], ALU.mult))
                ins = dve.reduce_sum(head_ss[:, tb * 8:tb * 8 + 8], heads(rope_a), AX.X)
                if tb == 0:
                    chain(ins)
            ins.then_inc(sem("qa_ss"), 1)
            dve.wait_ge(sem("qa_rms"), 1)
            chain(dve.reciprocal(head_rstd[:, :], head_rms[:, :]))
            for tb in range(TB):
                ins = dve.tensor_tensor(heads(staged[:, tb, :]), heads(staged[:, tb, :]),
                                        heads_bc(head_rstd[:, tb * 8:tb * 8 + 8], HEADS, HD), ALU.mult)
            chain(ins)
            for tb in range(TB):
                rope(staged[:, tb, :], tables[:, 0, tb * HD:(tb + 1) * HD], tables[:, 1, tb * HD:(tb + 1) * HD],
                     qan[:, tb, :].rearrange("p (j k d) -> p k j d", k=KV_HEADS, d=HD), HEADS)
            b = filled(dve, "states")
            for e in range(2):
                half = slice(64 * e, 64 * e + 64)
                ins = dve.tensor_copy(state.rearrange("p a (n e) c -> p a n e c", e=2)[half, :, :, e, :],
                                      b[half, :].rearrange("p (a n c) -> p a n c", a=2, c=HD))
            ins.then_inc(read_sem("states"), 1)

            def decay_of(r):
                if r:
                    dve.wait_ge(sem("decay_mat"), r)
                chain(dve.tensor_scalar(decay_arg, c1("fwd_dist"), lg_rows[:, r:r + 1], None, ALU.mult))
                dve.scalar_tensor_tensor(out=decay_arg, in0=c1("bwd_dist"), scalar=lg_rows[:, 8 + r:9 + r], in1=decay_arg,
                                         op0=ALU.mult, op1=ALU.add).then_inc(sem("decay_arg"), 1)

            def negative_max(s, name, n, scale):
                b = filled(dve, name)
                chain(dve.reduce_max(row_max[:, s:s + 1], b[:, 0:n], AX.X))
                dve.tensor_scalar(row_max[:, s:s + 1], row_max[:, s:s + 1], -scale, None, ALU.mult).then_inc(sem("neg_max"), 1)

            def normalise(s):
                read_out(dve, ("scores", s))
                chain(dve.reciprocal(row_inv[:, s:s + 1], row_sum[:, s:s + 1]))
                dve.tensor_scalar(probs[:, s % 2, :], probs[:, s % 2, :], row_inv[:, s:s + 1], None, ALU.mult)\
                    .then_inc(sem("probs_ready"), 1)

            def mod_column(cs, name):
                b = bank_of(name)
                ins = dve.tensor_tensor(mod[:, 4 * cs[0]:4 * cs[-1] + 4, 0], b[:, 0:4 * len(cs)],
                                        col("b_mod", 4 * cs[0], 4 * cs[-1] + 4), ALU.add)
                ins.then_inc(read_sem(name), 1)
                read_out(dve, name)

            dve.wait_ge(sem("mod_col"), MODS_IN)
            mod_column(list(range(MOD_A // 2, MODS_IN)), "mod_b")

            def retention_queries():
                read_out(dve, ("qr", 1))
                filled(dve, ("krT", 1))
                for tb in range(TB):
                    rope(staged[:, 2 + tb, :], c1("rope_cos", tb * HD, (tb + 1) * HD), c1("rope_sin", tb * HD, (tb + 1) * HD),
                         heads(qrn[:, tb, :]), HEADS, (krn[:, 0, :], krn[:, 1, :]))

            for s in range(2):
                negative_max(s, ("scores", s), 512, HD ** -0.5)
            for s in range(2 * HEADS):
                normalise(s)
                if s + 2 < 2 * HEADS:
                    negative_max(s + 2, ("scores", s + 2), 512, HD ** -0.5)
                if s in WEIGH_STEPS:
                    weigh_mod(WEIGH_STEPS[s])
                for c, step in MOD_STEPS.items():
                    if step == s:
                        filled(dve, ("mod_col", c))
                        mod_column([c], ("mod_col", c))
                if s == QR_STEP:
                    retention_queries()
                if s in (2 * HEADS - 3, 2 * HEADS - 1):
                    decay_of((s - (2 * HEADS - 3)) // 2)

            for r in range(HEADS):
                if r % 2 == 0:
                    dve.wait_ge(sem("q_dec"), r // 2 + 1)
                    read_out(dve, ("qrT", 1))
                    if r:
                        dve.wait_ge(sem("ret_step"), r)
                    for fb in range(2):
                        dve.tensor_tensor(q_decayed[:, fb, :], qrT[:, r // 2, :], q_dec[:, fb, :], ALU.mult)\
                            .then_inc(sem("q_decayed"), 1)
                dve.wait_ge(sem("decay_mat"), r + 1)
                m = decay_mats[r % 2]
                chain(dve.tensor_tensor(m[:, P:2 * P], m[:, P:2 * P], ident, ALU.add))
                b = filled(dve, ("ret_scores", r))
                if r >= 2:
                    dve.wait_ge(sem("ret_step"), r - 1)
                for jb in range(TB):
                    ins = dve.scalar_tensor_tensor(out=ret_p[:, r % 2, jb * T:(jb + 1) * T], in0=b[:, jb * T:(jb + 1) * T],
                                                   scalar=HD ** -0.5, in1=m[:, (1 - jb) * P:(3 - jb) * P],
                                                   op0=ALU.mult, op1=ALU.mult)
                ins.then_inc(read_sem(("ret_scores", r)), 1)
                if r + 2 < HEADS:
                    decay_of(r + 2)
                if r in WEIGH_HEADS:
                    weigh_mod(WEIGH_HEADS[r])
                if r == 1:
                    for tb in range(TB):
                        hi_seen[0] += 1
                        dve.wait_ge(sem("T_hi"), hi_seen[0])
                        t = slice(tb * P, (tb + 1) * P)
                        dve.tensor_tensor(hT_lo[:, 0:4, t], bank_of(("att", tb))[:, :].rearrange("p (a t) -> p a t", t=P),
                                          hT_hi[:, 0:4, t].bitcast(F32), ALU.subtract).then_inc(read_sem(("att", tb)), 1)
            def late_column(c):
                filled(dve, ("mod_col", c))
                mod_column([c], ("mod_col", c))

            late_column(N_MOD // 2 - 2)
            dve.wait_ge(sem("ret_step"), HEADS)
            for tb in range(TB):
                b = bank_of(("ret", tb))
                chain(dve.reduce_sum(row_max[:, tb * 8:tb * 8 + 8], heads(b[:, :]), AX.X))
                chain(dve.tensor_scalar(row_max[:, tb * 8:tb * 8 + 8], row_max[:, tb * 8:tb * 8 + 8], -1.0 / HD, None, ALU.mult))
                ins = dve.tensor_tensor(heads(xn[:, tb, 512:1024]), heads(b[:, :]),
                                        heads_bc(row_max[:, tb * 8:tb * 8 + 8], HEADS, HD), ALU.add)
                ins.then_inc(sem("ret_centred"), 1)
            for tb in range(TB):
                dve.wait_ge(sem("ret_sq"), tb + 1)
                ins = dve.reduce_sum(head_ss[:, tb * 8:tb * 8 + 8], heads(probs[:, tb, :]), AX.X)
            ins.then_inc(sem("ret_var"), 1)
            dve.wait_ge(sem("ret_rms"), 1)
            chain(dve.reciprocal(head_rstd[:, :], head_rms[:, :]))
            for tb in range(TB):
                v = xn[:, tb, 512:1024]
                chain(dve.tensor_tensor(heads(v), heads(v), heads_bc(head_rstd[:, tb * 8:tb * 8 + 8], HEADS, HD), ALU.mult))
                dve.wait_ge(sem("silu_gr"), 1)
                dve.tensor_tensor(v, v, silu_gr[:, tb, :], ALU.mult).then_inc(read_sem(("ret", tb)), 1)
            split_T("mixT", n=2, first=4)
            late_column(N_MOD // 2 - 1)
            dve.tensor_tensor(gain_col[:, 0, :], mod[:, 16:24, 0], col("g_post_mix"), ALU.mult)
            chain(dve.tensor_tensor(gain_col[:, 1, :], mod[:, 40:48, 0], col("g_post_ffn"), ALU.mult))
            for g in range(2):
                dve.tensor_tensor(gain_diag[g].rearrange("p (k t) -> p k t", t=P), over_heads(ident, KC, P),
                                  heads_bc(gain_col[:, g, :], KC, P), ALU.mult).then_inc(sem("gain_diag"), 1)
            chain(dve.tensor_scalar(a_ffn[:, :], mod[:, 32:40, 0], 1.0, None, ALU.add))
            chain(dve.tensor_tensor(a_ffn[:, :], a_ffn[:, :], col("g_pre_ffn"), ALU.mult))

            def post_norm(y, name, g):
                n = norms[0]
                norms[0] += 1
                read_out(dve, ("gain_row", 2 * g + 1))
                for c in range(2):
                    product_done(dve, name, c)
                    d = slice(c * 512, (c + 1) * 512)
                    for tb in (1, 0):
                        if tb == 0:
                            dve.wait_ge(sem("tile0_squared"), 2 * g + c + 1)
                        dve.tensor_tensor(y[:, tb, d], bank_of((*name, tb, c))[:, :], rows[:, g, d], ALU.mult)\
                            .then_inc(sem("y_gained"), 1)
                    if c == 0:
                        dve.wait_ge(sem("half_ss_ready"), g + 1)
                        dve.tensor_scalar(half_mean[:, :], half_ss[:, 0, :], 1.0 / D, EPS, ALU.mult, ALU.add)\
                            .then_inc(sem("norm_ss_v"), 1)
                dve.wait_ge(sem("norm_rms"), n + 1)
                dve.reciprocal(rstd[:, :], rms[:, :]).then_inc(sem("norm_rstd"), 1)
                dve.wait_ge(sem("norm_rstd"), n + 1)
                dve.wait_ge(sem("y_gained"), 4 * g + 4)
                order = [(tb, c) for tb in range(TB) for c in range(2)]
                if g:
                    order.sort(key=lambda o: o[1])
                for tb, c in order:
                    xs = x[:, tb, c * 512:(c + 1) * 512]
                    dve.scalar_tensor_tensor(out=xs, in0=y[:, tb, c * 512:(c + 1) * 512], scalar=rstd[:, tb:tb + 1],
                                             in1=xs, op0=ALU.mult, op1=ALU.add).then_inc(read_sem((*name, tb, c)), 1)

            squares_out[0] = xn[:, 1, :]

            def pre_norm(stage, ready, gain):
                split_T(stage, gain)
                norm_stats(x, ready)

            def add_to_x(name, scale=None):
                for c in range(2):
                    product_done(dve, name, c)
                    for tb in range(TB):
                        key = (*name, tb, c)
                        xs = x[:, tb, c * 512:(c + 1) * 512]
                        dve.scalar_tensor_tensor(out=xs, in0=bank_of(key)[:, :], scalar=1.0 if scale is None else scale,
                                                 in1=xs, op0=ALU.mult, op1=ALU.add).then_inc(read_sem(key), 1)

            def ffn(f):
                silu0 = 2 * UP * f

                def gated(c, silus):
                    for tb in range(TB):
                        dve.wait_ge(sem("gate_silu"), silus + tb + 1)
                        b = (c % 3) * 2 + tb
                        g = gate[:, c % 3, tb, :]
                        dve.scalar_tensor_tensor(out=g, in0=bank[b][:, 256:512], scalar=rstd[:, tb:tb + 1] if f else 1.0,
                                                 in1=g, op0=ALU.mult, op1=ALU.mult).then_inc(bank_read[b], 1)

                def gate_lo(his, at):
                    dve.wait_ge(sem("gateT_hi"), his)
                    s = at if isinstance(at, slice) else bass.ds(at, 2)
                    dve.tensor_tensor(gT_lo[:, s, :], bank[6][:, :].rearrange("p (a t) -> p a t", t=T),
                                      gT_hi[:, s, :].bitcast(F32), ALU.subtract).then_inc(bank_read[6], 1)

                gated(0, silu0)
                gated(1, silu0 + 2)
                gate_lo(UP * f + 1, slice(0, 2))
                with dve.Fori(0, 3) as i:
                    for j in range(3):
                        c = 2 + j
                        gated(c, i * 6 + (silu0 + 2 * c))
                        gate_lo(i * 3 + (UP * f + c), i * 6 + 2 * (c - 1))
                gate_lo(UP * (f + 1), slice(2 * UP - 2, 2 * UP))

            post_norm(y_mix, ("mix_out",), 0)
            norm_stats(x, x_added(("mix_out",), 1))
            norm_scale(x, xn)
            split_T("ffn0T", shift=(a_ffn, mod[:, 24:32, 0]))
            ffn(0)
            post_norm(y_ffn, ("down", 0), 1)
            pre_norm("ffn1T", x_added(("down", 0), 1), col("ffn1_norm"))
            ffn(1)
            add_to_x(("down", 1), 0.5)
            pre_norm("mix2T", x_added(("down", 1), 1), col("mix_norm"))

            dve.wait_ge(sem("lb_loaded"), 16)
            chain(dve.tensor_tensor(lb, lb_p[:, 0, :], lb_p[:, 1, :], ALU.max))
            dve.tensor_tensor(lb_p[:], lb_p[:], over_heads(lb, 2, 512), ALU.subtract).then_inc(sem("lb_diff"), 1)
            dve.wait_ge(sem("lb_exp"), 1)
            chain(dve.tensor_tensor(lb, lb_p[:, 0, :], lb_p[:, 1, :], ALU.add))
            chain(dve.reciprocal(lb, lb))
            chain(dve.tensor_tensor(lb, lb, lb_p[:, 0, :], ALU.mult))
            chain(dve.tensor_scalar(one_lb, lb, -1.0, 1.0, ALU.mult, ALU.add))
            chain(dve.memset(scT, 0.0))
            read_out(dve, ("zf", 1))
            chain(dve.tensor_tensor(fgate[:], fgate[:], over_heads(one_lb, TB, 512), ALU.mult))
            chain(dve.tensor_tensor(fgate[:], fgate[:], over_heads(lb, TB, 512), ALU.add))
            dve.tensor_scalar(hk[:], fgate[:], -1.0, 1.0, ALU.mult, ALU.add).then_inc(sem("fgate"), 1)
            dve.wait_ge(sem("logf_hi"), 1)
            dve.tensor_tensor(logf_lo[:], fgate[:], logf_hi[:].bitcast(F32), ALU.subtract).then_inc(sem("logf_lo"), 1)

            mask = lambda n: over_heads(level_mask[:, n, :], 4, P).bitcast(I32)
            sc = lambda blk: scT[:, blk * 512:(blk + 1) * 512].rearrange("p (h t) -> p h t", t=P)

            def keep_pairs(level, name):
                for blk in range(TB):
                    b = filled(dve, (*name, blk))
                    dve.copy_predicated(sc(blk), mask(level + 1), b[:, :].rearrange("p (h t) -> p h t", t=P))\
                        .then_inc(read_sem((*name, blk)), 1)

            def decayed(level):
                buf = qk_dec[level % 2]
                for late, other in ((1, hqT), (0, hkT)):
                    h = 1 << level
                    v = buf.rearrange("p (n two h) -> p n two h", two=2, h=h)[:, :, late, :] if level < LEVELS else \
                        buf[:, late * 512:late * 512 + 512]
                    o = other.rearrange("p (n two h) -> p n two h", two=2, h=h)[:, :, late, :] if level < LEVELS else \
                        other[:, late * 512:late * 512 + 512]
                    ins = dve.tensor_tensor(v, v, o, ALU.mult)
                ins.then_inc(sem("level_decayed"), 1)

            dve.wait_ge(sem("const2_loaded"), 16)
            read_out(dve, ("hkT", 0))
            read_out(dve, ("hkT", 1))
            keep_pairs(-1, ("diag",))
            def convolution():
                u3 = uT.rearrange("p (c t) -> p c t", t=T + 2)
                dve.memset(u3[:, :, 0:2], 0.0).then_inc(sem("u_pad"), 1)
                read_out(dve, "uT0")
                read_out(dve, "uT1")
                dve.wait_ge(sem("u_pad"), 1)
                taps = lambda c, j: col("conv_w", 3 * c + j, 3 * c + j + 1)
                for c in range(4):
                    ins = dve.tensor_scalar(conv[:, c, :], u3[:, c, 2:T + 2], taps(c, 2), None, ALU.mult)
                chain(ins)
                for j in (1, 0):
                    for c in range(4):
                        ins = dve.scalar_tensor_tensor(out=conv[:, c, :], in0=u3[:, c, j:T + j], scalar=taps(c, j),
                                                       in1=conv[:, c, :], op0=ALU.mult, op1=ALU.add)
                    chain(ins)

            def gated_convolution():
                for j in range(2):
                    b = filled(dve, f"bT{j}")
                    dve.tensor_tensor(conv[:, 2 * j:2 * j + 2, :], conv[:, 2 * j:2 * j + 2, :],
                                      b[:, :].rearrange("p (c t) -> p c t", t=T), ALU.mult).then_inc(read_sem(f"bT{j}"), 1)

            for level in range(LEVELS + 1):
                read_out(dve, ("decay", level, 0))
                read_out(dve, ("decay", level, 1))
                decayed(level)
                if level:
                    keep_pairs(level - 1, ("pairs", level - 1))
                if level == LEVELS - 1:
                    convolution()
                if level == LEVELS:
                    gated_convolution()
                if level == 4:
                    dve.wait_ge(split_used, W_IN2 + 10)
                    read_out(dve, ("zc", 1))
                    for tb in range(TB):
                        dve.scalar_tensor_tensor(out=zc_sb[:, tb, :], in0=bank_of(("zu", tb))[:, :], scalar=rstd[:, tb:tb + 1],
                                                 in1=zc_sb[:, tb, :], op0=ALU.mult, op1=ALU.mult).then_inc(read_sem(("zu", tb)), 1)
            b = filled(dve, "cross")
            dve.tensor_copy(crossT, b[:, :]).then_inc(read_sem("cross"), 1)
            for j in range(2):
                dve.wait_ge(sem("conv_hi"), j + 1)
                dve.tensor_tensor(hT_lo[:, 4 + 2 * j:6 + 2 * j, :], conv[:, 2 * j:2 * j + 2, :],
                                  hT_hi[:, 4 + 2 * j:6 + 2 * j, :].bitcast(F32), ALU.subtract).then_inc(sem("conv_lo"), 1)
            read_out(dve, ("zg", 1))
            dve.wait_ge(sem("head_row_loaded"), 16)
            chain(dve.tensor_tensor(silu_zg[:], silu_zg[:], over_heads(head_row, TB, 512), ALU.mult))
            for blk in range(TB):
                dve.wait_ge(sem("hgrn_sq"), blk + 1)
                dve.reduce_sum(head_ss[:, 4 * blk:4 * blk + 4], hgrn_sq.rearrange("p (h d) -> p h d", d=P), AX.X)\
                    .then_inc(sem("hgrn_ss"), 1)
            dve.wait_ge(sem("hgrn_rms"), 1)
            chain(dve.reciprocal(head_rstd[:, 0:8], head_rms[:, 0:8]))
            for blk in range(TB):
                b = bank_of(("hgrn", blk))
                v = xn[:, blk, 0:512]
                dve.tensor_tensor(v.rearrange("p (h d) -> p h d", d=P), b[:, :].rearrange("p (h d) -> p h d", d=P),
                                  heads_bc(head_rstd[:, 4 * blk:4 * blk + 4], 4, P), ALU.mult)\
                    .then_inc(read_sem(("hgrn", blk)), 1)
                read_out(dve, ("hgrn", blk))
                dve.tensor_tensor(v, v, silu_zg[:, blk, :], ALU.mult).then_inc(sem("hgrn_out"), 1)
            split_T("mix2oT", n=2)
            add_to_x(("mix2_out",))
            pre_norm("xattT", x_added(("mix2_out",), 1), col("xattn_norm"))

            for h in range(MEM_HEADS):
                for tb in range(TB):
                    negative_max(TB * h + tb, ("mscores", h, tb), T, MEM_HD ** -0.5)
            for tb in range(TB):
                read_out(dve, ("mscores", MEM_HEADS - 1, tb))
            chain(dve.reciprocal(row_inv[:, 0:8], row_sum[:, 0:8]))
            inv = row_inv[:, 0:8].rearrange("p (h b) -> p h b", b=TB)
            for h2 in range(2):
                dve.wait_ge(sem("matt_step"), 2 * h2 + 2)
                for tb in range(TB):
                    b = bank_of(("matt", h2, tb))
                    dve.tensor_tensor(xn[:, tb, h2 * 512:(h2 + 1) * 512].rearrange("p (h d) -> p h d", d=MEM_HD),
                                      b[:, :].rearrange("p (h d) -> p h d", d=MEM_HD),
                                      heads_bc(inv[:, 2 * h2:2 * h2 + 2, tb], 2, MEM_HD), ALU.mult)\
                        .then_inc(read_sem(("matt", h2, tb)), 1)
            split_T("mattT")
            add_to_x(("mem_out",))
            pre_norm("ffn2T", x_added(("mem_out",), 1), col("ffn2_norm"))
            ffn(2)
            add_to_x(("down", 2), 0.5)

            norm_stats(x, x_added(("down", 2), 1))
            dve.wait_ge(sem("final_loaded"), 16)
            for tb in range(TB):
                dve.scalar_tensor_tensor(out=xn[:, tb, :], in0=x[:, tb, :], scalar=rstd[:, tb:tb + 1], in1=rows[:, 0, :],
                                         op0=ALU.mult, op1=ALU.mult).then_inc(sem("out_ready"), 1)

        @block.tensor
        def _(pe):
            def three(out, hi, lo, rhi, rlo, start, stop):
                pe.matmul(out, hi, rhi, start=start, stop=False)
                pe.matmul(out, hi, rlo, start=False, stop=False)
                return pe.matmul(out, lo, rhi, start=False, stop=stop)

            def unit(v, ready, tiles, ks, n, first, last, slot=None):
                pe.wait_ge(split_ready, ready)
                s = v % RING
                for hi, lo, tb, out in tiles:
                    for e, k in enumerate(ks):
                        t = slice(tb * P, (tb + 1) * P)
                        w = slice(e * n, (e + 1) * n)
                        ins = three(out[:, 0:n], hi[:, k, t], lo[:, k, t], w_hi[:, s, w], w_lo[:, s, w],
                                    first and e == 0, last and e == len(ks) - 1)
                ins.then_inc(split_used, 1)

            def project(v, names, tiles=None, halves=(0, 1), ready=None):
                tiles = tiles or [(hT_hi, hT_lo, 0), (hT_hi, hT_lo, 1)]
                for n, half in enumerate(halves):
                    if ready:
                        ready(half)
                    if n == 0:
                        outs = [free(pe, name) for name in names]
                    unit(v + n, v + n + 1, [(*t, o) for t, o in zip(tiles, outs)], range(4 * half, 4 * half + 4), 512,
                         n == 0, n == 1)

            def input_ready(stage):
                return lambda half: [read_out(pe, (stage, 2 * half + e)) for e in range(2)]

            scaled = [0]

            def transpose_input(stage, src):
                scaled[0] += 1
                pe.wait_ge(sem("xn_a"), scaled[0])
                pe.wait_ge(sem("xn_v"), scaled[0])
                transposes(stage, src)

            def transpose_x(stage, ready):
                for q in range(4):
                    if q % 2 == 0:
                        ready(q // 2)
                    transposes(stage, x, qs=[q])

            def added(name):
                return lambda c: [read_out(pe, (*name, tb, c)) for tb in range(TB)]

            def transposes(stage, src, n=4, qs=None):
                for q in qs or range(n):
                    b = free(pe, (stage, q))
                    for e in range(2):
                        for tb in range(TB):
                            ins = pe.transpose(b[:, e * T + tb * P:e * T + (tb + 1) * P],
                                               src[:, tb, (2 * q + e) * P:(2 * q + e + 1) * P], ident)
                    ins.then_inc(full_sem((stage, q)), 1)

            def mod_columns(name, c, accs, col0=0):
                b = bank_of(name)
                for e in range(4):
                    for cond, acc in enumerate(accs):
                        ins = pe.matmul(b[:, col0 + len(accs) * e + cond:col0 + len(accs) * e + cond + 1],
                                        acc[:, e * P:(e + 1) * P], ones[:, 0:1], start=True, stop=True)
                return ins

            def mod_columns_a(c):
                pe.wait_ge(mod_used, 2 * c + 2)
                mod_columns("mod_a", c, [acc_a[:, c % 2, cond, :] for cond in range(2)], 8 * c).then_inc(sem("mod_col"), 1)

            def mod_columns_b(c):
                pe.wait_ge(mod_used, 2 * c + 2)
                if c >= MODS_IN:
                    free(pe, ("mod_col", c))
                    mod_columns(("mod_col", c), c, [acc_b[:, c % 2, :]]).then_inc(full_sem(("mod_col", c)), 1)
                else:
                    mod_columns("mod_b", c, [acc_b[:, c % 2, :]], 4 * (c - 4)).then_inc(sem("mod_col"), 1)

            pe.wait_ge(sem("fixed_loaded"), 16)
            pe.wait_ge(sem("mem_loaded"), 16)
            transposes("memT", mem_in)
            for c in range(4):
                project(W_KV + 2 * c, [("kv", c, 0), ("kv", c, 1)], ready=input_ready("memT") if c == 0 else None)
                if c:
                    mod_columns_a(c - 1)
            read_out(pe, ("kv", 1, 0))
            read_out(pe, ("kv", 1, 1))
            transposes("keyT", mem_k)
            mod_columns_a(3)
            pe.wait_ge(sem("xn_a"), 2)
            pe.wait_ge(sem("xn_v"), 2)
            scaled[0] += 2

            def first_transposes(names):
                for stage, q in names:
                    b = free(pe, (stage, q))
                    for e in range(2):
                        for tb in range(TB):
                            ins = pe.transpose(b[:, e * T + tb * P:e * T + (tb + 1) * P],
                                               (xn if stage == "xT" else rows)[:, tb, (2 * q + e) * P:(2 * q + e + 1) * P], ident)
                    ins.then_inc(full_sem((stage, q)), 1)

            first_transposes(FIRST_T)

            both = [(hT_hi, hT_lo, 0), (hT_hi, hT_lo, 1), (hcT_hi, hcT_lo, 0), (hcT_hi, hcT_lo, 1)]
            chunk = [MOD_A // 2]
            j = 0
            for part, units, tiles in [("kr", 2, both), ("vr", 2, both), ("kava", 1, both), ("qa", 2, both[:2]), ("qr", 2, both[:2])]:
                for e in range(units):
                    if j < 2:
                        for stage in ("xT", "ctxT"):
                            for q in range(2):
                                read_out(pe, (stage, 2 * j + q))
                    if e == 0:
                        outs = [free(pe, (part, t)) for t in range(len(tiles))]
                    if j == 2:
                        free(pe, "mod_b")
                    while j >= 2 and chunk[0] < (MOD_A + sum(IN_MODS[:j - 1])) // 2:
                        mod_columns_b(chunk[0])
                        chunk[0] += 1
                    ks, n = (range(4 * e, 4 * e + 4), 512) if units == 2 else (range(8), 256)
                    unit(W_IN + j, W_IN + j + 1, [(*t, o) for t, o in zip(tiles, outs)], ks, n, e == 0, e == units - 1)
                    j += 1
            for c in range(chunk[0], MODS_IN):
                mod_columns_b(c)

            pe.wait_ge(sem("kr_done"), 1)
            read_out(pe, ("vr", 3))
            b = free(pe, "states")
            for fb in range(2):
                for h in range(HEADS):
                    o = b[64 * (h % 2):64 * (h % 2) + 64, fb * 256 + (h // 2) * HD:fb * 256 + (h // 2 + 1) * HD]
                    for jb in range(TB):
                        ins = pe.matmul(o, k_fb[:, fb, jb, h * HD:(h + 1) * HD], vr[:, 2 + jb, h * HD:(h + 1) * HD],
                                        start=(jb == 0), stop=(jb == 1))
            ins.then_inc(full_sem("states"), 1)
            pe.wait_ge(sem("rope_done"), 6)
            transposes("krT", krn, 2)
            b = free(pe, ("kaT", 0))
            for tile in range(4):
                ins = pe.transpose(b[:, tile * P:(tile + 1) * P], ka_all[:, tile, :], ident)
            ins.then_inc(full_sem(("kaT", 0)), 1)
            transposes("qaT", qan, 2)
            for name, n in (("krT", 2), ("kaT", 1), ("qaT", 2)):
                for q in range(n):
                    read_out(pe, (name, q))

            pe.wait_ge(sem("keys_padded"), 1)

            def scores(s):
                h, tb = s // 2, s % 2
                j, kv = h % GROUP, h // GROUP
                b = free(pe, ("scores", s))
                pe.matmul(b[:, :], qaT[:, j, tb * P:(tb + 1) * P], kaT[:, kv, :],
                          start=True, stop=True).then_inc(full_sem(("scores", s)), 1)

            def weighted(s):
                h, tb = s // 2, s % 2
                kv = h // GROUP
                read_out(pe, ("probsT", s))
                j = h % GROUP
                b = free(pe, ("att", tb))
                for kb, tile in enumerate((2, 3, 0, 1)):
                    ins = pe.matmul(b[kv * HD:(kv + 1) * HD, j * P:(j + 1) * P], kava[:, tile, P + kv * HD:P + (kv + 1) * HD],
                                    probsT[:, s % 2, kb * P:(kb + 1) * P], start=(kb == 0), stop=(kb == 3))
                ins.then_inc(sem("att_step"), 1)

            def retained(r):
                read_out(pe, ("ret_scores", r))
                pe.wait_ge(sem("q_decayed"), 2 * (r // 2) + 2)
                read_out(pe, "states")
                for ib in range(TB):
                    o = free(pe, ("ret", ib))[:, r * HD:(r + 1) * HD]
                    for jb in range(TB):
                        pe.matmul(o, ret_p[:, r % 2, jb * T + ib * P:jb * T + (ib + 1) * P], vr[:, jb, r * HD:(r + 1) * HD],
                                  start=(jb == 0), stop=False)
                    for fb in range(2):
                        ins = pe.matmul(o, q_decayed[:, fb, ib * P:(ib + 1) * P], state[:, fb, r, :],
                                        start=False, stop=(fb == 1))
                ins.then_inc(sem("ret_step"), 1)

            def input_unit(j):
                part, e = "gr", (j - 9) % 2
                outs = [(free(pe, (part, tb)) if e == 0 else bank_of((part, tb))) for tb in range(TB)]
                unit(W_IN + j, W_IN + j + 1, [(hT_hi, hT_lo, tb, outs[tb]) for tb in range(TB)], range(4 * e, 4 * e + 4), 512,
                     e == 0, e == 1)

            scores(0)
            scores(1)
            for s in range(2 * HEADS):
                if s + 2 < 2 * HEADS:
                    scores(s + 2)
                if s:
                    weighted(s - 1)
                if s in UNIT_STEPS:
                    input_unit(UNIT_STEPS[s])
                pe.wait_ge(sem("probs_ready"), s + 1)
                b = free(pe, ("probsT", s))
                for kb in range(4):
                    ins = pe.transpose(b[:, kb * P:(kb + 1) * P], probs[:, s % 2, kb * P:(kb + 1) * P], ident)
                ins.then_inc(full_sem(("probsT", s)), 1)
                for c, step in MOD_STEPS.items():
                    if step == s:
                        mod_columns_b(c)
                if 2 * HEADS - 3 <= s < 2 * HEADS - 1:
                    pe.wait_ge(sem("rope_done"), 8)
                    transposes("qrT", qrn, qs=[s - (2 * HEADS - 3)])
            weighted(2 * HEADS - 1)

            def retention_scores(r):
                b = free(pe, ("ret_scores", r))
                for jb in range(TB):
                    ins = pe.matmul(b[:, jb * T:(jb + 1) * T], krT[:, r, jb * P:(jb + 1) * P], qrT[:, r // 2, :],
                                    start=True, stop=True)
                ins.then_inc(full_sem(("ret_scores", r)), 1)

            def mix_out(half, c):
                v = W_OUT + 2 * half + c
                outs = [(free(pe, ("mix_out", tb, c)) if half == 0 else bank_of(("mix_out", tb, c))) for tb in range(TB)]
                unit(v, v + 1, [(hT_hi, hT_lo, tb, outs[tb]) for tb in range(TB)], range(4 * half, 4 * half + 4), 512,
                     half == 0, half == 1)

            for q in range(2):
                read_out(pe, ("qrT", q))
            retention_scores(0)
            for r in range(HEADS):
                if r + 1 < HEADS:
                    retention_scores(r + 1)
                if r == 4:
                    mix_out(0, 0)
                retained(r)
                if r == HEADS - 2:
                    mod_columns_b(N_MOD // 2 - 2)
            mix_out(0, 1)
            mod_columns_b(N_MOD // 2 - 1)
            for q in range(2):
                read_out(pe, ("ret", q))
            for q in range(2):
                b = free(pe, ("mixT", q))
                for e in range(2):
                    for tb in range(TB):
                        k = 4 + 2 * q + e
                        ins = pe.transpose(b[:, e * T + tb * P:e * T + (tb + 1) * P], xn[:, tb, k * P:(k + 1) * P], ident)
                ins.then_inc(full_sem(("mixT", q)), 1)
            for q in range(2):
                read_out(pe, ("mixT", q))
            mix_out(1, 0)
            for q in range(4):
                if q % 2 == 0:
                    pe.wait_ge(sem("gain_diag"), q // 2 + 1)
                b = free(pe, ("gain_row", q))
                pe.matmul(b[:, :], ones, gain_diag[q // 2][:, (q % 2) * 512:(q % 2 + 1) * 512], start=True, stop=True)\
                    .then_inc(full_sem(("gain_row", q)), 1)

            mix_out(1, 1)

            def ffn(f, stage):
                up, dn = W_UP[f], W_DN[f]

                def up_chunk(c, ready, frees, inputs=None):
                    for half in range(2):
                        if inputs:
                            inputs(half)
                        if half == 0:
                            for tb in range(TB):
                                pe.wait_ge(bank_read[(c % 3) * 2 + tb], frees[tb])
                        unit(up + 2 * c + half, ready + half + 1,
                             [(hT_hi, hT_lo, tb, bank[(c % 3) * 2 + tb]) for tb in range(TB)],
                             range(4 * half, 4 * half + 4), 512, half == 0, half == 1)

                def gate_T(c, reads, before):
                    for tb in range(TB):
                        pe.wait_ge(bank_read[(c % 3) * 2 + tb], reads[tb])
                    pe.wait_ge(bank_read[6], before)
                    for e in range(2):
                        for tb in range(TB):
                            ins = pe.transpose(bank[6][:, e * T + tb * P:e * T + (tb + 1) * P],
                                               gate[:, c % 3, tb, e * P:(e + 1) * P], ident)
                    ins.then_inc(bank_full[6], 1)

                fills = lambda c: [plan.of[("up", f, c, tb)][1] for tb in range(TB)]
                g0 = plan.of[("gateT", f, 0)][1]
                up_chunk(0, up, fills(0), input_ready(stage))
                up_chunk(1, up + 2, fills(1))
                gate_T(0, [n + 1 for n in fills(0)], g0)
                with pe.Fori(0, 3) as i:
                    for j in range(3):
                        c = 2 + j
                        up_chunk(c, i * 6 + (up + 2 * c), [i + n for n in fills(c)])
                        gate_T(c - 1, [i + (n + 1) for n in fills(c - 1)], i * 3 + (g0 + c - 1))

                def down(k):
                    pe.wait_ge(split_ready, dn + k + 1)
                    pe.wait_ge(bank_read[6], g0 + k + 1)
                    s = (dn + k) % RING
                    order = [(tb, e, half) for tb in range(TB) for e in range(2) for half in range(2)]
                    if k == UP - 1:
                        order.sort(key=lambda o: o[2])
                    for n, (tb, e, half) in enumerate(order):
                        t = slice(tb * P, (tb + 1) * P)
                        o = free(pe, ("down", f, tb, half)) if k == 0 and e == 0 else bank_of(("down", f, tb, half))
                        w = slice(e * D + half * 512, e * D + half * 512 + 512)
                        ins = three(o[:, :], gT_hi[:, 2 * k + e, t], gT_lo[:, 2 * k + e, t], w_hi[:, s, w], w_lo[:, s, w],
                                    k == 0 and e == 0, k == UP - 1 and e == 1)
                        if k == UP - 1 and n == 3:
                            ins.then_inc(sem("down_half"), 1)
                    ins.then_inc(split_used, 1)

                down(0)
                gate_T(UP - 1, [n + 1 for n in fills(UP - 1)], g0 + UP - 1)
                for k in range(1, UP):
                    down(k)

            transpose_input("ffn0T", xn)
            ffn(0, "ffn0T")
            transpose_x("ffn1T", added(("down", 0)))
            ffn(1, "ffn1T")
            transpose_x("mix2T", added(("down", 1)))

            z = lambda k, part: project(W_IN2 + 2 * k, [(part, 0), (part, 1)], ready=input_ready("mix2T") if k == 0 else None)
            z(0, "zf")
            z(1, "zq")
            z(2, "zi")
            read_out(pe, ("zq", 1))
            pe.wait_ge(sem("fgate"), 1)
            for name, src in (("hqT", hq), ("hkT", hk)):
                for blk in range(TB):
                    b = free(pe, (name, blk))
                    for h in range(HG_HEADS):
                        ins = pe.transpose(b[:, h * P:(h + 1) * P], src[:, blk, h * P:(h + 1) * P], ident)
                    ins.then_inc(full_sem((name, blk)), 1)

            def decay_sums(level):
                for blk in range(TB):
                    b = free(pe, ("decay", level, blk))
                    m = sums_r[:, level + blk if level == LEVELS else level, :]
                    for h in range(HG_HEADS):
                        o = b[:, h * P:(h + 1) * P]
                        pe.matmul(o, logf_hi[:, blk, h * P:(h + 1) * P], m, start=True, stop=False)
                        ins = pe.matmul(o, logf_lo[:, blk, h * P:(h + 1) * P], m, start=False, stop=True)
                    ins.then_inc(full_sem(("decay", level, blk)), 1)

            def pair_scores(level):
                pe.wait_ge(sem("level_decayed"), level + 1)
                buf = qk_dec[level % 2]
                if level == LEVELS:
                    b = free(pe, "cross")
                    for h in range(HG_HEADS):
                        ins = pe.matmul(b[:, h * P:(h + 1) * P], buf[:, h * P:(h + 1) * P],
                                        buf[:, 512 + h * P:512 + (h + 1) * P], start=True, stop=True)
                    ins.then_inc(full_sem("cross"), 1)
                    return
                for blk in range(TB):
                    b = free(pe, ("pairs", level, blk))
                    for h in range(HG_HEADS):
                        v = buf[:, blk * 512 + h * P:blk * 512 + (h + 1) * P]
                        ins = pe.matmul(b[:, h * P:(h + 1) * P], v, v, start=True, stop=True)
                    ins.then_inc(full_sem(("pairs", level, blk)), 1)

            def positions_last(name, src):
                for j in range(2):
                    b = free(pe, f"{name}{j}")
                    for e in range(2):
                        for tb in range(TB):
                            ins = pe.transpose(b[:, e * T + tb * P:e * T + (tb + 1) * P],
                                               src[:, tb, (2 * j + e) * P:(2 * j + e + 1) * P], ident)
                    ins.then_inc(full_sem(f"{name}{j}"), 1)

            pe.wait_ge(sem("sums_ready"), 1)
            pe.wait_ge(sem("logf_lo"), 1)
            decay_sums(0)
            for name in ("hqT", "hkT"):
                for q in range(2):
                    read_out(pe, (name, q))
            for blk in range(TB):
                b = free(pe, ("diag", blk))
                for h in range(HG_HEADS):
                    s = slice(blk * 512 + h * P, blk * 512 + (h + 1) * P)
                    ins = pe.matmul(b[:, h * P:(h + 1) * P], hkT[:, s], hqT[:, s], start=True, stop=True)
                ins.then_inc(full_sem(("diag", blk)), 1)
            parts = ["zc", "zu", "zb", "zg"]
            for step in range(8):
                k, half = step // 2, step % 2
                v = W_IN2 + 6 + step
                if half == 0:
                    outs = [free(pe, (parts[k], tb)) for tb in range(TB)]
                unit(v, v + 1, [(hT_hi, hT_lo, tb, outs[tb]) for tb in range(TB)], range(4 * half, 4 * half + 4), 512,
                     half == 0, half == 1)
                if step < LEVELS:
                    decay_sums(step + 1)
                    pair_scores(step)
                if step == LEVELS - 2:
                    read_out(pe, ("zu", 1))
                    positions_last("uT", zc_sb)
                if step == LEVELS - 1:
                    read_out(pe, ("zb", 1))
                    positions_last("bT", zb_sb)
            pair_scores(LEVELS)
            read_out(pe, ("pairs", LEVELS - 1, 0))
            read_out(pe, ("pairs", LEVELS - 1, 1))
            read_out(pe, "cross")
            for blk in range(TB):
                b = free(pe, ("hgrn", blk))
                for h in range(HG_HEADS):
                    d = slice(h * P, (h + 1) * P)
                    ins = pe.matmul(b[:, d], scT[:, blk * 512 + h * P:blk * 512 + (h + 1) * P], hv[:, blk, d],
                                    start=True, stop=(blk == 0))
                    if blk:
                        ins = pe.matmul(b[:, d], crossT[:, d], hv[:, 0, d], start=False, stop=True)
                ins.then_inc(full_sem(("hgrn", blk)), 1)
            pe.wait_ge(sem("conv_lo"), 2)

            def mix2_out(half, c):
                v = W_OUT2 + 2 * (1 - half) + c
                outs = [(free(pe, ("mix2_out", tb, c)) if half == 1 else bank_of(("mix2_out", tb, c))) for tb in range(TB)]
                unit(v, v + 1, [(hT_hi, hT_lo, tb, outs[tb]) for tb in range(TB)], range(4 * half, 4 * half + 4), 512,
                     half == 1, half == 0)

            mix2_out(1, 0)
            mix2_out(1, 1)
            pe.wait_ge(sem("hgrn_out"), TB)
            transposes("mix2oT", xn, 2)
            for q in range(2):
                read_out(pe, ("mix2oT", q))
            mix2_out(0, 0)
            mix2_out(0, 1)

            transpose_x("xattT", added(("mix2_out",)))
            project(W_Q, [("mq", tb, 0) for tb in range(TB)], ready=input_ready("xattT"))

            def mem_queries(c):
                for tb in range(TB):
                    read_out(pe, ("mq", tb, c))
                for q in (2 * c, 2 * c + 1):
                    transposes("mqT", mq, qs=[q])

            project(W_Q + 2, [("mq", tb, 1) for tb in range(TB)], ready=lambda half: mem_queries(0) if half else None)

            def mem_scores(h):
                for tb in range(TB):
                    b = free(pe, ("mscores", h, tb))
                    for e in range(2):
                        ins = pe.matmul(b[:, 0:T], mqT[:, 2 * h + e, tb * P:(tb + 1) * P], memKT[:, 2 * h + e, :],
                                        start=(e == 0), stop=(e == 1))
                    ins.then_inc(full_sem(("mscores", h, tb)), 1)

            def mem_weighted(h):
                read_out(pe, ("mprobsT", h))
                for tb in range(TB):
                    b = free(pe, ("matt", h // 2, tb))
                    for mb in range(TB):
                        ins = pe.matmul(b[:, (h % 2) * MEM_HD:(h % 2 + 1) * MEM_HD],
                                        mprobsT[:, h % 2, (mb * TB + tb) * P:(mb * TB + tb + 1) * P],
                                        memV[:, mb, h * MEM_HD:(h + 1) * MEM_HD], start=(mb == 0), stop=(mb == 1))
                ins.then_inc(sem("matt_step"), 1)

            for q in range(2):
                read_out(pe, ("mqT", q))
            mem_scores(0)
            mem_queries(1)
            for h in range(MEM_HEADS):
                if h == 1:
                    for q in range(2, 4):
                        read_out(pe, ("mqT", q))
                if h + 1 < MEM_HEADS:
                    mem_scores(h + 1)
                if h:
                    mem_weighted(h - 1)
                for tb in range(TB):
                    read_out(pe, ("mscores", h, tb))
                b = free(pe, ("mprobsT", h))
                for mb in range(TB):
                    for tb in range(TB):
                        ins = pe.transpose(b[:, (mb * TB + tb) * P:(mb * TB + tb + 1) * P], mprobs[:, tb, mb * P:(mb + 1) * P],
                                           ident)
                ins.then_inc(full_sem(("mprobsT", h)), 1)
            mem_weighted(MEM_HEADS - 1)
            for half in range(2):
                for tb in range(TB):
                    read_out(pe, ("matt", half, tb))
            transposes("mattT", xn)
            for c in range(2):
                project(W_O + 2 * c, [("mem_out", tb, c) for tb in range(TB)], ready=input_ready("mattT") if c == 0 else None)
            transpose_x("ffn2T", added(("mem_out",)))
            ffn(2, "ffn2T")



def lay_out(a):
    f = lambda name: np.asarray(a[name])
    halves = lambda w: [w[512 * h:512 * h + 512].reshape(4, P, -1).transpose(1, 0, 2).reshape(P, UNIT) for h in range(2)]
    whole = lambda w: w.reshape(KC, P, 256).transpose(1, 0, 2).reshape(P, UNIT)

    def project(w, halves_order=(0, 1)):
        return [halves(w[:, c:c + 512])[h] for c in range(0, w.shape[1], 512) for h in halves_order]

    def swiglu(gate, up, down):
        out = []
        for c in range(0, FFN, 256):
            out += halves(np.concatenate([gate[:, c:c + 256], up[:, c:c + 256]], axis=1))
        return out + [down[r:r + 256].reshape(2, P, D).transpose(1, 0, 2).reshape(P, UNIT) for r in range(0, FFN, 256)]

    w_in, w_in2 = f("w_in")[0], f("w_in_2")[0]
    cut = lambda w, at: w[:, at:at + 512]
    kr, vr, qa, qr, gr = (cut(w_in, at) for at in (1280, 1792, 0, 768, 2304))
    w = project(f("w_kv_mem_2")[0])
    w += project(kr) + project(vr) + [whole(w_in[:, 512:768])] + project(qa) + project(qr) + project(gr)
    w_out = f("w_out")[0]
    w_out = np.concatenate([w_out[:512].reshape(KV_HEADS, GROUP, HD, D).transpose(1, 0, 2, 3).reshape(512, D), w_out[512:]])
    w += [halves(w_out[:, c:c + 512])[h] for h in range(2) for c in range(0, D, 512)]
    w += swiglu(f("w_ffn_in")[0][:, :FFN], f("w_ffn_in")[0][:, FFN:], f("w_ffn_out")[0])
    w += swiglu(f("ffn1_gate_2")[0], f("ffn1_up_2")[0], f("ffn1_down_2")[0])
    for at in (512, 0, 1024, 2560, 3072, 2048, 1536):
        w += project(cut(w_in2, at))
    w += [halves(f("w_out_2")[0][:, c:c + 512])[h] for h in (1, 0) for c in range(0, D, 512)]
    w += project(f("w_q_mem_2")[0]) + project(f("w_o_mem_2")[0])
    w += swiglu(f("ffn2_gate_2")[0], f("ffn2_up_2")[0], f("ffn2_down_2")[0])
    mods = project(f("w_mod")[0])
    units = {"w": w, "mod": mods}

    col = lambda v: v.reshape(-1, P).T
    everywhere = lambda v: np.broadcast_to(v.reshape(1, -1), (P, v.size))
    decay = np.stack([f("ret_decay_fwd")[0], f("ret_decay_bwd")[0]])
    pairs = np.concatenate([np.repeat(decay[:, e::2].reshape(1, -1), HD, axis=0) for e in range(2)], axis=0)
    small = {name: col(f(src)) for name, src in [
        ("g_pre_mix", "g_pre_mix"), ("g_post_mix", "g_post_mix"), ("g_pre_ffn", "g_pre_ffn"),
        ("g_post_ffn", "g_post_ffn"), ("b_mod", "b_mod"), ("ffn1_norm", "ffn1_norm_2"), ("mix_norm", "mix_norm_2"),
        ("xattn_norm", "xattn_norm_2"), ("mem_norm", "mem_norm_2"), ("ffn2_norm", "ffn2_norm_2")]}
    small["conv_w"] = f("conv_w_2")[0].reshape(4, P, 3).transpose(1, 0, 2).reshape(P, 12)
    small["cond"] = np.stack([f("c")[0], f("c_ctx")], axis=1).reshape(KC, P, 2).transpose(1, 0, 2).reshape(P, 16)
    small["decay_rows"] = everywhere(decay)
    small["decay_pairs"] = pairs
    small["qk_gain"] = everywhere(np.concatenate([f("q_norm_g")[0], f("k_norm_g")[0]]))
    tiles = lambda v: v[0].reshape(TB, P, D).transpose(1, 0, 2)
    fixed, const1, const2 = shape_constants()
    out = {
        "weights": np.stack([units[kind][n] for kind, n in STREAM]),
        "cols": np.concatenate([small[name] for name in COLS], axis=1),
        "x": tiles(f("x")), "ctx": tiles(f("ctx")), "mem": tiles(f("mem_2")),
        "fixed": fixed, "const1": const1, "const2": const2,
        "lb_param": f("lb_param_2").reshape(1, D), "hgrn_out_norm": f("hgrn_out_norm_2").reshape(1, 512),
        "final_norm": f("final_norm_2").reshape(1, D),
    }
    return {name: np.ascontiguousarray(v) for name, v in out.items()}


def kernel(**inputs):
    import concourse.bacc as _bacc
    from concourse.bass_utils import run_bass_kernel_spmd as _run

    nc = _bacc.Bacc("TRN2", target_bir_lowering=False, num_devices=1)
    arrays = {f"in_{name}": v for name, v in lay_out(inputs).items()}
    io = {name[3:]: nc.dram_tensor(name, v.shape, mybir.dt.from_np(v.dtype), kind="ExternalInput").ap()
          for name, v in arrays.items()}
    out = nc.dram_tensor("out", (T, D), F32, kind="ExternalOutput").ap()
    io["out"] = out.rearrange("(b p) d -> b p d", p=P)
    two_blocks_kernel(nc, io)
    r = _run(nc, [arrays], core_ids=[0])
    return r.results[0]["out"].reshape(1, T, D)
```
